# Optimizing a Trainium2 kernel written in Bass

```python
import math
import jax
import jax.numpy as jnp
from jax import lax
import numpy as np

D_MODEL = 1024
BATCH = 1
SEQ = 512
DEPTH = 2

HEAD_DIM = 64
GROUP_HEADS = 4
GROUP_WIDTH = GROUP_HEADS * HEAD_DIM
N_MIXERS = 4
MIX_WIDTH = N_MIXERS * GROUP_WIDTH
DIFF_HALF = HEAD_DIM // 2
MLSTM_CHUNK = 64
MLSTM_CONV = 4
HGRN_KEY = 64
HGRN_CHUNK = 16
NSA_KV_DIM = HEAD_DIM
CMP_LEN = 32
CMP_STRIDE = 16
SEL_BLOCK = 64
SEL_TOPK = 16
WINDOW = 512
Q_BLOCK = 128
N_GROUPS = 4
EXPERTS_PER_GROUP = 8
TOPK_IN_GROUP = 2
D_EXPERT = 256
EPS = 1e-6
NEG_INF = -1e30
LB_FLOOR = 1e-30
F32 = jnp.float32

IN_WIDTHS = (
    GROUP_WIDTH, GROUP_WIDTH, GROUP_WIDTH,
    GROUP_WIDTH, GROUP_WIDTH, GROUP_WIDTH, GROUP_HEADS, GROUP_HEADS, GROUP_WIDTH,
    GROUP_HEADS * HGRN_KEY, GROUP_HEADS * HGRN_KEY, GROUP_WIDTH, GROUP_WIDTH,
    GROUP_WIDTH, 6 * NSA_KV_DIM, 3 * GROUP_HEADS,
)
IN_COLS = sum(IN_WIDTHS)

kernel_name = "hymba_style_diffattn_mlstm_hgrn2_nsa_hmoe"

def rms_norm(x, gain):
    xf = x.astype(F32)
    y = xf * lax.rsqrt(jnp.mean(xf * xf, axis=-1, keepdims=True) + EPS)
    return (y * gain.astype(F32)).astype(x.dtype)

def alibi_slopes():
    n = 2 * GROUP_HEADS
    s = 2.0 ** (-8.0 * np.arange(1, n + 1) / n)
    return jnp.asarray(s[0::2], F32), jnp.asarray(s[1::2], F32)

def causal_depthwise_conv(x, w):
    k_len, ch = w.shape
    xp = jnp.pad(x, ((0, 0), (k_len - 1, 0), (0, 0)))
    return lax.conv_general_dilated(xp, w[:, None, :].astype(x.dtype), (1,), 'VALID',
                                    dimension_numbers=('NWC', 'WIO', 'NWC'), feature_group_count=ch)

def diff_attention(q_in, k_in, v_in, q_gain, k_gain, lam_vecs, sub_gain, slopes, layer_idx):
    B, S, _ = q_in.shape
    H = GROUP_HEADS
    q = rms_norm(q_in.reshape(B, S, H, 2, DIFF_HALF), q_gain) * (DIFF_HALF ** -0.5)
    k = rms_norm(k_in.reshape(B, S, H, 2, DIFF_HALF), k_gain)
    v = v_in.reshape(B, S, H, HEAD_DIM)
    lam_init = 0.8 - 0.6 * math.exp(-0.3 * layer_idx)
    lv = lam_vecs.astype(F32)
    lam = jnp.exp(jnp.dot(lv[0], lv[1])) - jnp.exp(jnp.dot(lv[2], lv[3])) + lam_init
    nb = S // Q_BLOCK
    q_blocks = q.reshape(B, nb, Q_BLOCK, H, 2, DIFF_HALF).swapaxes(0, 1)
    k_pos = jnp.arange(S)

    def attend_block(args):
        q_blk, bi = args
        q_pos = bi * Q_BLOCK + jnp.arange(Q_BLOCK)
        dist = q_pos[:, None] - k_pos[None, :]
        s = jnp.einsum('bqhcd,bkhcd->bhcqk', q_blk, k).astype(F32)
        s = s - slopes[None, :, None, None, None] * dist.astype(F32)
        s = jnp.where(dist >= 0, s, NEG_INF)
        p = jax.nn.softmax(s, axis=-1)
        a = p[:, :, 0] - lam * p[:, :, 1]
        return jnp.einsum('bhqk,bkhd->bqhd', a.astype(v.dtype), v)

    o = lax.map(attend_block, (q_blocks, jnp.arange(nb)))
    o = o.swapaxes(0, 1).reshape(B, S, H, HEAD_DIM)
    o = rms_norm(o, sub_gain) * (1.0 - lam_init)
    return o.reshape(B, S, GROUP_WIDTH)

def mlstm(q_in, k_in, v_in, i_pre, f_pre, o_pre, out_gain):
    B, S, _ = q_in.shape
    H, d, L = GROUP_HEADS, HEAD_DIM, MLSTM_CHUNK
    nc = S // L

    def to_chunks(t, width):
        return t.astype(F32).reshape(B, nc, L, H, width).transpose(1, 0, 3, 2, 4)

    q = to_chunks(q_in, d) * (d ** -0.5)
    k = to_chunks(k_in, d)
    v = to_chunks(v_in, d)
    log_f = to_chunks(jax.nn.log_sigmoid(f_pre.astype(F32))[..., None], 1)[..., 0]
    log_i = to_chunks(i_pre[..., None], 1)[..., 0]
    causal = jnp.tril(jnp.ones((L, L), dtype=bool))

    def chunk_step(carry, inp):
        C, n, m = carry
        q_c, k_c, v_c, lf, li = inp
        g = jnp.cumsum(lf, axis=-1)
        g_last = g[..., -1]
        log_d = jnp.where(causal, g[..., :, None] - g[..., None, :] + li[..., None, :], NEG_INF)
        log_inter = g + m[..., None]
        m_t = jnp.maximum(log_inter, jnp.max(log_d, axis=-1))
        w_intra = jnp.einsum('bhtd,bhsd->bhts', q_c, k_c) * jnp.exp(log_d - m_t[..., None])
        w_inter = jnp.exp(log_inter - m_t)
        num = (w_inter[..., None] * jnp.einsum('bhtd,bhde->bhte', q_c, C)
               + jnp.einsum('bhts,bhse->bhte', w_intra, v_c))
        den = w_inter * jnp.einsum('bhtd,bhd->bht', q_c, n) + jnp.sum(w_intra, axis=-1)
        h = num / jnp.maximum(jnp.abs(den), jnp.exp(-m_t))[..., None]
        log_a = g_last[..., None] - g + li
        m_new = jnp.maximum(g_last + m, jnp.max(log_a, axis=-1))
        a = jnp.exp(log_a - m_new[..., None])
        decay = jnp.exp(g_last + m - m_new)
        C_new = decay[..., None, None] * C + jnp.einsum('bhs,bhsd,bhse->bhde', a, k_c, v_c)
        n_new = decay[..., None] * n + jnp.einsum('bhs,bhsd->bhd', a, k_c)
        return (C_new, n_new, m_new), h

    init = (jnp.zeros((B, H, d, d), F32), jnp.zeros((B, H, d), F32), jnp.zeros((B, H), F32))
    _, h = lax.scan(chunk_step, init, (q, k, v, log_f, log_i))
    h = h.transpose(1, 0, 3, 2, 4).reshape(B, S, H, d)
    h = rms_norm(h, out_gain) * jax.nn.sigmoid(o_pre.astype(F32)).reshape(B, S, H, d)
    return h.reshape(B, S, GROUP_WIDTH)

def hgrn2(q_in, f_in, i_in, g_in, lower_bound, out_gain):
    B, S, _ = q_in.shape
    H, dk, dv, L = GROUP_HEADS, HGRN_KEY, HEAD_DIM, HGRN_CHUNK
    nc = S // L
    lb = lower_bound.astype(F32)
    log_f = jnp.logaddexp(jnp.log(jnp.maximum(lb, LB_FLOOR)),
                          jnp.log1p(-lb) + jax.nn.log_sigmoid(f_in.astype(F32)))
    k = -jnp.expm1(log_f)
    q = jax.nn.silu(q_in.astype(F32))

    def to_chunks(t, width):
        return t.astype(F32).reshape(B, nc, L, H, width).transpose(1, 0, 3, 2, 4)

    causal = jnp.tril(jnp.ones((L, L), dtype=bool))

    def chunk_step(state, inp):
        q_c, k_c, v_c, lf = inp
        b = jnp.cumsum(lf, axis=2)
        b_last = b[:, :, -1]
        inter = jnp.einsum('bhtk,bhkv->bhtv', q_c * jnp.exp(b), state)
        rel = jnp.where(causal[:, :, None], b[:, :, :, None, :] - b[:, :, None, :, :], NEG_INF)
        attn = jnp.einsum('bhtk,bhsk,bhtsk->bhts', q_c, k_c, jnp.exp(rel))
        o = inter + jnp.einsum('bhts,bhsv->bhtv', attn, v_c)
        state = (jnp.exp(b_last)[..., None] * state
                 + jnp.einsum('bhsk,bhsv->bhkv', k_c * jnp.exp(b_last[:, :, None] - b), v_c))
        return state, o

    init = jnp.zeros((B, H, dk, dv), F32)
    _, o = lax.scan(chunk_step, init,
                    (to_chunks(q, dk), to_chunks(k, dk), to_chunks(i_in, dv), to_chunks(log_f, dk)))
    o = o.transpose(1, 0, 3, 2, 4).reshape(B, S, H, dv)
    o = rms_norm(o, out_gain) * jax.nn.sigmoid(g_in.astype(F32)).reshape(B, S, H, dv)
    return o.reshape(B, S, GROUP_WIDTH)

def nsa(q_in, kv_in, gate_in, cmp_pos, cmp_w1, cmp_w2, q_gain, k_gain, out_gain, slopes):
    B, S, _ = q_in.shape
    H, d = GROUP_HEADS, HEAD_DIM
    k_c, v_c, k_s, v_s, k_w, v_w = jnp.split(kv_in, 6, axis=-1)
    q = rms_norm(q_in.reshape(B, S, H, d), q_gain) * (d ** -0.5)
    t_pos = jnp.arange(S)

    n_cmp = (S - CMP_LEN) // CMP_STRIDE + 1
    cmp_start = jnp.arange(n_cmp) * CMP_STRIDE
    cmp_idx = cmp_start[:, None] + jnp.arange(CMP_LEN)[None, :]

    def compress(t, j):
        blocks = t[:, cmp_idx] + cmp_pos[j]
        hdn = jax.nn.gelu(blocks.reshape(B, n_cmp, CMP_LEN * d) @ cmp_w1[j])
        return hdn @ cmp_w2[j]

    k_cmp = rms_norm(compress(k_c, 0), k_gain[0])
    v_cmp = compress(v_c, 1)
    dist_c = t_pos[:, None] - (cmp_start + CMP_LEN - 1)[None, :]
    s_c = (jnp.einsum('bshd,bnd->bhsn', q, k_cmp).astype(F32)
           - slopes[None, :, None, None] * dist_c.astype(F32))
    valid_c = dist_c >= 0
    p_c = jnp.where(valid_c, jax.nn.softmax(jnp.where(valid_c, s_c, NEG_INF), axis=-1), 0.0)
    o_cmp = jnp.einsum('bhsn,bnd->bshd', p_c.astype(v_cmp.dtype), v_cmp)

    n_sel = S // SEL_BLOCK
    n_top = min(SEL_TOPK, n_sel)
    sel_start = jnp.arange(n_sel) * SEL_BLOCK
    overlap = jnp.clip(jnp.minimum(cmp_start[:, None] + CMP_LEN, sel_start[None, :] + SEL_BLOCK)
                       - jnp.maximum(cmp_start[:, None], sel_start[None, :]), 0) / CMP_LEN
    importance = jnp.einsum('bhsn,nj->bsj', p_c, overlap.astype(F32))
    q_blk = t_pos // SEL_BLOCK
    blk = jnp.arange(n_sel)
    importance = jnp.where(blk[None, :] <= q_blk[:, None], importance, -1.0)
    forced = ((blk[None, :] == 0) | (blk[None, :] == q_blk[:, None])
              | (blk[None, :] == q_blk[:, None] - 1))
    importance = jnp.where(forced, 2.0, importance)
    _, sel_idx = lax.top_k(importance, n_top)

    k_sel_blocks = rms_norm(k_s, k_gain[1]).reshape(B, n_sel, SEL_BLOCK, d)
    v_sel_blocks = v_s.reshape(B, n_sel, SEL_BLOCK, d)
    nqb = S // Q_BLOCK
    q_blocks = q.reshape(B, nqb, Q_BLOCK, H, d).swapaxes(0, 1)
    idx_blocks = sel_idx.reshape(B, nqb, Q_BLOCK, n_top).swapaxes(0, 1)
    gather = jax.vmap(lambda blocks, ids: blocks[ids])

    def select_block(args):
        q_b, ids, bi = args
        kg = gather(k_sel_blocks, ids)
        vg = gather(v_sel_blocks, ids)
        q_pos = bi * Q_BLOCK + jnp.arange(Q_BLOCK)
        k_pos = ids[..., None] * SEL_BLOCK + jnp.arange(SEL_BLOCK)
        dist = (q_pos[None, :, None, None] - k_pos)[:, None]
        s = (jnp.einsum('bqhd,bqnld->bhqnl', q_b, kg).astype(F32)
             - slopes[None, :, None, None, None] * dist.astype(F32))
        s = jnp.where(dist >= 0, s, NEG_INF).reshape(B, H, Q_BLOCK, n_top * SEL_BLOCK)
        p = jax.nn.softmax(s, axis=-1).reshape(B, H, Q_BLOCK, n_top, SEL_BLOCK)
        return jnp.einsum('bhqnl,bqnld->bqhd', p.astype(vg.dtype), vg)

    o_sel = lax.map(select_block, (q_blocks, idx_blocks, jnp.arange(nqb)))
    o_sel = o_sel.swapaxes(0, 1).reshape(B, S, H, d)

    n_back = WINDOW // Q_BLOCK
    k_win = rms_norm(k_w, k_gain[2]).reshape(B, nqb, Q_BLOCK, d)
    v_win = v_w.reshape(B, nqb, Q_BLOCK, d)

    def band(t):
        tp = jnp.pad(t, ((0, 0), (n_back, 0), (0, 0), (0, 0)))
        return jnp.concatenate([tp[:, j:j + nqb] for j in range(n_back + 1)], axis=2)

    k_band, v_band = band(k_win), band(v_win)
    q_pos = jnp.arange(nqb)[:, None] * Q_BLOCK + jnp.arange(Q_BLOCK)[None, :]
    k_pos = (jnp.arange(nqb)[:, None] - n_back) * Q_BLOCK + jnp.arange((n_back + 1) * Q_BLOCK)[None, :]
    dist = q_pos[:, :, None] - k_pos[:, None, :]
    in_win = (dist >= 0) & (dist < WINDOW) & (k_pos[:, None, :] >= 0)
    s_w = jnp.einsum('bnqhd,bnkd->bnhqk', q.reshape(B, nqb, Q_BLOCK, H, d), k_band).astype(F32)
    s_w = s_w - slopes[None, None, :, None, None] * dist[None, :, None].astype(F32)
    s_w = jnp.where(in_win[None, :, None], s_w, NEG_INF)
    p_w = jax.nn.softmax(s_w, axis=-1)
    o_win = jnp.einsum('bnhqk,bnkd->bnqhd', p_w.astype(v_band.dtype), v_band).reshape(B, S, H, d)

    gates = jax.nn.sigmoid(gate_in.astype(F32)).reshape(B, S, H, 3)
    o = gates[..., 0:1] * o_cmp + gates[..., 1:2] * o_sel + gates[..., 2:3] * o_win
    o = rms_norm(o, out_gain)
    return o.reshape(B, S, GROUP_WIDTH)

def hier_moe(h, w_group, b_group, w_expert, b_expert, w_gate, w_up, w_down):
    B, S, D = h.shape
    t = h.reshape(B * S, D)
    p_group = jax.nn.softmax((t @ w_group).astype(F32) + b_group, axis=-1)
    g_sel = jnp.argmax(p_group, axis=-1)
    g_prob = jnp.max(p_group, axis=-1)
    logits_e = ((t @ w_expert).astype(F32) + b_expert).reshape(-1, N_GROUPS, EXPERTS_PER_GROUP)
    logits_e = jnp.take_along_axis(logits_e, g_sel[:, None, None], axis=1)[:, 0]
    top_p, top_i = lax.top_k(jax.nn.softmax(logits_e, axis=-1), TOPK_IN_GROUP)
    top_w = g_prob[:, None] * top_p / jnp.sum(top_p, axis=-1, keepdims=True)
    w_e = jnp.sum(jax.nn.one_hot(top_i, EXPERTS_PER_GROUP, dtype=F32) * top_w[..., None], axis=1)
    gate = jax.nn.one_hot(g_sel, N_GROUPS, dtype=F32)[:, :, None] * w_e[:, None, :]
    out = jnp.zeros_like(t)
    for g in range(N_GROUPS):
        a = jnp.einsum('td,edf->tef', t, w_gate[g])
        u = jnp.einsum('td,edf->tef', t, w_up[g])
        act = jax.nn.silu(a) * u * gate[:, g, :, None].astype(t.dtype)
        out = out + jnp.einsum('tef,efd->td', act, w_down[g])
    return out.reshape(B, S, D)

def setup_inputs(seed: int = 0) -> dict:
    key = jax.random.key(seed)
    keys = iter(jax.random.split(key, 40))

    def nrm(shape, scale):
        return jax.random.normal(next(keys), shape, F32) * scale

    L = DEPTH
    n_exp = N_GROUPS * EXPERTS_PER_GROUP
    f_bias = jnp.linspace(3.0, 6.0, GROUP_HEADS, dtype=F32)
    return {
        'x': nrm((BATCH, SEQ, D_MODEL), 1.0),
        'norm_mix': 1.0 + nrm((L, D_MODEL), 0.02),
        'norm_ffn': 1.0 + nrm((L, D_MODEL), 0.02),
        'w_in': nrm((L, D_MODEL, IN_COLS), D_MODEL ** -0.5),
        'w_out': nrm((L, MIX_WIDTH, D_MODEL), MIX_WIDTH ** -0.5),
        'diff_q_gain': 1.0 + nrm((L, DIFF_HALF), 0.02),
        'diff_k_gain': 1.0 + nrm((L, DIFF_HALF), 0.02),
        'diff_lambda': nrm((L, 4, DIFF_HALF), 0.1),
        'diff_sub_gain': 1.0 + nrm((L, GROUP_HEADS, HEAD_DIM), 0.02),
        'mlstm_conv': nrm((L, MLSTM_CONV, 2 * GROUP_WIDTH), MLSTM_CONV ** -0.5),
        'mlstm_gate_bias': jnp.stack([nrm((L, GROUP_HEADS), 0.1),
                                      f_bias + nrm((L, GROUP_HEADS), 0.1)], axis=1),
        'mlstm_out_gain': 1.0 + nrm((L, GROUP_HEADS, HEAD_DIM), 0.02),
        'hgrn_lower_bounds': nrm((L, GROUP_HEADS * HGRN_KEY), 0.5),
        'hgrn_out_gain': 1.0 + nrm((L, GROUP_HEADS, HEAD_DIM), 0.02),
        'nsa_cmp_pos': nrm((L, 2, CMP_LEN, HEAD_DIM), 0.1),
        'nsa_cmp_w1': nrm((L, 2, CMP_LEN * HEAD_DIM, HEAD_DIM), (CMP_LEN * HEAD_DIM) ** -0.5),
        'nsa_cmp_w2': nrm((L, 2, HEAD_DIM, HEAD_DIM), HEAD_DIM ** -0.5),
        'nsa_q_gain': 1.0 + nrm((L, HEAD_DIM), 0.02),
        'nsa_k_gain': 1.0 + nrm((L, 3, HEAD_DIM), 0.02),
        'nsa_out_gain': 1.0 + nrm((L, GROUP_HEADS, HEAD_DIM), 0.02),
        'moe_w_group': nrm((L, D_MODEL, N_GROUPS), D_MODEL ** -0.5),
        'moe_b_group': nrm((L, N_GROUPS), 0.01),
        'moe_w_expert': nrm((L, D_MODEL, n_exp), D_MODEL ** -0.5),
        'moe_b_expert': nrm((L, n_exp), 0.01),
        'moe_w_gate': nrm((L, N_GROUPS, EXPERTS_PER_GROUP, D_MODEL, D_EXPERT), D_MODEL ** -0.5),
        'moe_w_up': nrm((L, N_GROUPS, EXPERTS_PER_GROUP, D_MODEL, D_EXPERT), D_MODEL ** -0.5),
        'moe_w_down': nrm((L, N_GROUPS, EXPERTS_PER_GROUP, D_EXPERT, D_MODEL), D_EXPERT ** -0.5),
    }

def reference(x, norm_mix, norm_ffn, w_in, w_out, diff_q_gain, diff_k_gain, diff_lambda, diff_sub_gain,
              mlstm_conv, mlstm_gate_bias, mlstm_out_gain, hgrn_lower_bounds, hgrn_out_gain,
              nsa_cmp_pos, nsa_cmp_w1, nsa_cmp_w2, nsa_q_gain, nsa_k_gain, nsa_out_gain,
              moe_w_group, moe_b_group, moe_w_expert, moe_b_expert, moe_w_gate, moe_w_up, moe_w_down):
    slopes_diff, slopes_nsa = alibi_slopes()
    lb_soft = jax.nn.softmax(hgrn_lower_bounds.astype(F32), axis=0)
    lower_bounds = jnp.cumsum(lb_soft, axis=0) - lb_soft[0]
    split_at = [int(v) for v in np.cumsum(IN_WIDTHS)[:-1]]
    for l in range(DEPTH):
        h = rms_norm(x, norm_mix[l])
        (a_q, a_k, a_v, b_q, b_k, b_v, b_i, b_f, b_o,
         c_q, c_f, c_i, c_g, d_q, d_kv, d_g) = jnp.split(h @ w_in[l], split_at, axis=-1)
        y_a = diff_attention(a_q, a_k, a_v, diff_q_gain[l], diff_k_gain[l], diff_lambda[l],
                             diff_sub_gain[l], slopes_diff, l)
        qk = jax.nn.silu(causal_depthwise_conv(jnp.concatenate([b_q, b_k], axis=-1), mlstm_conv[l]))
        y_b = mlstm(qk[..., :GROUP_WIDTH], qk[..., GROUP_WIDTH:], b_v,
                    b_i + mlstm_gate_bias[l, 0], b_f + mlstm_gate_bias[l, 1], b_o, mlstm_out_gain[l])
        y_c = hgrn2(c_q, c_f, c_i, c_g, lower_bounds[l], hgrn_out_gain[l])
        y_d = nsa(d_q, d_kv, d_g, nsa_cmp_pos[l], nsa_cmp_w1[l], nsa_cmp_w2[l], nsa_q_gain[l],
                  nsa_k_gain[l], nsa_out_gain[l], slopes_nsa)
        mixed = jnp.concatenate([y_a.astype(x.dtype), y_b.astype(x.dtype),
                                 y_c.astype(x.dtype), y_d.astype(x.dtype)], axis=-1)
        x = x + mixed @ w_out[l]
        x = x + hier_moe(rms_norm(x, norm_ffn[l]), moe_w_group[l], moe_b_group[l], moe_w_expert[l],
                         moe_b_expert[l], moe_w_gate[l], moe_w_up[l], moe_w_down[l])
    return x


_drawn_inputs = setup_inputs


def setup_inputs(seed=0):
    import zlib

    import numpy as np

    out = dict(_drawn_inputs(seed))
    spreads = {}
    factors = {'diff_q_gain': 2.94,
     'mlstm_out_gain': 3.286,
     'hgrn_out_gain': 2.742,
     'nsa_q_gain': 5.016,
     'nsa_k_gain': 4.093,
     'moe_b_group': 3.208,
     'moe_b_expert': 3.264,
     'nsa_out_gain': 2.77}
    for name, (base, spread) in spreads.items():
        noise = np.random.default_rng([zlib.crc32(name.encode()), seed]).standard_normal(out[name].shape)
        drawn = base * np.exp(spread * noise) if base else spread * noise
        out[name] = jnp.asarray(drawn.astype(out[name].dtype))
    for name, factor in factors.items():
        out[name] = (out[name] * factor).astype(out[name].dtype)
    return out
```

```python
import math
from contextlib import ExitStack

import numpy as np
import concourse.bass as bass
from concourse import mybir

F32 = mybir.dt.float32
I32 = mybir.dt.int32
ALU = mybir.AluOpType
ACT = mybir.ActivationFunctionType
AX = mybir.AxisListType

LAYERS, SEQ, DIM = 2, 512, 1024
P = 128
NC = SEQ // P
KD = DIM // P
HEADS, HD = 4, 64
GW = HEADS * HD
HALF = HD // 2
IN_COLS = 3476
EPS = 1e-6
NEG = -1e30
CMP_LEN, CMP_STRIDE = 32, 16
NCMP = (SEQ - CMP_LEN) // CMP_STRIDE + 1
EXPERTS, GROUPS, PER_GROUP, FF = 32, 4, 8, 256
HB = 32
NB = SEQ // HB
LEVELS = 5
LN_SPLIT = 2.0 ** 50

AQ, AK, AV, BV, BI, BF, BO, CI, CG, DQ, KS, VS, KW, VW, DG, PW = (
    0, 256, 512, 768, 1024, 1028, 1032, 1288, 1544, 1800, 2056, 2120, 2184, 2248, 2312, 2324)
W_IN = [(0, 512), (2824, 384), (3208, 268), (512, 256), (768, 512), (1800, 512), (1280, 260), (1540, 260),
        (2312, 512)]
PROJ = [
    [("n", 0, 512, AQ)],
    [("n", 0, 256, DQ), ("t", 256, 128, "kv")],
    [("n", 0, 268, KS)],
    [("n", 0, 256, AV)],
    [("t", 128 * i, 128, f"m{i}") for i in range(4)],
    [("t", 128 * i, 128, f"g{i}") for i in range(4)],
    [("n", 0, 260, BV)],
    [("n", 0, 260, BF)],
    [("n", 0, 512, CI)],
]
LOADS = len(W_IN) + 2

R_DQ, R_DK, R_NQ, R_NK, R_OG, R_BG, R_BE, R_LAM, RW = 0, 32, 64, 128, 320, 1344, 1348, 1380, 1508
C_NM, C_NF, C_CONV, C_POS, C_LB, C_GB, CW = 0, 8, 16, 32, 64, 68, 70
K_ID, K_LVL, K_CAUS, K_CMPB, K_CMPV, K_SEG, K_IOTA, KW_ALL = (
    0, 128, 896, 1024, 1520, 1644, 2156, 2164)

MAPS = []
for _h in range(HEADS):
    for _c in range(2):
        MAPS.append((_h // 2, 2 + _h // 2, 64 * (_h % 2) + 32 * _c, HALF, AV + HD * _h, _h, _h))
for _h in range(HEADS):
    for _c in range(2):
        MAPS.append((4 + _h // 2, 6 + _c, 64 * (_h % 2), HD, (VS, VW)[_c], HEADS + _h, 12 + _h))
ITERS = [(m, c) for m in range(len(MAPS)) for c in range(NC)]


ST = 1200
MOE_UNROLL = 2
MOE_TILES = 12 * MOE_UNROLL
MOE_TURNS = EXPERTS // MOE_UNROLL
WOFF = [0, 512, 896, 1152]
ROOTS = 5


def attention_order():
    out = []
    for i in range(len(ITERS) + 2):
        if i < len(ITERS):
            out.append(("S", i))
        if 0 <= i - 1 < len(ITERS):
            out.append(("T", i - 1))
        if 0 <= i - 2:
            out.append(("O", i - 2))
    return out


def psum_plan():
    at, n = {}, 0

    def add(key):
        nonlocal n
        at[key] = n
        n += 1

    for l in range(LAYERS):
        for k in range(KD):
            add((l, "ht", k))
        for g, parts in enumerate(PROJ):
            for kind, _, _, what in parts:
                if kind == "t":
                    add((l, "pt", what))
                else:
                    for c in range(NC):
                        add((l, "pn", g, c))
        for j in range(8):
            add((l, "qk", j))
        for j in range(2):
            add((l, "ch", j))
        for j in range(2):
            add((l, "cc", j))
        add((l, "ck"))
        for o in range(2):
            add((l, "cs", o))
        for c in range(NC):
            add((l, "cp", c))
        for c in range(NC):
            add((l, "co", c))
        for kind, i in attention_order():
            add((l, kind, i))
        add((l, "gi"))
        add((l, "gf"))
        add((l, "gc"))
        for h in range(HEADS):
            add((l, "mb", h))
            for s in range(NC):
                add((l, "ms", h, s))
            add((l, "mo", h))
        for lev in range(LEVELS + 1):
            for h in range(HEADS):
                add((l, "ha", lev, h))
        for hp in range(2):
            add((l, "hn", hp))
        for j in range(P // HB):
            for hp in range(2):
                add((l, "hu", hp, j))
        for c in range(NC):
            for o in range(2):
                add((l, "ho", c, o))
        for k in range(KD):
            add((l, "yt", k))
        for c in range(NC):
            for j in range(2):
                add((l, "wo", c, j))
        for k in range(KD):
            add((l, "h2", k))
        add((l, "rt"))
        at[(l, "moe")] = n
        n += MOE_TILES * MOE_TURNS
    return at


class Steps:

    def __init__(self, eng, own):
        self.eng, self.own, self.n = eng, own, {}

    def count(self, ins, sem):
        ins.then_inc(sem, 1)
        self.n[id(sem)] = self.n.get(id(sem), 0) + 1
        return self.n[id(sem)]

    def then(self, ins, sem=None):
        sem = self.own if sem is None else sem
        self.eng.wait_ge(sem, self.count(ins, sem))


def build(nc, d, out):
    ctx = ExitStack()
    with ctx:
        def sb(name, shape, dt=F32):
            return ctx.enter_context(nc.sbuf_tensor(name, shape, dt))

        def sem(name):
            return ctx.enter_context(nc.semaphore(name))

        X = sb("X", [P, NC, DIM])
        hT = sb("hT", [P, KD, SEQ])
        K = sb("K", [P, KW_ALL])
        R = sb("R", [P, RW])
        C = sb("C", [P, CW])
        M = sb("area", [P, 39008])
        st = sb("stats", [P, ST])

        def area(a, shape):
            n = int(np.prod(shape))
            v = M[:, a:a + n]
            if len(shape) == 2:
                v = v.rearrange("p (a b) -> p a b", a=shape[0])
            if len(shape) == 3:
                v = v.rearrange("p (a b c) -> p a b c", a=shape[0], b=shape[1])
            return v

        tok = area(0, [NC, DIM])
        Pn = area(4096, [NC, PW])
        wring = area(13392, [2, KD, 512])
        bias = area(21584, [8, 512])
        QKT = area(25680, [8, SEQ])
        mraw = area(29776, [4, SEQ + 3])
        mqk = area(31836, [4, SEQ])
        hqf = area(33884, [4, SEQ])
        negS = area(35932, [2, 512])
        prob = area(36956, [2, 512])
        probT = area(37980, [2, 512])
        w1 = area(31836, [2, 16, HD])
        kcT = area(35932, [2, SEQ])
        Sc = area(36956, [16, NCMP])
        w2 = area(37984, [2, HD])
        PcT = area(31836, [16, P])
        gA, gMt, gM = (area(21584 + SEQ * i, [SEQ])[0:HEADS, :] for i in range(3))
        WT = area(25680, [2, 1280])
        D = area(28240, [2, SEQ])
        E = area(35932, [2, SEQ])
        Vm = area(36956, [NC, HEADS, HD + 1])
        b = area(25680, [2, SEQ])
        kk = area(26704, [2, SEQ])
        Xe = area(27728, [2, SEQ])
        qt = area(28752, [2, SEQ])
        kt = area(29776, [2, SEQ])
        kn = area(30800, [2, NC, P])
        A = area(31836, [HEADS, SEQ])
        St = area(21584, [2, 16, P])
        ering = area(0, [2, 6144])
        h2n = area(24576, [NC, DIM])
        actT = area(28672, [2, 2, SEQ])
        sil = area(30720, [2, SEQ])
        wr = area(31744, [KD, 36])
        rt = area(32100, [NC, 36])

        ident = K[:, K_ID:K_ID + P]
        caus = K[:, K_CAUS:K_CAUS + P]

        psum = [ctx.enter_context(nc.psum_tensor(f"bank{i}", [P, 512], F32)) for i in range(8)]
        at = psum_plan()

        at_st = [0]

        def small(*shape):
            n = int(np.prod(shape))
            v = st[:, at_st[0]:at_st[0] + n]
            at_st[0] += n
            if len(shape) == 2:
                v = v.rearrange("p (a b) -> p a b", a=shape[0])
            if len(shape) == 3:
                v = v.rearrange("p (a b c) -> p a b c", a=shape[0], b=shape[1])
            return v

        Hd, posb, Kc, KcT, Vc = small(2, NCMP), small(2), small(2, HD), small(NCMP), small(HD)
        nmax, psumcol, fac = small(len(ITERS)), small(len(ITERS)), small(len(ITERS))
        ms, rs = small(88), small(88)
        lam4, lam = small(2), small(1)
        cmx, cfac = small(16), small(16)
        gcol = small(2, NC, HEADS)
        mden = small(NC)
        lbx, lbs, lbc = small(2, 2), small(2, 2), small(4, 2)
        dec = small(2, NB)

        nopcell, tmp = small(1), sb("scratch", [P, 2 * HD])
        rbest, rsecond, rmark, gprob, rx1 = (small(NC) for _ in range(5))
        ghot, rx0 = small(NC, GROUPS), small(NC, GROUPS)
        hot1, hot2, l8 = (small(NC, PER_GROUP) for _ in range(3))
        rx = (rx0, rx1)
        gate = small(NC, GROUPS, PER_GROUP)
        assert at_st[0] <= ST

        names = """h2_ready const_in x_in par_in w1_in bias_in wr_in out_done
            act_own dve_own ss mean root h_ready kvs qkn_ready ck_n cs_x cs_e cs_p gsig exp_done
            lam_d lam_e conv_m silu_m gate_a gate_b gate_r en_d vm_ready md me w_ready
            lb_a lb_b hsig hF hln hx he hqk hst hq_in sq ysq y_ready rt_x rt_e""".split()
        s = {n: sem(n) for n in names}
        full = [sem(f"bank_full{i}") for i in range(8)]
        free = [sem(f"bank_free{i}") for i in range(8)]
        w_in_sem = [sem(f"w_in{i}") for i in range(2)]
        e_in = [sem(f"expert_in{i}") for i in range(MOE_UNROLL)]

        def take(eng, key):
            n = at[key]
            if n >= 8:
                eng.wait_ge(free[n % 8], n // 8)
            return psum[n % 8]

        def filled(ins, key):
            ins.then_inc(full[at[key] % 8], 1)

        def ready(eng, key):
            n = at[key]
            eng.wait_ge(full[n % 8], n // 8 + 1)
            return psum[n % 8]

        def release(ins, key):
            ins.then_inc(free[at[key] % 8], 1)

        def copied(eng, key):
            n = at[key]
            eng.wait_ge(free[n % 8], n // 8 + 1)

        def experts_done(eng, l):
            n = at[(l, "moe")] + MOE_TILES - 1
            eng.wait_ge(free[n % 8], n // 8 + 1 + MOE_TILES // 8 * (MOE_TURNS - 1))

        def x_ready(eng, l):
            if l:
                experts_done(eng, l - 1)
            else:
                eng.wait_ge(s["x_in"], 16)

        PTILES = []
        for g, parts in enumerate(PROJ):
            for kind, a, n, what in parts:
                for c in range(NC if kind == "n" else 1):
                    PTILES.append((g, kind, a, n, what, c, what == "kv" or len(PTILES) % 2 == 1))

        def ptile(l, g, kind, what, c):
            return (l, "pn", g, c) if kind == "n" else (l, "pt", what)

        LAST_OF = {g: ptile(0, *[(t[0], t[1], t[4], t[5]) for t in PTILES if t[0] == g][-1])[1:]
                   for g in range(len(PROJ))}

        def projected(eng, l, groups, mine):
            for g in groups:
                for t in [t for t in PTILES if t[0] == g][-4:]:
                    copied(eng, ptile(l, g, t[1], t[4], t[5]))

        block = ctx.enter_context(nc.Block())

        @block.sync
        def _(sp):
            sp.dma_start(X[:, :, :], d["x"].rearrange("(c p) n -> p c n", p=P)).then_inc(s["x_in"], 16)
            sp.dma_start(K[:, :], d["constants"]).then_inc(s["const_in"], 16)

            def load_expert(l, e, u):
                for n, name in enumerate(("moe_w_gate", "moe_w_up")):
                    sp.dma_start(ering[:, u, 2048 * n:2048 * n + 2048].rearrange("p (k f) -> p k f", k=KD),
                                 d[name][l, bass.ds(e, 1)].rearrange("e (k p) f -> p (e k) f", p=P)) \
                        .then_inc(e_in[u], 16)
                sp.dma_start(ering[:, u, 4096:6144].rearrange("p (k f) -> p k f", k=2),
                             d["moe_w_down"][l, bass.ds(e, 1)].rearrange("e (k p) f -> p (e k) f", p=P)) \
                    .then_inc(e_in[u], 16)

            for l in range(LAYERS):
                if l:
                    experts_done(sp, l - 1)
                sp.dma_start(R[:, :], d["rows"][l:l + 1, :].to_broadcast([P, RW])).then_inc(s["par_in"], 16)
                sp.dma_start(C[:, :], d["columns"][l]).then_inc(s["par_in"], 16)
                for n in range(LOADS):
                    j = l * LOADS + n
                    if n >= 2:
                        ready(sp, (l,) + LAST_OF[n - 2])
                    if n < len(W_IN):
                        a, w = W_IN[n]
                        src = d["w_in"][l, :, a:a + w].rearrange("(k p) n -> p k n", p=P)
                    else:
                        w = 512
                        a = 512 * (n - len(W_IN))
                        src = d["w_out"][l, :, a:a + w].rearrange("(k p) n -> p k n", p=P)
                    sp.dma_start(wring[:, j % 2, :, 0:w], src).then_inc(w_in_sem[j % 2], 16)
                    if n == 1:
                        for i in range(2):
                            sp.dma_start(w1[:, i], d["nsa_cmp_w1"][l, i].rearrange("(j p) m -> p j m", p=P)) \
                                .then_inc(s["w1_in"], 16)
                        sp.dma_start(w2[0:HD, :, :], d["nsa_cmp_w2"][l].rearrange("j k m -> k j m")) \
                            .then_inc(s["w1_in"], 16)
                        sp.dma_start(bias[:, :, :], d["alibi"].rearrange("p (n m) -> p n m", n=8)) \
                            .then_inc(s["bias_in"], 16)
                copied(sp, (l, "wo", NC - 1, 1))
                sp.dma_start(wr[:, :, 0:GROUPS], d["moe_w_group"][l].rearrange("(k p) n -> p k n", p=P)) \
                    .then_inc(s["wr_in"], 16)
                sp.dma_start(wr[:, :, GROUPS:], d["moe_w_expert"][l].rearrange("(k p) n -> p k n", p=P)) \
                    .then_inc(s["wr_in"], 16)
                base = at[(l, "moe")]
                for u in range(MOE_UNROLL):
                    load_expert(l, u, u)
                with sp.Fori(0, MOE_TURNS - 1) as turn:
                    for u in range(MOE_UNROLL):
                        n = base + 12 * u + 11
                        sp.wait_ge(full[n % 8], turn * (MOE_TILES // 8) + n // 8 + 1)
                        load_expert(l, turn * MOE_UNROLL + MOE_UNROLL + u, u)
            experts_done(sp, LAYERS - 1)
            sp.dma_start(out.rearrange("(c p) n -> p c n", p=P), X[:, :, :]).then_inc(s["out_done"], 16)
            sp.wait_ge(s["out_done"], 16)

        @block.tensor
        def _(pe):
            def to_channels(l, name, src):
                for k in range(KD):
                    t = take(pe, (l, name, k))
                    for c in range(NC):
                        last = pe.transpose(t[:, c * P:(c + 1) * P], src[:, c, k * P:(k + 1) * P], ident)
                    filled(last, (l, name, k))

            def loaded(j):
                pe.wait_ge(w_in_sem[j % 2], 16 * (j // 2 + 1))

            def project(l):
                for g, kind, a, n, what, c, _ in PTILES:
                    j = l * LOADS + g
                    if c == 0 and a == PROJ[g][0][1]:
                        loaded(j)
                    w = wring[:, j % 2]
                    key = ptile(l, g, kind, what, c)
                    t = take(pe, key)
                    for k in range(KD):
                        if kind == "n":
                            last = pe.matmul(t[:, 0:n], hT[:, k, c * P:(c + 1) * P], w[:, k, a:a + n],
                                             start=(k == 0), stop=(k == KD - 1))
                        else:
                            last = pe.matmul(t[:, :], w[:, k, a:a + n], hT[:, k, :],
                                             start=(k == 0), stop=(k == KD - 1))
                    filled(last, key)

            def compress(l):
                pe.wait_ge(s["w1_in"], 48 * (l + 1))
                copied(pe, (l, "pt", "kv"))
                for j in range(2):
                    t = take(pe, (l, "ch", j))
                    for i in range(16):
                        pe.matmul(t[0:HD, 0:NCMP], w1[:, j, i, :],
                                  kcT[:, j, 2 * i:2 * i + CMP_STRIDE * (NCMP - 1) + 1:CMP_STRIDE],
                                  start=(i == 0), stop=(i == 15))
                    for i in range(16):
                        last = pe.matmul(t[0:HD, NCMP:NCMP + 1], w1[:, j, i, :],
                                         C[:, C_POS + 16 * j + i:C_POS + 16 * j + i + 1],
                                         start=(i == 0), stop=(i == 15))
                    filled(last, (l, "ch", j))
                for j in range(2):
                    t = take(pe, (l, "cc", j))
                    copied(pe, (l, "ch", j))
                    filled(pe.matmul(t[0:NCMP, 0:HD], Hd[0:HD, j, :], w2[0:HD, j, :], start=True, stop=True),
                           (l, "cc", j))
                t = take(pe, (l, "ck"))
                pe.wait_ge(s["ck_n"], l + 1)
                filled(pe.transpose(t[:, 0:NCMP], Kc[0:NCMP, :, :].rearrange("p a b -> p (a b)"),
                                    ident[0:NCMP, 0:NCMP]), (l, "ck"))
                copied(pe, (l, "ck"))
                for o in range(2):
                    t = take(pe, (l, "cs", o))
                    for c in range(NC):
                        for i in range(2):
                            n = (2 * c + i) * NCMP
                            last = pe.matmul(t[:, n:n + NCMP], QKT[64 * o:64 * o + HD, 4 + i, c * P:(c + 1) * P],
                                             KcT[64 * o:64 * o + HD, :], start=True, stop=True)
                    filled(last, (l, "cs", o))
                pe.wait_ge(s["cs_p"], l + 1)
                for c in range(NC):
                    t = take(pe, (l, "cp", c))
                    for h in range(HEADS):
                        last = pe.transpose(t[0:NCMP, h * P:(h + 1) * P], Sc[:, c * HEADS + h, :], ident)
                    filled(last, (l, "cp", c))
                copied(pe, (l, "cc", 1))
                for c in range(NC):
                    t = take(pe, (l, "co", c))
                    copied(pe, (l, "cp", c))
                    for h in range(HEADS):
                        last = pe.matmul(t[:, h * HD:(h + 1) * HD], PcT[0:NCMP, c * HEADS + h, :], Vc[0:NCMP, :],
                                         start=True, stop=True)
                    filled(last, (l, "co", c))

            def attend(l):
                for kind, i in attention_order():
                    m, c = ITERS[i]
                    q, k, o, depth, v, _, _ = MAPS[m]
                    n = (c + 1) * P
                    t = take(pe, (l, kind, i))
                    if kind == "S":
                        last = pe.matmul(t[:, 0:n], QKT[o:o + depth, q, c * P:(c + 1) * P],
                                         QKT[o:o + depth, k, 0:n], start=True, stop=True, tile_position=(o, 0))
                    elif kind == "T":
                        pe.wait_ge(s["exp_done"], len(ITERS) * l + i + 1)
                        for j in range(c + 1):
                            last = pe.transpose(t[:, j * P:(j + 1) * P], prob[:, i % 2, j * P:(j + 1) * P], ident)
                    else:
                        copied(pe, (l, "T", i))
                        for j in range(c + 1):
                            last = pe.matmul(t[:, 0:HD], probT[:, i % 2, j * P:(j + 1) * P],
                                             Pn[:, j, v:v + HD], start=(j == 0), stop=(j == c))
                    filled(last, (l, kind, i))

            def mlstm(l):
                for name, a in (("gi", BI), ("gf", BF)):
                    t = take(pe, (l, name))
                    for c in range(NC):
                        last = pe.transpose(t[0:HEADS, c * P:(c + 1) * P], Pn[:, c, a:a + HEADS], ident)
                    filled(last, (l, name))
                t = take(pe, (l, "gc"))
                pe.wait_ge(s["gate_r"], l + 1)
                for n, row in enumerate((gA, gMt)):
                    for c in range(NC):
                        last = pe.transpose(t[:, 16 * n + HEADS * c:16 * n + HEADS * c + HEADS],
                                            row[:, c * P:(c + 1) * P], ident[0:HEADS, 0:HEADS])
                filled(last, (l, "gc"))
                pe.wait_ge(s["silu_m"], l + 1)
                pe.wait_ge(s["vm_ready"], l + 1)
                for h in range(HEADS):
                    o = 64 * (h % 2)
                    t = take(pe, (l, "mb", h))
                    filled(pe.matmul(t[:, :], ident[0:HEADS, h:h + 1].to_broadcast([HEADS, P]), gM[:, :],
                                     start=True, stop=True), (l, "mb", h))
                    for c in range(NC):
                        t = take(pe, (l, "ms", h, c))
                        filled(pe.matmul(t[:, 0:SEQ - c * P], mqk[o:o + HD, 2 + h // 2, c * P:(c + 1) * P],
                                         mqk[o:o + HD, h // 2, c * P:SEQ], start=True, stop=True), (l, "ms", h, c))
                    t = take(pe, (l, "mo", h))
                    pe.wait_ge(s["w_ready"], NC * (HEADS * l + h + 1))
                    for c in range(NC):
                        for j in range(c + 1):
                            a = WOFF[j] + (c - j) * P
                            last = pe.matmul(t[:, c * 65:c * 65 + 65], WT[:, h % 2, a:a + P], Vm[:, j, h, :],
                                             start=(j == 0), stop=(j == c))
                    filled(last, (l, "mo", h))

            def hgrn(l):
                for lev in range(LEVELS + 1):
                    qs, ks = (hqf, kk) if lev == 0 else (qt, kt)
                    pe.wait_ge(s["hqk"], (LEVELS + 2) * l + lev + 1)
                    for h in range(HEADS):
                        o = 64 * (h % 2)
                        t = take(pe, (l, "ha", lev, h))
                        for c in range(NC):
                            last = pe.matmul(t[:, c * P:(c + 1) * P], ks[o:o + HD, h // 2, c * P:(c + 1) * P],
                                             qs[o:o + HD, h // 2, c * P:(c + 1) * P], start=True, stop=True)
                        filled(last, (l, "ha", lev, h))
                pe.wait_ge(s["hqk"], (LEVELS + 2) * (l + 1))
                for hp in range(2):
                    t = take(pe, (l, "hn", hp))
                    for c in range(NC):
                        last = pe.transpose(t[:, c * P:(c + 1) * P], kt[:, hp, c * P:(c + 1) * P], ident)
                    filled(last, (l, "hn", hp))
                for hp in range(2):
                    copied(pe, (l, "hn", hp))
                for j in range(P // HB):
                    r = slice(j * HB, (j + 1) * HB)
                    for hp in range(2):
                        t = take(pe, (l, "hu", hp, j))
                        for c in range(NC):
                            last = pe.matmul(t[:, c * P:(c + 1) * P], kn[r, hp, c, :],
                                             Pn[r, c, CI + hp * P:CI + (hp + 1) * P], start=True, stop=True,
                                             tile_position=(j * HB, 0))
                        filled(last, (l, "hu", hp, j))
                pe.wait_ge(s["hq_in"], l + 1)
                pe.wait_ge(s["hst"], l + 1)
                for c in range(NC):
                    for o in range(2):
                        t = take(pe, (l, "ho", c, o))
                        for hp in range(2):
                            h = 2 * hp + o
                            last = pe.matmul(t[:, hp * HD:(hp + 1) * HD], A[:, h, c * P:(c + 1) * P],
                                             Pn[:, c, CI + h * HD:CI + (h + 1) * HD], start=True, stop=False)
                            for j in range(P // HB):
                                i = c * (P // HB) + j
                                last = pe.matmul(t[j * HB:(j + 1) * HB, hp * HD:(hp + 1) * HD],
                                                 qt[64 * o:64 * o + HD, hp, i * HB:(i + 1) * HB],
                                                 St[64 * o:64 * o + HD, hp, i, 64 * o:64 * o + HD],
                                                 start=False, stop=True, tile_position=(64 * o, j * HB))
                        filled(last, (l, "ho", c, o))

            def experts(l):
                base = at[(l, "moe")]
                per = MOE_TILES // 8
                with pe.Fori(0, MOE_TURNS) as turn:
                    for u in range(MOE_UNROLL):
                        w = ering[:, u, :]
                        pe.wait_ge(e_in[u], turn * 48 + 48 * (l * MOE_TURNS + 1))
                        for j in range(4):
                            n = base + 12 * u + j
                            pe.wait_ge(free[n % 8], turn * per + n // 8)
                            t = psum[n % 8]
                            fh, gu = j // 2, j % 2
                            for k in range(KD):
                                a = 2048 * gu + FF * k + P * fh
                                last = pe.matmul(t[:, :], w[:, a:a + P], hT[:, k, :],
                                                 start=(k == 0), stop=(k == KD - 1))
                            last.then_inc(full[n % 8], 1)
                        for j in (1, 3):
                            n = base + 12 * u + j
                            pe.wait_ge(free[n % 8], turn * per + n // 8 + 1)
                        for j in range(8):
                            n = base + 12 * u + 4 + j
                            pe.wait_ge(free[n % 8], turn * per + n // 8)
                            t = psum[n % 8]
                            c, dh = j // 2, j % 2
                            for k in range(2):
                                last = pe.matmul(t[:, :], actT[:, u, k, c * P:(c + 1) * P],
                                                 w[:, 4096 + 1024 * k + 512 * dh:4096 + 1024 * k + 512 * dh + 512],
                                                 start=(k == 0), stop=(k == 1))
                            last.then_inc(full[n % 8], 1)

            pe.wait_ge(s["const_in"], 16)
            for l in range(LAYERS):
                pe.wait_ge(s["h_ready"], l + 1)
                to_channels(l, "ht", tok)
                for k in range(KD):
                    copied(pe, (l, "ht", k))
                project(l)
                pe.wait_ge(s["qkn_ready"], l + 1)
                to_channels(l, "qk", tok)
                for k in range(KD):
                    copied(pe, (l, "qk", k))
                projected(pe, l, (2, 3), False)
                compress(l)
                attend(l)
                projected(pe, l, (6, 7, 8), False)
                mlstm(l)
                hgrn(l)
                pe.wait_ge(s["y_ready"], l + 1)
                to_channels(l, "yt", tok)
                for k in range(KD):
                    copied(pe, (l, "yt", k))
                for j in range(2):
                    loaded(l * LOADS + len(W_IN) + j)
                for c in range(NC):
                    for j in range(2):
                        w = wring[:, (l * LOADS + len(W_IN) + j) % 2]
                        t = take(pe, (l, "wo", c, j))
                        for k in range(KD):
                            last = pe.matmul(t[:, :], hT[:, k, c * P:(c + 1) * P], w[:, k, :],
                                             start=(k == 0), stop=(k == KD - 1))
                        filled(last, (l, "wo", c, j))
                pe.wait_ge(s["h2_ready"], l + 1)
                to_channels(l, "h2", h2n)
                for k in range(KD):
                    copied(pe, (l, "h2", k))
                pe.wait_ge(s["wr_in"], 32 * (l + 1))
                t = take(pe, (l, "rt"))
                for c in range(NC):
                    for k in range(KD):
                        last = pe.matmul(t[:, 36 * c:36 * c + 36], hT[:, k, c * P:(c + 1) * P], wr[:, k, :],
                                         start=(k == 0), stop=(k == KD - 1))
                filled(last, (l, "rt"))
                experts(l)

        @block.scalar
        def _(act):
            sc = Steps(act, s["act_own"])

            def squares(l, junk):
                for c in range(NC):
                    act.activation(junk[:, c, :], X[:, c, :], ACT.Square, accum_out=ms[:, c:c + 1]).then_inc(s["ss"], 1)

            def root(l, u, a):
                act.wait_ge(s["mean"], ROOTS * l + u + 1)
                act.activation(a, a, ACT.Sqrt).then_inc(s["root"], 1)

            def evens(l, name, col):
                for k in range(0, KD, 2):
                    t = ready(act, (l, name, k))
                    if col is None:
                        ins = act.activation(hT[:, k, :] if name != "qk" else QKT[:, k, :], t[:, :], ACT.Copy)
                    else:
                        ins = act.activation(hT[:, k, :], t[:, :], ACT.Copy, scale=C[:, col + k:col + k + 1])
                    release(ins, (l, name, k))

            act.wait_ge(s["const_in"], 16)
            for l in range(LAYERS):
                x_ready(act, l)
                squares(l, tok)
                root(l, 0, ms[:, 0:NC])
                act.wait_ge(s["par_in"], 32 * (l + 1))
                evens(l, "ht", C_NM)
                for g, kind, a, n, what, c, vector in PTILES:
                    if vector:
                        continue
                    key = ptile(l, g, kind, what, c)
                    t = ready(act, key)
                    if kind == "n":
                        ins = act.activation(Pn[:, c, what:what + n], t[:, 0:n], ACT.Copy)
                    elif what[0] == "m":
                        ins = act.activation(mraw[:, int(what[1]), 3:], t[:, :], ACT.Copy)
                    else:
                        ins = act.activation(hqf[:, int(what[1]), :], t[:, :], ACT.Copy)
                    release(ins, key)
                act.wait_ge(s["lam_d"], l + 1)
                act.activation(lam4, lam4, ACT.Exp).then_inc(s["lam_e"], 1)
                projected(act, l, (2, 7, 8), True)
                for a, n in ((DG, 12), (BO, GW), (CG, GW)):
                    act.activation(Pn[:, :, a:a + n], Pn[:, :, a:a + n], ACT.Sigmoid).then_inc(s["gsig"], 1)
                root(l, 1, ms[:, 0:88])
                evens(l, "qk", None)
                for j in range(2):
                    t = ready(act, (l, "ch", j))
                    sc.then(act.activation(posb[0:HD, j:j + 1], t[0:HD, NCMP:NCMP + 1], ACT.Copy))
                    release(act.activation(Hd[0:HD, j, :], t[0:HD, 0:NCMP], ACT.Gelu_apprx_tanh,
                                           bias=posb[0:HD, j:j + 1]), (l, "ch", j))
                root(l, 2, ms[0:NCMP, 0:1])
                act.wait_ge(s["cs_x"], l + 1)
                act.activation(Sc[:, :, :], Sc[:, :, :], ACT.Exp).then_inc(s["cs_e"], 1)
                for i in range(len(ITERS) + 1):
                    if i < len(ITERS):
                        n = (ITERS[i][1] + 1) * P
                        copied(act, (l, "S", i))
                        act.activation(prob[:, i % 2, 0:n], negS[:, i % 2, 0:n], ACT.Exp, scale=-1.0,
                                       bias=nmax[:, i:i + 1], accum_out=psumcol[:, i:i + 1]).then_inc(s["exp_done"], 1)
                    if i:
                        n = (ITERS[i - 1][1] + 1) * P
                        t = ready(act, (l, "T", i - 1))
                        if i >= 3:
                            ready(act, (l, "O", i - 3))
                        release(act.activation(probT[:, (i - 1) % 2, 0:n], t[:, 0:n], ACT.Copy), (l, "T", i - 1))
                act.wait_ge(s["gate_a"], l + 1)
                sc.then(act.activation(gMt[:, :], gMt[:, :], ACT.Exp))
                act.activation(gMt[:, :], gMt[:, :], ACT.Ln, bias=1.0).then_inc(s["gate_b"], 1)
                act.wait_ge(s["conv_m"], l + 1)
                act.activation(mqk[:, :, :], mqk[:, :, :], ACT.Silu).then_inc(s["silu_m"], 1)
                copied(act, (l, "gc"))
                act.activation(gcol[:, 1], gcol[:, 1], ACT.Exp, scale=-1.0).then_inc(s["en_d"], 1)
                for h in range(HEADS):
                    for c in range(NC):
                        i = NC * h + c
                        n = SEQ - c * P
                        if c < NC - 1:
                            act.wait_ge(s["md"], 3 * (HEADS * l + h) + c + 1)
                        else:
                            copied(act, (l, "mb", h))
                        if i >= 2:
                            act.wait_ge(s["w_ready"], NC * HEADS * l + i - 1)
                        act.activation(E[:, c % 2, 0:n], D[:, c % 2, 0:n], ACT.Exp, scale=-1.0).then_inc(s["me"], 1)
                ready(act, (l, "mo", HEADS - 1))
                hq = hqf[:, 0:2, :]
                act.activation(hq, hq, ACT.Silu).then_inc(s["hsig"], 1)
                act.activation(Xe[:, :, :], hqf[:, 2:4, :], ACT.Sigmoid).then_inc(s["hsig"], 1)
                act.activation(kk[:, :, :], hqf[:, 2:4, :], ACT.Sigmoid, scale=-1.0).then_inc(s["hsig"], 1)
                act.wait_ge(s["lb_a"], l + 1)
                act.activation(lbx[:, :, :], lbx[:, :, :], ACT.Exp).then_inc(s["lb_b"], 1)
                act.wait_ge(s["hF"], l + 1)
                act.activation(qt[:, :, :], qt[:, :, :], ACT.Ln).then_inc(s["hln"], 1)
                act.activation(Xe[:, :, :], Xe[:, :, :], ACT.Ln).then_inc(s["hln"], 1)
                for lev in range(LEVELS + 1):
                    act.wait_ge(s["hx"], (LEVELS + 1) * l + lev + 1)
                    act.activation(Xe[:, :, :], Xe[:, :, :], ACT.Exp).then_inc(s["he"], 1)
                ready(act, (l, "ha", LEVELS, HEADS - 1))
                act.activation(qt[:, :, :], b[:, :, :], ACT.Exp).then_inc(s["he"], 1)
                for hp in range(2):
                    t = ready(act, (l, "hn", hp))
                    release(act.activation(kn[:, hp, :, :], t[:, :].rearrange("p (c n) -> p c n", c=NC), ACT.Copy),
                            (l, "hn", hp))
                act.wait_ge(s["ysq"], l + 1)
                act.activation(QKT[:, :, :].rearrange("p a b -> p (a b)"), tok[:, :, :].rearrange("p a b -> p (a b)"),
                               ACT.Square).then_inc(s["sq"], 1)
                root(l, 3, ms[:, 0:64])
                evens(l, "yt", None)
                copied(act, (l, "wo", NC - 1, 1))
                squares(l, h2n)
                root(l, 4, ms[:, 0:NC])
                evens(l, "h2", C_NF)
                for i in range(2):
                    act.wait_ge(s["rt_x"], 2 * l + i + 1)
                    a = rx[i]
                    act.activation(a, a, ACT.Exp).then_inc(s["rt_e"], 1)
                base = at[(l, "moe")]
                per = MOE_TILES // 8
                with act.Fori(0, MOE_TURNS) as turn:
                    for u in range(MOE_UNROLL):
                        for fh in range(2):
                            n = base + 12 * u + 2 * fh
                            p = n + 1 - 12
                            act.wait_ge(free[p % 8], turn * per + p // 8 + 1)
                            act.wait_ge(full[n % 8], turn * per + n // 8 + 1)
                            act.activation(sil[:, fh, :], psum[n % 8][:, :], ACT.Silu).then_inc(free[n % 8], 1)

        @block.vector
        def _(dve):
            sv = Steps(dve, s["dve_own"])
            then = sv.then

            def inv_root(l, u, a):
                dve.wait_ge(s["root"], ROOTS * l + u + 1)
                then(dve.reciprocal(rs[:a.shape[0], 0:a.shape[1]], a))

            def normalise(l, u, dst, sig):
                dve.wait_ge(s["ss"], NC * (2 * l + (u == 4) + 1))
                dve.tensor_scalar(ms[:, 0:NC], ms[:, 0:NC], 1.0 / DIM, EPS, ALU.mult, ALU.add).then_inc(s["mean"], 1)
                inv_root(l, u, ms[:, 0:NC])
                for c in range(NC):
                    ins = dve.tensor_scalar(dst[:, c, :], X[:, c, :], rs[:, c:c + 1], None, ALU.mult)
                ins.then_inc(sig, 1)

            def odds(l, name, col):
                for k in range(1, KD, 2):
                    t = ready(dve, (l, name, k))
                    if col is None:
                        ins = dve.tensor_copy(hT[:, k, :] if name != "qk" else QKT[:, k, :], t[:, :])
                    else:
                        ins = dve.tensor_scalar(hT[:, k, :], t[:, :], C[:, col + k:col + k + 1], None, ALU.mult)
                    release(ins, (l, name, k))

            def mul(o, a, c):
                return dve.tensor_tensor(o, a, c, ALU.mult)

            def qk_norm(l):
                projected(dve, l, (0, 1, 2), True)
                for a, n, o in ((AQ, 512, 0), (DQ, GW, 512), (KS, HD, 768), (KW, HD, 896)):
                    last = mul(tok[:, :, o:o + n], Pn[:, :, a:a + n], Pn[:, :, a:a + n])
                then(last)
                for o, n, w, a in ((0, 512, HALF, 0), (512, GW, HD, 64), (768, HD, HD, 80), (896, HD, HD, 84)):
                    g = n // w
                    last = dve.tensor_reduce(ms[:, a:a + NC * g].rearrange("p (c g) -> p c g", c=NC),
                                             tok[:, :, o:o + n].rearrange("p c (g w) -> p c g w", w=w),
                                             AX.X, ALU.add)
                then(last)
                then(dve.tensor_scalar(ms[:, 0:64], ms[:, 0:64], 1.0 / HALF, EPS, ALU.mult, ALU.add))
                dve.tensor_scalar(ms[:, 64:88], ms[:, 64:88], 1.0 / HD, EPS, ALU.mult, ALU.add).then_inc(s["mean"], 1)
                inv_root(l, 1, ms[:, 0:88])
                rq = rs[:, 0:64].rearrange("p (c g) -> p c g", c=NC)[:, :, 0:8]
                then(dve.tensor_scalar(rq, rq, HALF ** -0.5, None, ALU.mult))
                then(dve.tensor_scalar(rs[:, 64:80], rs[:, 64:80], HD ** -0.5, None, ALU.mult))
                for a, n, w, o, r, g0 in ((AQ, 512, HALF, 0, 0, None), (DQ, GW, HD, 512, 64, None)):
                    g = n // w
                    last = mul(tok[:, :, o:o + n].rearrange("p c (g w) -> p c g w", w=w),
                               Pn[:, :, a:a + n].rearrange("p c (g w) -> p c g w", w=w),
                               rs[:, r:r + NC * g].rearrange("p (c g o) -> p c g o", c=NC, o=1)
                               .to_broadcast([P, NC, g, w]))
                for a, o, r in ((KS, 768, 80), (KW, 896, 84)):
                    for i in range(2):
                        last = mul(tok[:, :, o + HD * i:o + HD * (i + 1)], Pn[:, :, a:a + HD],
                                   rs[:, r:r + NC].rearrange("p (c o) -> p c o", o=1).to_broadcast([P, NC, HD]))
                then(last)
                for o, n, w, r in ((0, GW, HALF, R_DQ), (GW, GW, HALF, R_DK), (512, GW, HD, R_NQ),
                                   (768, P, HD, R_NK + HD), (896, P, HD, R_NK + 2 * HD)):
                    v = tok[:, :, o:o + n].rearrange("p c (g w) -> p c g w", w=w)
                    last = mul(v, v, R[:, r:r + w].rearrange("p (a b w) -> p a b w", a=1, b=1)
                               .to_broadcast([P, NC, n // w, w]))
                last.then_inc(s["qkn_ready"], 1)

            def differential_lambda(l):
                v = R[:, R_LAM:R_LAM + 4 * HALF].rearrange("p (a b w) -> p a b w", a=2, b=2)
                then(mul(tmp[:, 0:2 * HALF].rearrange("p (a w) -> p a w", a=2), v[:, :, 0, :], v[:, :, 1, :]))
                dve.tensor_reduce(lam4, tmp[:, 0:2 * HALF].rearrange("p (a w) -> p a w", a=2), AX.X, ALU.add) \
                    .then_inc(s["lam_d"], 1)
                dve.wait_ge(s["lam_e"], l + 1)
                then(dve.tensor_tensor(lam, lam4[:, 1:2], lam4[:, 0:1], ALU.subtract))
                then(dve.tensor_scalar(lam, lam, -(0.8 - 0.6 * math.exp(-0.3 * l)), None, ALU.add))

            def compress(l):
                t = ready(dve, (l, "cc", 0))
                release(dve.tensor_copy(Kc[0:NCMP, 0, :], t[0:NCMP, 0:HD]), (l, "cc", 0))
                t = ready(dve, (l, "cc", 1))
                release(dve.tensor_copy(Vc[0:NCMP, :], t[0:NCMP, 0:HD]), (l, "cc", 1))
                copied(dve, (l, "cc", 0))
                then(mul(tmp[0:NCMP, 0:HD], Kc[0:NCMP, 0, :], Kc[0:NCMP, 0, :]))
                then(dve.tensor_reduce(ms[0:NCMP, 0:1], tmp[0:NCMP, 0:HD], AX.X, ALU.add))
                dve.tensor_scalar(ms[0:NCMP, 0:1], ms[0:NCMP, 0:1], 1.0 / HD, EPS, ALU.mult, ALU.add) \
                    .then_inc(s["mean"], 1)
                inv_root(l, 2, ms[0:NCMP, 0:1])
                for i in (1, 0):
                    last = dve.scalar_tensor_tensor(Kc[0:NCMP, i, :], Kc[0:NCMP, 0, :], rs[0:NCMP, 0:1],
                                                    R[0:NCMP, R_NK:R_NK + HD], ALU.mult, ALU.mult)
                last.then_inc(s["ck_n"], 1)
                t = ready(dve, (l, "ck"))
                release(dve.tensor_copy(KcT[:, :], t[:, 0:NCMP]), (l, "ck"))
                bc = K[:, K_CMPB:K_CMPB + 16 * NCMP].rearrange("p (a n) -> p a n", n=NCMP)
                for o in range(2):
                    t = ready(dve, (l, "cs", o))
                    release(dve.tensor_tensor(Sc[:, o::2, :], t[:, 0:8 * NCMP].rearrange("p (a n) -> p a n", n=NCMP),
                                              bc[:, o::2, :], ALU.add), (l, "cs", o))
                for o in range(2):
                    copied(dve, (l, "cs", o))
                then(dve.tensor_reduce(cmx[:, :], Sc[:, :, :], AX.X, ALU.max))
                dve.tensor_tensor(Sc[:, :, :], Sc[:, :, :],
                                  cmx.rearrange("p (a o) -> p a o", o=1).to_broadcast([P, 16, NCMP]),
                                  ALU.subtract).then_inc(s["cs_x"], 1)
                dve.wait_ge(s["cs_e"], l + 1)
                dve.wait_ge(s["gsig"], 3 * (l + 1))
                then(dve.tensor_reduce(cfac[:, :], Sc[:, :, :], AX.X, ALU.add))
                then(dve.reciprocal(cfac[:, :], cfac[:, :]))
                f = cfac.rearrange("p (c h) -> p c h", c=NC)
                then(mul(f, f, Pn[:, :, DG:DG + 12:3]))
                S4 = Sc[:, :, :].rearrange("p (c h) n -> p c h n", c=NC)
                V4 = K[:, K_CMPV:K_CMPV + NC * NCMP].rearrange("p (c o n) -> p c o n", c=NC, o=1)
                then(mul(S4, S4, V4.to_broadcast([P, NC, HEADS, NCMP])))
                mul(Sc[:, :, :], Sc[:, :, :], cfac.rearrange("p (a o) -> p a o", o=1).to_broadcast([P, 16, NCMP])) \
                    .then_inc(s["cs_p"], 1)
                for c in range(NC):
                    t = ready(dve, (l, "cp", c))
                    release(dve.tensor_copy(PcT[0:NCMP, HEADS * c:HEADS * (c + 1), :],
                                            t[0:NCMP, :].rearrange("p (h q) -> p h q", h=HEADS)), (l, "cp", c))
                for c in range(NC):
                    t = ready(dve, (l, "co", c))
                    release(dve.tensor_copy(tok[:, c, 768:1024], t[:, 0:GW]), (l, "co", c))

            def attend(l):
                dve.wait_ge(s["bias_in"], 16 * (l + 1))
                for i in range(len(ITERS) + 2):
                    if i < len(ITERS):
                        m, c = ITERS[i]
                        n = (c + 1) * P
                        t = ready(dve, (l, "S", i))
                        if i >= 2:
                            dve.wait_ge(s["exp_done"], len(ITERS) * l + i - 1)
                        release(dve.tensor_tensor_reduce(
                            out=negS[:, i % 2, 0:n], in0=t[:, 0:n], in1=bias[:, MAPS[m][5], SEQ - n:SEQ],
                            scale=-1.0, scalar=3e38, op0=ALU.add, op1=ALU.min, accum_out=nmax[:, i:i + 1]),
                            (l, "S", i))
                    if i < 2:
                        continue
                    i -= 2
                    m, c = ITERS[i]
                    t = ready(dve, (l, "O", i))
                    dst = tok[:, c, MAPS[m][6] * HD:MAPS[m][6] * HD + HD]
                    f = fac[:, i:i + 1]
                    then(dve.reciprocal(f, psumcol[:, i:i + 1]))
                    if m < 8 and m % 2 == 0:
                        release(dve.tensor_scalar(dst, t[:, 0:HD], f, None, ALU.mult), (l, "O", i))
                        continue
                    if m < 8:
                        coef = lam
                    else:
                        g = DG + 3 * (MAPS[m][6] - 12) + 1 + m % 2
                        coef = Pn[:, c, g:g + 1]
                    then(mul(f, f, coef))
                    copied(dve, (l, "co", c) if m >= 8 and m % 2 == 0 else (l, "O", i - NC))
                    release(dve.scalar_tensor_tensor(dst, t[:, 0:HD], f, dst, ALU.mult, ALU.add), (l, "O", i))

            def mlstm(l):
                then(dve.memset(mraw[:, :, 0:3], 0.0))
                projected(dve, l, (4,), True)
                for j in range(4):
                    for i in range(4):
                        w = C[:, C_CONV + 4 * i + j:C_CONV + 4 * i + j + 1]
                        src = mraw[:, i, j:j + SEQ]
                        if j == 0:
                            last = dve.tensor_scalar(mqk[:, i, :], src, w, None, ALU.mult)
                        else:
                            last = dve.scalar_tensor_tensor(mqk[:, i, :], src, w, mqk[:, i, :], ALU.mult, ALU.add)
                    if j < 3:
                        then(last)
                last.then_inc(s["conv_m"], 1)
                t = ready(dve, (l, "gi"))
                release(dve.tensor_scalar(gA[:, :], t[0:HEADS, :], C[0:HEADS, C_GB:C_GB + 1], None, ALU.add),
                        (l, "gi"))
                t = ready(dve, (l, "gf"))
                release(dve.tensor_scalar(gM[:, :], t[0:HEADS, :], C[0:HEADS, C_GB + 1:C_GB + 2], None, ALU.add),
                        (l, "gf"))
                copied(dve, (l, "gf"))
                dve.scalar_tensor_tensor(gMt[:, :], gM[:, :], -1.0, gM[:, :], ALU.mult, ALU.min).then_inc(s["gate_a"], 1)
                dve.wait_ge(s["gate_b"], l + 1)
                then(dve.scalar_tensor_tensor(gM[:, :], gM[:, :], 0.0, gMt[:, :], ALU.min, ALU.subtract))
                then(dve.tensor_tensor_scan(gMt[:, :], K[0:HEADS, K_IOTA + PER_GROUP - 1:K_IOTA + PER_GROUP].to_broadcast([HEADS, SEQ]), gM[:, :], 0.0,
                                            ALU.mult, ALU.add))
                then(dve.tensor_tensor(gA[:, :], gA[:, :], gMt[:, :], ALU.subtract))
                then(dve.tensor_tensor_scan(gM[:, :], gA[:, :], gA[:, :], 0.0, ALU.max, ALU.max))
                dve.tensor_tensor(gMt[:, :], gMt[:, :], gM[:, :], ALU.add).then_inc(s["gate_r"], 1)
                t = ready(dve, (l, "gc"))
                release(dve.tensor_copy(gcol[:, :, :, :].rearrange("p a c h -> p (a c h)"), t[:, 0:32]), (l, "gc"))
                projected(dve, l, (6,), True)
                dve.memset(Vm[:, :, :, HD:HD + 1], 1.0)
                dve.tensor_copy(Vm[:, :, :, 0:HD], Pn[:, :, BV:BV + GW].rearrange("p c (h w) -> p c h w", h=HEADS)) \
                    .then_inc(s["vm_ready"], 1)
                copied(dve, (l, "gc"))
                dve.wait_ge(s["en_d"], l + 1)
                for h in range(HEADS):
                    mb = ready(dve, (l, "mb", h))

                    def weights(c):
                        n = SEQ - c * P
                        i = NC * h + c
                        dve.wait_ge(s["me"], NC * HEADS * l + i + 1)
                        t = ready(dve, (l, "ms", h, c))
                        w = WT[:, h % 2, WOFF[c]:WOFF[c] + n]
                        release(dve.scalar_tensor_tensor(w, t[:, 0:n], HD ** -0.5, E[:, c % 2, 0:n],
                                                         ALU.mult, ALU.mult), (l, "ms", h, c))
                        copied(dve, (l, "ms", h, c))
                        mul(w[:, 0:P], w[:, 0:P], caus).then_inc(s["w_ready"], 1)

                    for c in range(NC):
                        n = SEQ - c * P
                        i = NC * h + c
                        if i >= 2:
                            dve.wait_ge(s["me"], NC * HEADS * l + i - 1)
                        ins = dve.tensor_scalar(D[:, c % 2, 0:n], mb[:, c * P:SEQ], gcol[:, 0, c, h:h + 1], 0.0,
                                                ALU.subtract, ALU.max)
                        if c < NC - 1:
                            ins.then_inc(s["md"], 1)
                        else:
                            release(ins, (l, "mb", h))
                        if c:
                            weights(c - 1)
                    weights(NC - 1)
                    t = ready(dve, (l, "mo", h))
                    t = t[:, 0:NC * 65].rearrange("p (c w) -> p c w", c=NC)
                    den = t[:, :, HD]
                    md = mden[:, :]
                    then(dve.tensor_copy(md, den))
                    then(dve.scalar_tensor_tensor(md, md, -1.0, md, ALU.mult, ALU.max))
                    then(dve.tensor_tensor(md, md, gcol[:, 1, :, h], ALU.max))
                    then(dve.reciprocal(md, md))
                    release(mul(tok[:, :, GW + h * HD:GW + (h + 1) * HD], t[:, :, 0:HD],
                                md.rearrange("p (c o) -> p c o", o=1).to_broadcast([P, NC, HD])), (l, "mo", h))

            def hgrn(l):
                x = C[:, C_LB:C_LB + 4].rearrange("p (l t) -> p l t", l=2)
                m = lbc[:, 0, :]
                then(dve.tensor_tensor(m, x[:, 0, :], x[:, 1, :], ALU.max))
                dve.tensor_tensor(lbx[:, :, :], x, m.rearrange("p (o t) -> p o t", o=1).to_broadcast([P, 2, 2]),
                                  ALU.subtract).then_inc(s["lb_a"], 1)
                dve.wait_ge(s["lb_b"], l + 1)
                then(dve.tensor_tensor(m, lbx[:, 0, :], lbx[:, 1, :], ALU.add))
                then(dve.reciprocal(m, m))
                then(mul(lbs[:, :, :], lbx[:, :, :], m.rearrange("p (o t) -> p o t", o=1).to_broadcast([P, 2, 2])))
                lb, lf, om, df = (lbc[:, i, :] for i in range(4))
                if l == 0:
                    then(dve.tensor_copy(lb, lbs[:, 0, :]))
                else:
                    then(dve.tensor_tensor(lb, lbs[:, 0, :], lbs[:, 1, :], ALU.add))
                then(dve.tensor_tensor(lb, lb, lbs[:, 0, :], ALU.subtract))
                then(dve.tensor_scalar(lf, lb, 1e-30, None, ALU.max))
                then(dve.tensor_scalar(om, lb, -1.0, 1.0, ALU.mult, ALU.add))
                then(dve.tensor_tensor(df, lf, lb, ALU.subtract))
                dve.wait_ge(s["hsig"], 3 * (l + 1))
                for i in range(2):
                    dve.tensor_scalar(Xe[:, i, :], Xe[:, i, :], om[:, i:i + 1], lf[:, i:i + 1], ALU.mult, ALU.add)
                    last = dve.tensor_scalar(kk[:, i, :], kk[:, i, :], om[:, i:i + 1], df[:, i:i + 1],
                                             ALU.mult, ALU.subtract)
                then(last)
                dve.tensor_scalar(qt[:, :, :], Xe[:, :, :], 1.0 / LN_SPLIT, None, ALU.max)
                then(dve.memset(A[:, :, :], 0.0))
                dve.tensor_scalar(Xe[:, :, :], Xe[:, :, :], LN_SPLIT, 1.0, ALU.mult, ALU.min).then_inc(s["hF"], 1)
                dve.wait_ge(s["hF"], l + 1)
                dve.memset(nopcell, 0.0).then_inc(s["hqk"], 1)
                dve.wait_ge(s["hln"], 2 * (l + 1))
                then(dve.tensor_tensor(qt[:, :, :], qt[:, :, :], Xe[:, :, :], ALU.add))
                for i in range(2):
                    last = dve.tensor_tensor_scan(b[:, i, :], K[:, K_SEG:K_SEG + SEQ], qt[:, i, :], 0.0,
                                                  ALU.mult, ALU.add)
                then(last)

                def products(lev):
                    mask = K[:, K_LVL + lev * P:K_LVL + (lev + 1) * P].bitcast(I32) \
                        .rearrange("p (o t) -> p o t", o=1).to_broadcast([P, NC, P])
                    for h in range(HEADS):
                        t = ready(dve, (l, "ha", lev, h))
                        release(dve.copy_predicated(A[:, h, :].rearrange("p (c t) -> p c t", c=NC), mask,
                                                    t[:, :].rearrange("p (c t) -> p c t", c=NC)), (l, "ha", lev, h))

                flat = lambda v: v[:, :, :].rearrange("p a n -> p (a n)")
                for lev in range(1, LEVELS + 2):
                    if lev <= LEVELS:
                        w = HB >> (lev - 1)
                        bv, xv = (flat(v).rearrange("p (n w) -> p n w", w=w) for v in (b, Xe))
                        seam = bv[:, :, w // 2 - 1:w // 2].to_broadcast([P, 2 * SEQ // w, w // 2])
                        dve.tensor_tensor(xv[:, :, w // 2:], bv[:, :, w // 2:], seam, ALU.subtract)
                        dve.tensor_tensor(xv[:, :, 0:w // 2], seam, bv[:, :, 0:w // 2], ALU.subtract) \
                            .then_inc(s["hx"], 1)
                    else:
                        bv, xv = (flat(v).rearrange("p (n w) -> p n w", w=HB) for v in (b, Xe))
                        dve.tensor_tensor(xv, bv[:, :, HB - 1:HB].to_broadcast([P, 2 * NB, HB]), bv, ALU.subtract) \
                            .then_inc(s["hx"], 1)
                    products(lev - 1)
                    dve.wait_ge(s["he"], (LEVELS + 2) * l + lev)
                    if lev <= LEVELS:
                        mul(qt[:, :, :], hqf[:, 0:2, :], Xe[:, :, :])
                    mul(kt[:, :, :], kk[:, :, :], Xe[:, :, :]).then_inc(s["hqk"], 1)
                    dve.wait_ge(s["hqk"], (LEVELS + 2) * l + lev + 1)
                dve.wait_ge(s["he"], (LEVELS + 2) * (l + 1))
                then(dve.tensor_copy(dec[:, :, :], qt[:, :, HB - 1:SEQ:HB]))
                mul(qt[:, :, :], hqf[:, 0:2, :], qt[:, :, :]).then_inc(s["hq_in"], 1)
                for i in range(NB - 1):
                    c, j = i // 4, i % 4
                    for hp in range(2):
                        t = ready(dve, (l, "hu", hp, j))
                        u = t[:, c * P:(c + 1) * P]
                        if i == 0:
                            ins = dve.tensor_copy(St[:, hp, 1, :], u)
                        else:
                            ins = dve.scalar_tensor_tensor(St[:, hp, i + 1, :], St[:, hp, i, :],
                                                           dec[:, hp, i:i + 1], u, ALU.mult, ALU.add)
                        if c == (2 if j == 3 else 3):
                            release(ins, (l, "hu", hp, j))
                            if hp:
                                copied(dve, (l, "hu", 1, j))
                        elif hp:
                            then(ins)
                dve.memset(St[:, :, 0, :], 0.0).then_inc(s["hst"], 1)
                for c in range(NC):
                    for o in range(2):
                        t = ready(dve, (l, "ho", c, o))
                        v = tok[:, c, 512:768].rearrange("p (a o n) -> p o a n", a=2, o=2)
                        release(dve.tensor_copy(v[:, o], t[:, 0:P].rearrange("p (a n) -> p a n", a=2)),
                                (l, "ho", c, o))

            def output_norms(l):
                copied(dve, (l, "ho", NC - 1, 1))
                copied(dve, (l, "O", len(ITERS) - 1))
                dve.memset(nopcell, 0.0).then_inc(s["ysq"], 1)
                dve.wait_ge(s["sq"], l + 1)
                then(dve.tensor_reduce(ms[:, 0:64], QKT[:, :, :].rearrange("p a (g w) -> p (a g) w", w=HD), AX.X, ALU.add))
                dve.tensor_scalar(ms[:, 0:64], ms[:, 0:64], 1.0 / HD, EPS, ALU.mult, ALU.add).then_inc(s["mean"], 1)
                inv_root(l, 3, ms[:, 0:64])
                ra = rs[:, 0:64].rearrange("p (c h) -> p c h", c=NC)[:, :, 0:HEADS]
                then(dve.tensor_scalar(ra, ra, 1.0 - (0.8 - 0.6 * math.exp(-0.3 * l)), None, ALU.mult))
                tv = tok[:, :, :].rearrange("p c (h w) -> p (c h) w", w=HD)
                then(mul(tv, tv, rs[:, 0:64].rearrange("p (g o) -> p g o", o=1).to_broadcast([P, 64, HD])))
                then(mul(tok[:, :, :], tok[:, :, :], R[:, R_OG:R_OG + DIM].rearrange("p (o n) -> p o n", o=1)
                         .to_broadcast([P, NC, DIM])))
                mul(tok[:, :, GW:2 * GW], tok[:, :, GW:2 * GW], Pn[:, :, BO:BO + GW])
                mul(tok[:, :, 2 * GW:3 * GW], tok[:, :, 2 * GW:3 * GW], Pn[:, :, CG:CG + GW]).then_inc(s["y_ready"], 1)

            def route(l):
                t = ready(dve, (l, "rt"))
                release(dve.tensor_tensor(rt[:, :, :], t[:, 0:36 * NC].rearrange("p (c n) -> p c n", c=NC),
                                          R[:, R_BG:R_BG + 36].rearrange("p (o n) -> p o n", o=1)
                                          .to_broadcast([P, NC, 36]), ALU.add), (l, "rt"))
                copied(dve, (l, "rt"))
                desc = K[:, K_IOTA:K_IOTA + PER_GROUP].rearrange("p (o n) -> p o n", o=1)

                def col(v, n):
                    return v.rearrange("p (c o) -> p c o", o=1).to_broadcast([P, NC, n])

                def first_best(v, n, best, hot):
                    then(dve.tensor_reduce(best, v, AX.X, ALU.max))
                    then(dve.tensor_tensor(hot, v, col(best, n), ALU.is_equal))
                    then(mul(hot, hot, desc[:, :, PER_GROUP - n:].to_broadcast([P, NC, n])))
                    then(dve.tensor_reduce(rmark, hot, AX.X, ALU.max))
                    then(dve.tensor_tensor(hot, hot, col(rmark, n), ALU.is_equal))

                first_best(rt[:, :, 0:GROUPS], GROUPS, rbest, ghot)
                dve.tensor_tensor(rx[0], rt[:, :, 0:GROUPS], col(rbest, GROUPS), ALU.subtract).then_inc(s["rt_x"], 1)
                dve.wait_ge(s["rt_e"], 2 * l + 1)
                then(dve.tensor_reduce(gprob, rx[0], AX.X, ALU.add))
                then(dve.reciprocal(gprob, gprob))
                gh4 = ghot.rearrange("p c (g o) -> p c g o", o=1).to_broadcast([P, NC, GROUPS, PER_GROUP])
                then(mul(gate[:, :, :, :], rt[:, :, GROUPS:].rearrange("p c (g e) -> p c g e", g=GROUPS), gh4))
                then(dve.tensor_reduce(l8, gate[:, :, :, :].rearrange("p c g e -> p c e g"), AX.X, ALU.add))
                first_best(l8, PER_GROUP, rbest, hot1)
                then(dve.scalar_tensor_tensor(l8, hot1, -3e38, l8, ALU.mult, ALU.add))
                first_best(l8, PER_GROUP, rsecond, hot2)
                dve.tensor_tensor(rx[1], rsecond, rbest, ALU.subtract).then_inc(s["rt_x"], 1)
                dve.wait_ge(s["rt_e"], 2 * l + 2)
                then(dve.tensor_scalar(rbest, rx[1], 1.0, None, ALU.add))
                then(dve.reciprocal(rbest, rbest))
                then(mul(gprob, gprob, rbest))
                then(mul(rx[1], rx[1], gprob))
                then(mul(hot1, hot1, col(gprob, PER_GROUP)))
                then(mul(hot2, hot2, col(rx[1], PER_GROUP)))
                then(dve.tensor_tensor(hot1, hot1, hot2, ALU.add))
                h4 = hot1.rearrange("p c (o e) -> p c o e", o=1).to_broadcast([P, NC, GROUPS, PER_GROUP])
                then(mul(gate[:, :, :, :], h4, gh4))

            def experts(l):
                base = at[(l, "moe")]
                per = MOE_TILES // 8
                G = gate[:, :, :, :].rearrange("p c g e -> p c (g e)")
                with dve.Fori(0, MOE_TURNS) as turn:
                    for u in range(MOE_UNROLL):
                        for fh in range(2):
                            n = base + 12 * u + 2 * fh
                            dve.wait_ge(free[n % 8], turn * per + n // 8 + 1)
                            dve.wait_ge(full[(n + 1) % 8], turn * per + (n + 1) // 8 + 1)
                            mul(actT[:, u, fh, :], sil[:, fh, :], psum[(n + 1) % 8][:, :]) \
                                .then_inc(free[(n + 1) % 8], 1)
                        for j in range(8):
                            n = base + 12 * u + 4 + j
                            c, dh = j // 2, j % 2
                            dve.wait_ge(full[n % 8], turn * per + n // 8 + 1)
                            x = X[:, c, 512 * dh:512 * dh + 512]
                            dve.scalar_tensor_tensor(x, psum[n % 8][:, :],
                                                     G[:, c, bass.ds(turn * MOE_UNROLL + u, 1)], x,
                                                     ALU.mult, ALU.add).then_inc(free[n % 8], 1)

            dve.wait_ge(s["const_in"], 16)
            for l in range(LAYERS):
                x_ready(dve, l)
                normalise(l, 0, tok, s["h_ready"])
                dve.wait_ge(s["par_in"], 32 * (l + 1))
                odds(l, "ht", C_NM)
                for g, kind, a, n, what, c, vector in PTILES:
                    if not vector:
                        continue
                    key = ptile(l, g, kind, what, c)
                    t = ready(dve, key)
                    if kind == "n":
                        ins = dve.tensor_copy(Pn[:, c, what:what + n], t[:, 0:n])
                    elif what == "kv":
                        for j in range(2):
                            src = t[HD * j:HD * (j + 1), :]
                            dve.tensor_copy(kcT[0:HD, j, :], src)
                            ins = dve.tensor_copy(kcT[HD:P, j, 0:SEQ - 1], src[:, 1:])
                    elif what[0] == "m":
                        ins = dve.tensor_copy(mraw[:, int(what[1]), 3:], t[:, :])
                    else:
                        ins = dve.tensor_copy(hqf[:, int(what[1]), :], t[:, :])
                    release(ins, key)
                differential_lambda(l)
                qk_norm(l)
                odds(l, "qk", None)
                compress(l)
                attend(l)
                mlstm(l)
                hgrn(l)
                output_norms(l)
                odds(l, "yt", None)
                for c in range(NC):
                    for j in range(2):
                        t = ready(dve, (l, "wo", c, j))
                        x = X[:, c, 512 * j:512 * j + 512]
                        release(dve.tensor_tensor(x, x, t[:, :], ALU.add), (l, "wo", c, j))
                normalise(l, 4, h2n, s["h2_ready"])
                odds(l, "h2", C_NF)
                route(l)
                experts(l)


_NAMED = ["x", "w_in", "w_out", "nsa_cmp_w1", "nsa_cmp_w2", "moe_w_group", "moe_w_expert",
          "moe_w_gate", "moe_w_up", "moe_w_down"]


def _constants():
    p = np.arange(P)
    k = np.zeros((P, KW_ALL), np.float32)
    k[:, K_ID:K_ID + P] = np.eye(P)
    k[:, K_LVL:K_LVL + P] = np.eye(P)
    s_, t_ = p[:, None], p[None, :]
    for lev in range(1, LEVELS + 1):
        w = HB >> (lev - 1)
        k[:, K_LVL + lev * P:K_LVL + (lev + 1) * P] = \
            (s_ // w == t_ // w) & (s_ % w < w // 2) & (t_ % w >= w // 2)
    k[:, K_CAUS:K_CAUS + P] = s_ <= t_
    slopes = 2.0 ** (-8.0 * np.arange(1, 2 * HEADS + 1) / (2 * HEADS))
    diff, nsa = slopes[0::2].astype(np.float32), slopes[1::2].astype(np.float32)
    tokens = P * np.arange(NC)[None, :, None] + p[:, None, None]
    dist = tokens - (CMP_STRIDE * np.arange(NCMP) + CMP_LEN - 1)[None, None, :]
    v = dist >= 0
    cb = np.where(v[:, :, None, :], -nsa[None, None, :, None] * dist[:, :, None, :].astype(np.float32),
                  np.float32(NEG))
    k[:, K_CMPB:K_CMPB + 16 * NCMP] = cb.reshape(P, -1)
    k[:, K_CMPV:K_CMPV + NC * NCMP] = v.reshape(P, -1)
    k[:, K_SEG:K_SEG + SEQ] = np.arange(SEQ) % HB != 0
    k[:, K_IOTA:K_IOTA + PER_GROUP] = np.arange(PER_GROUP, 0, -1)
    d = (p[:, None] + (SEQ - P) - np.arange(SEQ)[None, :]).astype(np.float32)
    al = np.stack([np.where(d >= 0, -sl * d, np.float32(NEG)) for sl in np.concatenate([diff, nsa])], 1)
    return k, al.reshape(P, -1).astype(np.float32)


def _layout(v):
    rows = np.concatenate([v[n].reshape(LAYERS, -1) for n in (
        "diff_q_gain", "diff_k_gain", "nsa_q_gain", "nsa_k_gain", "diff_sub_gain", "mlstm_out_gain",
        "hgrn_out_gain", "nsa_out_gain", "moe_b_group", "moe_b_expert", "diff_lambda")], 1)
    cols = np.zeros((LAYERS, P, CW), np.float32)
    for l in range(LAYERS):
        cols[l, :, C_NM:C_NM + KD] = v["norm_mix"][l].reshape(KD, P).T
        cols[l, :, C_NF:C_NF + KD] = v["norm_ffn"][l].reshape(KD, P).T
        cols[l, :, C_CONV:C_CONV + 16] = v["mlstm_conv"][l].reshape(4, 4, P).transpose(2, 1, 0).reshape(P, 16)
        cols[l, :, C_POS:C_POS + 32] = v["nsa_cmp_pos"][l].reshape(2, 16, P).transpose(2, 0, 1).reshape(P, 32)
        cols[l, :, C_LB:C_LB + 4] = v["hgrn_lower_bounds"].reshape(LAYERS, 2, P).transpose(2, 0, 1).reshape(P, 4)
        cols[l, 0:HEADS, C_GB:C_GB + 2] = v["mlstm_gate_bias"][l].T
    return rows, cols


def kernel(**inputs):
    import concourse.bacc as bacc
    from concourse.bass_utils import run_bass_kernel_spmd

    nc = bacc.Bacc("TRN2", target_bir_lowering=False, num_devices=1)
    v = {n: np.ascontiguousarray(a) for n, a in inputs.items()}
    arrays = {n: v[n] for n in _NAMED}
    arrays["x"] = v["x"].reshape(SEQ, DIM)
    for n in ("moe_w_gate", "moe_w_up", "moe_w_down"):
        arrays[n] = v[n].reshape(LAYERS, EXPERTS, *v[n].shape[3:])
    arrays["rows"], arrays["columns"] = _layout(v)
    arrays["constants"], arrays["alibi"] = _constants()
    d = {n: nc.dram_tensor(n, a.shape, mybir.dt.from_np(a.dtype), kind="ExternalInput").ap()
         for n, a in arrays.items()}
    out = nc.dram_tensor("out", (SEQ, DIM), F32, kind="ExternalOutput").ap()
    build(nc, d, out)
    r = run_bass_kernel_spmd(nc, [arrays], core_ids=[0])
    return r.results[0]["out"].reshape(1, SEQ, DIM)
```

```python
import math
from contextlib import ExitStack

import numpy as np
import concourse.bass as bass
from concourse import mybir

F32 = mybir.dt.float32
I32 = mybir.dt.int32
ALU = mybir.AluOpType
ACT = mybir.ActivationFunctionType
AX = mybir.AxisListType

LAYERS, SEQ, DIM = 2, 512, 1024
P = 128
NC = SEQ // P
KD = DIM // P
HEADS, HD = 4, 64
GW = HEADS * HD
HALF = HD // 2
IN_COLS = 3476
EPS = 1e-6
NEG = -1e30
CMP_LEN, CMP_STRIDE = 32, 16
NCMP = (SEQ - CMP_LEN) // CMP_STRIDE + 1
EXPERTS, GROUPS, PER_GROUP, FF = 32, 4, 8, 256
HB = 32
NB = SEQ // HB
LEVELS = 5
LN_SPLIT = 2.0 ** 50

AQ, AK, AV, BV, BI, BF, BO, CI, CG, DQ, KS, VS, KW, VW, DG, PW = (
    0, 256, 512, 768, 1024, 1028, 1032, 1288, 1544, 1800, 2056, 2120, 2184, 2248, 2312, 2324)
W_IN = [(0, 512), (2824, 384), (3208, 268), (512, 256), (768, 512), (1800, 512), (1280, 260), (1540, 260),
        (2312, 512)]
PROJ = [
    [("n", 0, 512, AQ)],
    [("n", 0, 256, DQ), ("t", 256, 128, "kv")],
    [("n", 0, 268, KS)],
    [("n", 0, 256, AV)],
    [("t", 128 * i, 128, f"m{i}") for i in range(4)],
    [("t", 128 * i, 128, f"g{i}") for i in range(4)],
    [("n", 0, 260, BV)],
    [("n", 0, 260, BF)],
    [("n", 0, 512, CI)],
]
LOADS = len(W_IN) + 2

R_DQ, R_DK, R_NQ, R_NK, R_OG, R_BG, R_BE, R_LAM, RW = 0, 32, 64, 128, 320, 1344, 1348, 1380, 1508
C_NM, C_NF, C_CONV, C_POS, C_LB, C_GB, CW = 0, 8, 16, 32, 64, 68, 70
K_ID, K_LVL, K_CAUS, K_CMPB, K_CMPV, K_SEG, K_IOTA = (
    0, 128, 896, 1024, 1520, 1644, 2156)
K_SLOT, K_BLK, K_THR, K_UP, K_FOLD, K_T2, K_T4, K_HALF, K_OOB, KW_ALL = (
    2164, 2292, 2344, 2352, 2480, 2544, 2552, 2560, 2561, 2562)

MAPS = []
for _h in range(HEADS):
    for _c in range(2):
        MAPS.append((_h // 2, 2 + _h // 2, 64 * (_h % 2) + 32 * _c, HALF, AV + HD * _h, _h, _h))
for _h in range(HEADS):
    for _c in range(2):
        MAPS.append((4 + _h // 2, 6 + _c, 64 * (_h % 2), HD, (VS, VW)[_c], HEADS + _h, 12 + _h))
ITERS = [(m, c) for m in range(len(MAPS)) for c in range(NC)]


ST = 1560
SLOTS = 64
BLOCKS = 48
TABW = BLOCKS + 4
OUTSIDE = 8192
PEEL = 4
WOFF = [0, 512, 896, 1152]
ROOTS = 5


def attention_order():
    out = []
    for i in range(len(ITERS) + 2):
        if i < len(ITERS):
            out.append(("S", i))
        if 0 <= i - 1 < len(ITERS):
            out.append(("T", i - 1))
        if 0 <= i - 2:
            out.append(("O", i - 2))
    return out


def psum_plan():
    at, n = {}, 0

    def add(key):
        nonlocal n
        at[key] = n
        n += 1

    for l in range(LAYERS):
        for k in range(KD):
            add((l, "ht", k))
        for g, parts in enumerate(PROJ):
            for kind, _, _, what in parts:
                if kind == "t":
                    add((l, "pt", what))
                else:
                    for c in range(NC):
                        add((l, "pn", g, c))
        for j in range(8):
            add((l, "qk", j))
        for j in range(2):
            add((l, "ch", j))
        for j in range(2):
            add((l, "cc", j))
        add((l, "ck"))
        for o in range(2):
            add((l, "cs", o))
        for c in range(NC):
            add((l, "cp", c))
        for c in range(NC):
            add((l, "co", c))
        for kind, i in attention_order():
            add((l, kind, i))
        add((l, "gi"))
        add((l, "gf"))
        add((l, "gc"))
        for h in range(HEADS):
            add((l, "mb", h))
            for s in range(NC):
                add((l, "ms", h, s))
            add((l, "mo", h))
        for lev in range(LEVELS + 1):
            for h in range(HEADS):
                add((l, "ha", lev, h))
        for hp in range(2):
            add((l, "hn", hp))
        for j in range(P // HB):
            for hp in range(2):
                add((l, "hu", hp, j))
        for c in range(NC):
            for o in range(2):
                add((l, "ho", c, o))
        for k in range(KD):
            add((l, "yt", k))
        for c in range(NC):
            for j in range(2):
                add((l, "wo", c, j))
        for k in range(KD):
            add((l, "h2", k))
        add((l, "rt"))
        add((l, "rk"))
        add((l, "rb"))
    return at


class Steps:

    def __init__(self, eng, own):
        self.eng, self.own, self.n = eng, own, {}

    def count(self, ins, sem):
        ins.then_inc(sem, 1)
        self.n[id(sem)] = self.n.get(id(sem), 0) + 1
        return self.n[id(sem)]

    def then(self, ins, sem=None):
        sem = self.own if sem is None else sem
        self.eng.wait_ge(sem, self.count(ins, sem))


def build(nc, d, out):
    ctx = ExitStack()
    with ctx:
        def sb(name, shape, dt=F32):
            return ctx.enter_context(nc.sbuf_tensor(name, shape, dt))

        def sem(name):
            return ctx.enter_context(nc.semaphore(name))

        X = sb("X", [P, NC, DIM])
        hT = sb("hT", [P, KD, SEQ])
        K = sb("K", [P, KW_ALL])
        R = sb("R", [P, RW])
        C = sb("C", [P, CW])
        M = sb("area", [P, 39008])
        st = sb("stats", [P, ST])

        def area(a, shape):
            n = int(np.prod(shape))
            v = M[:, a:a + n]
            if len(shape) == 2:
                v = v.rearrange("p (a b) -> p a b", a=shape[0])
            if len(shape) == 3:
                v = v.rearrange("p (a b c) -> p a b c", a=shape[0], b=shape[1])
            return v

        tok = area(0, [NC, DIM])
        Pn = area(4096, [NC, PW])
        wring = area(13392, [2, KD, 512])
        bias = area(21584, [8, 512])
        QKT = area(25680, [8, SEQ])
        mraw = area(29776, [4, SEQ + 3])
        mqk = area(31836, [4, SEQ])
        hqf = area(33884, [4, SEQ])
        negS = area(35932, [2, 512])
        prob = area(36956, [2, 512])
        probT = area(37980, [2, 512])
        w1 = area(31836, [2, 16, HD])
        kcT = area(35932, [2, SEQ])
        Sc = area(36956, [16, NCMP])
        w2 = area(37984, [2, HD])
        PcT = area(31836, [16, P])
        gA, gMt, gM = (area(21584 + SEQ * i, [SEQ])[0:HEADS, :] for i in range(3))
        WT = area(25680, [2, 1280])
        D = area(28240, [2, SEQ])
        E = area(35932, [2, SEQ])
        Vm = area(36956, [NC, HEADS, HD + 1])
        b = area(25680, [2, SEQ])
        kk = area(26704, [2, SEQ])
        Xe = area(27728, [2, SEQ])
        qt = area(28752, [2, SEQ])
        kt = area(29776, [2, SEQ])
        kn = area(30800, [2, NC, P])
        A = area(31836, [HEADS, SEQ])
        St = area(21584, [2, 16, P])
        wgu = area(0, [2, KD, 2 * FF])
        wdn = area(8192, [2, 2, DIM])
        h2n = area(13392, [NC, DIM])
        gi = area(21584, [TABW]).bitcast(I32)
        si = area(21636, [TABW]).bitcast(I32)
        ebt = area(21688, [TABW])[0:1, :].bitcast(I32)
        hots = area(21744, [NC, 2 * EXPERTS])
        hots8 = area(21744, [2 * NC, EXPERTS])
        rk = area(22000, [NC + 1, EXPERTS])
        nblk = area(22160, [EXPERTS])
        bend = area(22192, [EXPERTS])
        bst = area(22224, [EXPERTS])
        selsum = area(22256, [NC, EXPERTS])
        oslot = area(22384, [2 * NC, P])
        oblk = area(23408, [2 * NC, 3, TABW])
        tab = area(24656, [3, TABW])
        rtmp = area(25680, [BLOCKS * EXPERTS])
        yc = area(25680, [NC, 2 * DIM])
        wr = area(33872, [KD, 36])
        rt = area(34160, [NC, 36])
        hg = area(34304, [2, 512])
        hgT = area(35328, [2, 4, P])
        au = area(36352, [2, 512])
        ysb = area(37376, [2, 512])
        sil = area(38400, [2, P])
        actT = area(38656, [2, P])

        ident = K[:, K_ID:K_ID + P]
        caus = K[:, K_CAUS:K_CAUS + P]

        index = sb("index", [P, 2, 2], I32)

        psum = [ctx.enter_context(nc.psum_tensor(f"bank{i}", [P, 512], F32)) for i in range(8)]
        at = psum_plan()

        at_st = [0]

        def small(*shape):
            n = int(np.prod(shape))
            v = st[:, at_st[0]:at_st[0] + n]
            at_st[0] += n
            if len(shape) == 2:
                v = v.rearrange("p (a b) -> p a b", a=shape[0])
            if len(shape) == 3:
                v = v.rearrange("p (a b c) -> p a b c", a=shape[0], b=shape[1])
            return v

        Hd, posb, Kc, KcT, Vc = small(2, NCMP), small(2), small(2, HD), small(NCMP), small(HD)
        nmax, psumcol, fac = small(len(ITERS)), small(len(ITERS)), small(len(ITERS))
        ms, rs = small(88), small(88)
        lam4, lam = small(2), small(1)
        cmx, cfac = small(16), small(16)
        gcol = small(2, NC, HEADS)
        mden = small(NC)
        lbx, lbs, lbc = small(2, 2), small(2, 2), small(4, 2)
        dec = small(2, NB)

        nopcell, tmp = small(1), sb("scratch", [P, 2 * HD])
        rbest, rsecond, rmark, gprob, rx1 = (small(NC) for _ in range(5))
        ghot, rx0 = small(NC, GROUPS), small(NC, GROUPS)
        hot1, hot2, l8 = (small(NC, PER_GROUP) for _ in range(3))
        rx = (rx0, rx1)
        gate = small(NC, GROUPS, PER_GROUP)
        rank, blk, quot = (small(2 * NC) for _ in range(3))
        ebf = small(TABW)
        oblk8 = small(2 * NC, EXPERTS)
        assert at_st[0] <= ST

        names = """h2_ready h2_out sel_ready ob_ready route_ready x_new const_in x_in par_in w1_in bias_in wr_in out_done
            act_own dve_own ss mean root h_ready kvs qkn_ready ck_n cs_x cs_e cs_p gsig exp_done
            lam_d lam_e conv_m silu_m gate_a gate_b gate_r en_d vm_ready md me w_ready
            lb_a lb_b hsig hF hln hx he hqk hst hq_in sq ysq y_ready rt_x rt_e""".split()
        s = {n: sem(n) for n in names}
        full = [sem(f"bank_full{i}") for i in range(8)]
        free = [sem(f"bank_free{i}") for i in range(8)]
        yc_in = [sem(f"yc_in{c}") for c in range(NC)]
        w_in_sem = [sem(f"w_in{i}") for i in range(2)]
        moe = [{n: sem(f"{n}_{l}") for n in """tr_full tr_copied au_full au_copied fold_full silu_done act_ready
            y_full y_copied gather0 gather1 scatter0 scatter1 gu_in0 gu_in1 dn_in0 dn_in1 gather_index scatter_index""".split()}
               for l in range(LAYERS)]
        h_rows = nc.dram_tensor("h_rows", (2 * SEQ, 512), F32, kind="Internal").ap()
        y_rows = nc.dram_tensor("y_rows", (4 * SEQ, 512), F32, kind="Internal").ap()

        def take(eng, key):
            n = at[key]
            if n >= 8:
                eng.wait_ge(free[n % 8], n // 8)
            return psum[n % 8]

        def filled(ins, key):
            ins.then_inc(full[at[key] % 8], 1)

        def ready(eng, key):
            n = at[key]
            eng.wait_ge(full[n % 8], n // 8 + 1)
            return psum[n % 8]

        def release(ins, key):
            ins.then_inc(free[at[key] % 8], 1)

        def copied(eng, key):
            n = at[key]
            eng.wait_ge(free[n % 8], n // 8 + 1)

        def x_ready(eng, l):
            if l:
                eng.wait_ge(s["x_new"], l)
            else:
                eng.wait_ge(s["x_in"], 16)

        def pairs(eng, l):
            eng.wait_ge(s["route_ready"], l + 1)
            return eng.value_load(ebt[0:1, BLOCKS:BLOCKS + 1], min_val=7, max_val=BLOCKS // 2 - 1)

        def gathered(e, u):
            return 16 * (e // 2 + 1) if isinstance(e, int) else e * 8 + (16 - 8 * u)

        def blocks(eng, last_pair, step):
            for e in range(PEEL):
                step(e, e % 2)
            with eng.Fori(PEEL // 2, last_pair + 1) as turn:
                for u in range(2):
                    step(turn * 2 + u, u)

        PTILES = []
        for g, parts in enumerate(PROJ):
            for kind, a, n, what in parts:
                for c in range(NC if kind == "n" else 1):
                    PTILES.append((g, kind, a, n, what, c, what == "kv" or len(PTILES) % 2 == 1))

        def ptile(l, g, kind, what, c):
            return (l, "pn", g, c) if kind == "n" else (l, "pt", what)

        LAST_OF = {g: ptile(0, *[(t[0], t[1], t[4], t[5]) for t in PTILES if t[0] == g][-1])[1:]
                   for g in range(len(PROJ))}

        def projected(eng, l, groups, mine):
            for g in groups:
                for t in [t for t in PTILES if t[0] == g][-4:]:
                    copied(eng, ptile(l, g, t[1], t[4], t[5]))

        block = ctx.enter_context(nc.Block())

        @block.sync
        def _(sp):
            sp.dma_start(X[:, :, :], d["x"].rearrange("(c p) n -> p c n", p=P)).then_inc(s["x_in"], 16)
            sp.dma_start(K[:, :], d["constants"]).then_inc(s["const_in"], 16)

            def load_in(l, n):
                j = l * LOADS + n
                if n >= 2:
                    ready(sp, (l,) + LAST_OF[n - 2])
                if n < len(W_IN):
                    a, w = W_IN[n]
                    src = d["w_in"][l, :, a:a + w].rearrange("(k p) n -> p k n", p=P)
                else:
                    w = 512
                    a = 512 * (n - len(W_IN))
                    src = d["w_out"][l, :, a:a + w].rearrange("(k p) n -> p k n", p=P)
                sp.dma_start(wring[:, j % 2, :, 0:w], src).then_inc(w_in_sem[j % 2], 16)

            def load_experts(l):
                m = moe[l]
                last_pair = pairs(sp, l)

                def step(e, u):
                    x = sp.value_load(ebt[0:1, bass.ds(e, 1)], min_val=0, max_val=EXPERTS - 1)
                    if not isinstance(e, int) or e >= 2:
                        sp.wait_ge(m["au_full"], e - 1)
                    for i, name in enumerate(("moe_w_gate", "moe_w_up")):
                        sp.dma_start(wgu[:, u, :, FF * i:FF * (i + 1)],
                                     d[name][l, bass.ds(x, 1)].rearrange("e (k p) f -> p (e k) f", p=P)) \
                            .then_inc(m[f"gu_in{u}"], 16)
                    if not isinstance(e, int) or e >= 2:
                        sp.wait_ge(m["y_full"], e - 1)
                    sp.dma_start(wdn[:, u, :, :],
                                 d["moe_w_down"][l, bass.ds(x, 1)].rearrange("e (k p) f -> p (e k) f", p=P)) \
                        .then_inc(m[f"dn_in{u}"], 16)

                blocks(sp, last_pair, step)
                if l + 1 < LAYERS:
                    for i in range(2):
                        load_in(l + 1, i)
                for u in range(2):
                    sp.wait_ge(m[f"scatter{u}"], last_pair * 16 + 16)
                sp.wait_ge(m["scatter_index"], last_pair * 2 + 3)
                for c in range(NC):
                    sp.dma_start(yc[:, c, :], y_rows[4 * P * c:4 * P * (c + 1), :]
                                 .rearrange("(p j) n -> p (j n)", j=4)).then_inc(yc_in[c], 16)

            for l in range(LAYERS):
                if l:
                    sp.wait_ge(s["x_new"], l)
                sp.dma_start(R[:, :], d["rows"][l:l + 1, :].to_broadcast([P, RW])).then_inc(s["par_in"], 16)
                sp.dma_start(C[:, :], d["columns"][l]).then_inc(s["par_in"], 16)
                for n in range(LOADS):
                    if l == 0 or n >= 2:
                        load_in(l, n)
                    if n == 1:
                        for i in range(2):
                            sp.dma_start(w1[:, i], d["nsa_cmp_w1"][l, i].rearrange("(j p) m -> p j m", p=P)) \
                                .then_inc(s["w1_in"], 16)
                        sp.dma_start(w2[0:HD, :, :], d["nsa_cmp_w2"][l].rearrange("j k m -> k j m")) \
                            .then_inc(s["w1_in"], 16)
                        sp.dma_start(bias[:, :, :], d["alibi"].rearrange("p (n m) -> p n m", n=8)) \
                            .then_inc(s["bias_in"], 16)
                copied(sp, (l, "wo", NC - 1, 1))
                sp.dma_start(wr[:, :, 0:GROUPS], d["moe_w_group"][l].rearrange("(k p) n -> p k n", p=P)) \
                    .then_inc(s["wr_in"], 16)
                sp.dma_start(wr[:, :, GROUPS:], d["moe_w_expert"][l].rearrange("(k p) n -> p k n", p=P)) \
                    .then_inc(s["wr_in"], 16)
                sp.wait_ge(s["h2_ready"], l + 1)
                sp.dma_start(h_rows.rearrange("(c p t) n -> p c (t n)", p=P, t=2), h2n[:, :, :]) \
                    .then_inc(s["h2_out"], 16)
                load_experts(l)
            sp.wait_ge(s["x_new"], LAYERS)
            sp.dma_start(out.rearrange("(c p) n -> p c n", p=P), X[:, :, :]).then_inc(s["out_done"], 16)
            sp.wait_ge(s["out_done"], 16)

        @block.tensor
        def _(pe):
            def to_channels(l, name, src):
                for k in range(KD):
                    t = take(pe, (l, name, k))
                    for c in range(NC):
                        last = pe.transpose(t[:, c * P:(c + 1) * P], src[:, c, k * P:(k + 1) * P], ident)
                    filled(last, (l, name, k))

            def loaded(j):
                pe.wait_ge(w_in_sem[j % 2], 16 * (j // 2 + 1))

            def project(l):
                for g, kind, a, n, what, c, _ in PTILES:
                    j = l * LOADS + g
                    if c == 0 and a == PROJ[g][0][1]:
                        loaded(j)
                    w = wring[:, j % 2]
                    key = ptile(l, g, kind, what, c)
                    t = take(pe, key)
                    for k in range(KD):
                        if kind == "n":
                            last = pe.matmul(t[:, 0:n], hT[:, k, c * P:(c + 1) * P], w[:, k, a:a + n],
                                             start=(k == 0), stop=(k == KD - 1))
                        else:
                            last = pe.matmul(t[:, :], w[:, k, a:a + n], hT[:, k, :],
                                             start=(k == 0), stop=(k == KD - 1))
                    filled(last, key)

            def compress(l):
                pe.wait_ge(s["w1_in"], 48 * (l + 1))
                copied(pe, (l, "pt", "kv"))
                for j in range(2):
                    t = take(pe, (l, "ch", j))
                    for i in range(16):
                        pe.matmul(t[0:HD, 0:NCMP], w1[:, j, i, :],
                                  kcT[:, j, 2 * i:2 * i + CMP_STRIDE * (NCMP - 1) + 1:CMP_STRIDE],
                                  start=(i == 0), stop=(i == 15))
                    for i in range(16):
                        last = pe.matmul(t[0:HD, NCMP:NCMP + 1], w1[:, j, i, :],
                                         C[:, C_POS + 16 * j + i:C_POS + 16 * j + i + 1],
                                         start=(i == 0), stop=(i == 15))
                    filled(last, (l, "ch", j))
                for j in range(2):
                    t = take(pe, (l, "cc", j))
                    copied(pe, (l, "ch", j))
                    filled(pe.matmul(t[0:NCMP, 0:HD], Hd[0:HD, j, :], w2[0:HD, j, :], start=True, stop=True),
                           (l, "cc", j))
                t = take(pe, (l, "ck"))
                pe.wait_ge(s["ck_n"], l + 1)
                filled(pe.transpose(t[:, 0:NCMP], Kc[0:NCMP, :, :].rearrange("p a b -> p (a b)"),
                                    ident[0:NCMP, 0:NCMP]), (l, "ck"))
                copied(pe, (l, "ck"))
                for o in range(2):
                    t = take(pe, (l, "cs", o))
                    for c in range(NC):
                        for i in range(2):
                            n = (2 * c + i) * NCMP
                            last = pe.matmul(t[:, n:n + NCMP], QKT[64 * o:64 * o + HD, 4 + i, c * P:(c + 1) * P],
                                             KcT[64 * o:64 * o + HD, :], start=True, stop=True)
                    filled(last, (l, "cs", o))
                pe.wait_ge(s["cs_p"], l + 1)
                for c in range(NC):
                    t = take(pe, (l, "cp", c))
                    for h in range(HEADS):
                        last = pe.transpose(t[0:NCMP, h * P:(h + 1) * P], Sc[:, c * HEADS + h, :], ident)
                    filled(last, (l, "cp", c))
                copied(pe, (l, "cc", 1))
                for c in range(NC):
                    t = take(pe, (l, "co", c))
                    copied(pe, (l, "cp", c))
                    for h in range(HEADS):
                        last = pe.matmul(t[:, h * HD:(h + 1) * HD], PcT[0:NCMP, c * HEADS + h, :], Vc[0:NCMP, :],
                                         start=True, stop=True)
                    filled(last, (l, "co", c))

            def attend(l):
                for kind, i in attention_order():
                    m, c = ITERS[i]
                    q, k, o, depth, v, _, _ = MAPS[m]
                    n = (c + 1) * P
                    t = take(pe, (l, kind, i))
                    if kind == "S":
                        last = pe.matmul(t[:, 0:n], QKT[o:o + depth, q, c * P:(c + 1) * P],
                                         QKT[o:o + depth, k, 0:n], start=True, stop=True, tile_position=(o, 0))
                    elif kind == "T":
                        pe.wait_ge(s["exp_done"], len(ITERS) * l + i + 1)
                        for j in range(c + 1):
                            last = pe.transpose(t[:, j * P:(j + 1) * P], prob[:, i % 2, j * P:(j + 1) * P], ident)
                    else:
                        copied(pe, (l, "T", i))
                        for j in range(c + 1):
                            last = pe.matmul(t[:, 0:HD], probT[:, i % 2, j * P:(j + 1) * P],
                                             Pn[:, j, v:v + HD], start=(j == 0), stop=(j == c))
                    filled(last, (l, kind, i))

            def mlstm(l):
                for name, a in (("gi", BI), ("gf", BF)):
                    t = take(pe, (l, name))
                    for c in range(NC):
                        last = pe.transpose(t[0:HEADS, c * P:(c + 1) * P], Pn[:, c, a:a + HEADS], ident)
                    filled(last, (l, name))
                t = take(pe, (l, "gc"))
                pe.wait_ge(s["gate_r"], l + 1)
                for n, row in enumerate((gA, gMt)):
                    for c in range(NC):
                        last = pe.transpose(t[:, 16 * n + HEADS * c:16 * n + HEADS * c + HEADS],
                                            row[:, c * P:(c + 1) * P], ident[0:HEADS, 0:HEADS])
                filled(last, (l, "gc"))
                pe.wait_ge(s["silu_m"], l + 1)
                pe.wait_ge(s["vm_ready"], l + 1)
                for h in range(HEADS):
                    o = 64 * (h % 2)
                    t = take(pe, (l, "mb", h))
                    filled(pe.matmul(t[:, :], ident[0:HEADS, h:h + 1].to_broadcast([HEADS, P]), gM[:, :],
                                     start=True, stop=True), (l, "mb", h))
                    for c in range(NC):
                        t = take(pe, (l, "ms", h, c))
                        filled(pe.matmul(t[:, 0:SEQ - c * P], mqk[o:o + HD, 2 + h // 2, c * P:(c + 1) * P],
                                         mqk[o:o + HD, h // 2, c * P:SEQ], start=True, stop=True), (l, "ms", h, c))
                    t = take(pe, (l, "mo", h))
                    pe.wait_ge(s["w_ready"], NC * (HEADS * l + h + 1))
                    for c in range(NC):
                        for j in range(c + 1):
                            a = WOFF[j] + (c - j) * P
                            last = pe.matmul(t[:, c * 65:c * 65 + 65], WT[:, h % 2, a:a + P], Vm[:, j, h, :],
                                             start=(j == 0), stop=(j == c))
                    filled(last, (l, "mo", h))

            def hgrn(l):
                for lev in range(LEVELS + 1):
                    qs, ks = (hqf, kk) if lev == 0 else (qt, kt)
                    pe.wait_ge(s["hqk"], (LEVELS + 2) * l + lev + 1)
                    for h in range(HEADS):
                        o = 64 * (h % 2)
                        t = take(pe, (l, "ha", lev, h))
                        for c in range(NC):
                            last = pe.matmul(t[:, c * P:(c + 1) * P], ks[o:o + HD, h // 2, c * P:(c + 1) * P],
                                             qs[o:o + HD, h // 2, c * P:(c + 1) * P], start=True, stop=True)
                        filled(last, (l, "ha", lev, h))
                pe.wait_ge(s["hqk"], (LEVELS + 2) * (l + 1))
                for hp in range(2):
                    t = take(pe, (l, "hn", hp))
                    for c in range(NC):
                        last = pe.transpose(t[:, c * P:(c + 1) * P], kt[:, hp, c * P:(c + 1) * P], ident)
                    filled(last, (l, "hn", hp))
                for hp in range(2):
                    copied(pe, (l, "hn", hp))
                for j in range(P // HB):
                    r = slice(j * HB, (j + 1) * HB)
                    for hp in range(2):
                        t = take(pe, (l, "hu", hp, j))
                        for c in range(NC):
                            last = pe.matmul(t[:, c * P:(c + 1) * P], kn[r, hp, c, :],
                                             Pn[r, c, CI + hp * P:CI + (hp + 1) * P], start=True, stop=True,
                                             tile_position=(j * HB, 0))
                        filled(last, (l, "hu", hp, j))
                pe.wait_ge(s["hq_in"], l + 1)
                pe.wait_ge(s["hst"], l + 1)
                for c in range(NC):
                    for o in range(2):
                        t = take(pe, (l, "ho", c, o))
                        for hp in range(2):
                            h = 2 * hp + o
                            last = pe.matmul(t[:, hp * HD:(hp + 1) * HD], A[:, h, c * P:(c + 1) * P],
                                             Pn[:, c, CI + h * HD:CI + (h + 1) * HD], start=True, stop=False)
                            for j in range(P // HB):
                                i = c * (P // HB) + j
                                last = pe.matmul(t[j * HB:(j + 1) * HB, hp * HD:(hp + 1) * HD],
                                                 qt[64 * o:64 * o + HD, hp, i * HB:(i + 1) * HB],
                                                 St[64 * o:64 * o + HD, hp, i, 64 * o:64 * o + HD],
                                                 start=False, stop=True, tile_position=(64 * o, j * HB))
                        filled(last, (l, "ho", c, o))

            def route(l):
                t = take(pe, (l, "rk"))
                pe.wait_ge(s["sel_ready"], l + 1)
                one = K[:, K_IOTA + PER_GROUP - 1:K_IOTA + PER_GROUP].to_broadcast([P, P])
                for c in range(NC + 1):
                    before = min(c, NC)
                    for i in range(before):
                        last = pe.matmul(t[:, EXPERTS * c:EXPERTS * (c + 1)], one, selsum[:, i, :],
                                         start=(i == 0), stop=(c == NC and i == NC - 1))
                    if c < NC:
                        last = pe.matmul(t[:, EXPERTS * c:EXPERTS * (c + 1)], K[:, K_UP:K_UP + P], selsum[:, c, :],
                                         start=(c == 0), stop=True)
                filled(last, (l, "rk"))
                t = take(pe, (l, "rb"))
                pe.wait_ge(s["ob_ready"], l + 1)
                for i in range(2 * NC):
                    last = pe.matmul(t[:, 0:3 * TABW], oslot[:, i, :],
                                     oblk[:, i, :, :].rearrange("p a b -> p (a b)"),
                                     start=(i == 0), stop=(i == 2 * NC - 1))
                filled(last, (l, "rb"))

            def experts(l):
                m = moe[l]
                last_pair = pairs(pe, l)
                for i in range(8):
                    last = max(v for v in at.values() if v % 8 == i and v <= at[(l, "rb")])
                    pe.wait_ge(free[i], last // 8 + 1)

                def turn_tokens(e, u):
                    half = e // 2 if isinstance(e, int) else None
                    pe.wait_ge(m[f"gather{u}"], gathered(e, u))
                    if not isinstance(e, int) or e >= 2:
                        pe.wait_ge(m["tr_copied"], e - 1)
                    for k in range(4):
                        last = pe.transpose(psum[u][:, k * P:(k + 1) * P], hg[:, u, k * P:(k + 1) * P], ident)
                    last.then_inc(m["tr_full"], 1)

                def down(e, u):
                    static = isinstance(e, int)
                    pe.wait_ge(m["act_ready"], e + 1)
                    pe.wait_ge(m[f"dn_in{u}"], gathered(e, u))
                    if not static or e >= 2:
                        pe.wait_ge(m["y_copied"], e - 1)
                    for k in range(2):
                        for j in range(2):
                            last = pe.matmul(psum[6 + u][SLOTS * j:SLOTS * (j + 1), :],
                                             actT[:, u, SLOTS * k:SLOTS * (k + 1)],
                                             wdn[:, u, k, 512 * j:512 * (j + 1)], start=(k == 0), stop=(k == 1),
                                             tile_position=(0, SLOTS * j))
                    last.then_inc(m["y_full"], 1)

                def step(e, u):
                    static = isinstance(e, int)
                    pe.wait_ge(m["tr_copied"], e + 1)
                    pe.wait_ge(m[f"gu_in{u}"], gathered(e, u) * 2)
                    if not static or e >= 2:
                        pe.wait_ge(m["au_copied"], e - 1)
                    for k in range(4):
                        for j in range(2):
                            last = pe.matmul(psum[2 + u][SLOTS * j:SLOTS * (j + 1), :],
                                             hgT[:, u, k, SLOTS * j:SLOTS * (j + 1)], wgu[:, u, 4 * j + k, :],
                                             start=(k == 0), stop=(k == 3), tile_position=(0, SLOTS * j))
                    last.then_inc(m["au_full"], 1)
                    turn_tokens(e + 1, 1 - u)
                    if not static or e >= 1:
                        down(e - 1, 1 - u)
                    pe.wait_ge(m["au_copied"], e + 1)
                    if not static or e >= 2:
                        pe.wait_ge(m["act_ready"], e - 1)
                    for k in range(4):
                        last = pe.matmul(psum[4 + u][:, SLOTS * k:SLOTS * (k + 1)], au[:, u, k * P:(k + 1) * P],
                                         K[:, K_FOLD:K_FOLD + SLOTS], start=True, stop=True)
                    last.then_inc(m["fold_full"], 1)

                turn_tokens(0, 0)
                blocks(pe, last_pair, step)
                pe.wait_ge(m["gather1"], last_pair * 16 + 32)
                pe.wait_ge(m["gather_index"], last_pair * 2 + 5)
                down(last_pair * 2 + 1, 1)

            pe.wait_ge(s["const_in"], 16)
            for l in range(LAYERS):
                pe.wait_ge(s["h_ready"], l + 1)
                to_channels(l, "ht", tok)
                for k in range(KD):
                    copied(pe, (l, "ht", k))
                project(l)
                pe.wait_ge(s["qkn_ready"], l + 1)
                to_channels(l, "qk", tok)
                for k in range(KD):
                    copied(pe, (l, "qk", k))
                projected(pe, l, (2, 3), False)
                compress(l)
                attend(l)
                projected(pe, l, (6, 7, 8), False)
                mlstm(l)
                hgrn(l)
                pe.wait_ge(s["y_ready"], l + 1)
                to_channels(l, "yt", tok)
                for k in range(KD):
                    copied(pe, (l, "yt", k))
                for j in range(2):
                    loaded(l * LOADS + len(W_IN) + j)
                for c in range(NC):
                    for j in range(2):
                        w = wring[:, (l * LOADS + len(W_IN) + j) % 2]
                        t = take(pe, (l, "wo", c, j))
                        for k in range(KD):
                            last = pe.matmul(t[:, :], hT[:, k, c * P:(c + 1) * P], w[:, k, :],
                                             start=(k == 0), stop=(k == KD - 1))
                        filled(last, (l, "wo", c, j))
                pe.wait_ge(s["h2_ready"], l + 1)
                to_channels(l, "h2", h2n)
                for k in range(KD):
                    copied(pe, (l, "h2", k))
                pe.wait_ge(s["wr_in"], 32 * (l + 1))
                t = take(pe, (l, "rt"))
                for c in range(NC):
                    for k in range(KD):
                        last = pe.matmul(t[:, 36 * c:36 * c + 36], hT[:, k, c * P:(c + 1) * P], wr[:, k, :],
                                         start=(k == 0), stop=(k == KD - 1))
                filled(last, (l, "rt"))
                route(l)
                experts(l)

        @block.gpsimd
        def _(pool):
            last_h_row, last_y_row = pool.to_reg(2 * SEQ - 1), pool.to_reg(4 * SEQ - 1)
            for l in range(LAYERS):
                m = moe[l]
                last_pair = pairs(pool, l)
                pool.wait_ge(s["h2_out"], 16 * (l + 1))

                def next_column(table, i, e, u, done, filled):
                    if not isinstance(e, int) or e >= 1:
                        pool.wait_ge(m[f"{done}{1 - u}"], gathered(e - 1, 1 - u))
                    pool.wait_ge(m[filled], e + 1)
                    pool.tensor_copy(index[:, i, 1 - u:2 - u], table[:, bass.ds(e + 1, 1)]).then_inc(m[filled], 1)

                def gather(e, u):
                    if not isinstance(e, int) or e >= 2:
                        pool.wait_ge(m["tr_full"], e - 1)
                    next_column(gi, 0, e, u, "gather", "gather_index")
                    pool.indirect_dma_start(
                        out=hg[:, u, :], out_offset=None, in_=h_rows,
                        in_offset=bass.IndirectOffsetOnAxis(ap=index[:, 0, u:u + 1], axis=0),
                        bounds_check=last_h_row, oob_is_err=False).then_inc(m[f"gather{u}"], 16)

                def step(e, u):
                    gather(e + 2, u)
                    pool.wait_ge(m["y_copied"], e + 1)
                    next_column(si, 1, e, u, "scatter", "scatter_index")
                    pool.indirect_dma_start(
                        out=y_rows, out_offset=bass.IndirectOffsetOnAxis(ap=index[:, 1, u:u + 1], axis=0),
                        in_=ysb[:, u, :], in_offset=None,
                        bounds_check=last_y_row, oob_is_err=False).then_inc(m[f"scatter{u}"], 16)

                for i, table in enumerate((gi, si)):
                    pool.tensor_copy(index[:, i, 0:1], table[:, 0:1]) \
                        .then_inc(m[("gather_index", "scatter_index")[i]], 1)
                for e in range(2):
                    gather(e, e)
                blocks(pool, last_pair, step)

        @block.scalar
        def _(act):
            sc = Steps(act, s["act_own"])

            def squares(l, junk):
                for c in range(NC):
                    act.activation(junk[:, c, :], X[:, c, :], ACT.Square, accum_out=ms[:, c:c + 1]).then_inc(s["ss"], 1)

            def root(l, u, a):
                act.wait_ge(s["mean"], ROOTS * l + u + 1)
                act.activation(a, a, ACT.Sqrt).then_inc(s["root"], 1)

            def evens(l, name, col):
                for k in range(0, KD, 2):
                    t = ready(act, (l, name, k))
                    if col is None:
                        ins = act.activation(hT[:, k, :] if name != "qk" else QKT[:, k, :], t[:, :], ACT.Copy)
                    else:
                        ins = act.activation(hT[:, k, :], t[:, :], ACT.Copy, scale=C[:, col + k:col + k + 1])
                    release(ins, (l, name, k))

            def experts(l):
                m = moe[l]
                last_pair = pairs(act, l)

                def outputs(e, u):
                    act.wait_ge(m["y_full"], e + 1)
                    if not isinstance(e, int) or e >= 2:
                        act.wait_ge(m[f"scatter{u}"], gathered(e - 2, u))
                    act.activation(ysb[:, u, :], psum[6 + u][:, :], ACT.Copy).then_inc(m["y_copied"], 1)

                def step(e, u):
                    static = isinstance(e, int)
                    act.wait_ge(m["au_full"], e + 1)
                    if not static or e >= 2:
                        act.wait_ge(m["fold_full"], e - 1)
                    act.activation(au[:, u, :], psum[2 + u][:, :], ACT.Copy).then_inc(m["au_copied"], 1)
                    if not static or e >= 1:
                        outputs(e - 1, 1 - u)
                    act.wait_ge(m["fold_full"], e + 1)
                    if not static or e >= 2:
                        act.wait_ge(m["act_ready"], e - 1)
                    act.activation(sil[:, u, :], psum[4 + u][:, 0:P], ACT.Silu).then_inc(m["silu_done"], 1)

                blocks(act, last_pair, step)
                outputs(last_pair * 2 + 1, 1)

            act.wait_ge(s["const_in"], 16)
            for l in range(LAYERS):
                x_ready(act, l)
                squares(l, tok)
                root(l, 0, ms[:, 0:NC])
                act.wait_ge(s["par_in"], 32 * (l + 1))
                evens(l, "ht", C_NM)
                for g, kind, a, n, what, c, vector in PTILES:
                    if vector:
                        continue
                    key = ptile(l, g, kind, what, c)
                    t = ready(act, key)
                    if kind == "n":
                        ins = act.activation(Pn[:, c, what:what + n], t[:, 0:n], ACT.Copy)
                    elif what[0] == "m":
                        ins = act.activation(mraw[:, int(what[1]), 3:], t[:, :], ACT.Copy)
                    else:
                        ins = act.activation(hqf[:, int(what[1]), :], t[:, :], ACT.Copy)
                    release(ins, key)
                act.wait_ge(s["lam_d"], l + 1)
                act.activation(lam4, lam4, ACT.Exp).then_inc(s["lam_e"], 1)
                projected(act, l, (2, 7, 8), True)
                for a, n in ((DG, 12), (BO, GW), (CG, GW)):
                    act.activation(Pn[:, :, a:a + n], Pn[:, :, a:a + n], ACT.Sigmoid).then_inc(s["gsig"], 1)
                root(l, 1, ms[:, 0:88])
                evens(l, "qk", None)
                for j in range(2):
                    t = ready(act, (l, "ch", j))
                    sc.then(act.activation(posb[0:HD, j:j + 1], t[0:HD, NCMP:NCMP + 1], ACT.Copy))
                    release(act.activation(Hd[0:HD, j, :], t[0:HD, 0:NCMP], ACT.Gelu_apprx_tanh,
                                           bias=posb[0:HD, j:j + 1]), (l, "ch", j))
                root(l, 2, ms[0:NCMP, 0:1])
                act.wait_ge(s["cs_x"], l + 1)
                act.activation(Sc[:, :, :], Sc[:, :, :], ACT.Exp).then_inc(s["cs_e"], 1)
                for i in range(len(ITERS) + 1):
                    if i < len(ITERS):
                        n = (ITERS[i][1] + 1) * P
                        copied(act, (l, "S", i))
                        act.activation(prob[:, i % 2, 0:n], negS[:, i % 2, 0:n], ACT.Exp, scale=-1.0,
                                       bias=nmax[:, i:i + 1], accum_out=psumcol[:, i:i + 1]).then_inc(s["exp_done"], 1)
                    if i:
                        n = (ITERS[i - 1][1] + 1) * P
                        t = ready(act, (l, "T", i - 1))
                        if i >= 3:
                            ready(act, (l, "O", i - 3))
                        release(act.activation(probT[:, (i - 1) % 2, 0:n], t[:, 0:n], ACT.Copy), (l, "T", i - 1))
                act.wait_ge(s["gate_a"], l + 1)
                sc.then(act.activation(gMt[:, :], gMt[:, :], ACT.Exp))
                act.activation(gMt[:, :], gMt[:, :], ACT.Ln, bias=1.0).then_inc(s["gate_b"], 1)
                act.wait_ge(s["conv_m"], l + 1)
                act.activation(mqk[:, :, :], mqk[:, :, :], ACT.Silu).then_inc(s["silu_m"], 1)
                copied(act, (l, "gc"))
                act.activation(gcol[:, 1], gcol[:, 1], ACT.Exp, scale=-1.0).then_inc(s["en_d"], 1)
                for h in range(HEADS):
                    for c in range(NC):
                        i = NC * h + c
                        n = SEQ - c * P
                        if c < NC - 1:
                            act.wait_ge(s["md"], 3 * (HEADS * l + h) + c + 1)
                        else:
                            copied(act, (l, "mb", h))
                        if i >= 2:
                            act.wait_ge(s["w_ready"], NC * HEADS * l + i - 1)
                        act.activation(E[:, c % 2, 0:n], D[:, c % 2, 0:n], ACT.Exp, scale=-1.0).then_inc(s["me"], 1)
                ready(act, (l, "mo", HEADS - 1))
                hq = hqf[:, 0:2, :]
                act.activation(hq, hq, ACT.Silu).then_inc(s["hsig"], 1)
                act.activation(Xe[:, :, :], hqf[:, 2:4, :], ACT.Sigmoid).then_inc(s["hsig"], 1)
                act.activation(kk[:, :, :], hqf[:, 2:4, :], ACT.Sigmoid, scale=-1.0).then_inc(s["hsig"], 1)
                act.wait_ge(s["lb_a"], l + 1)
                act.activation(lbx[:, :, :], lbx[:, :, :], ACT.Exp).then_inc(s["lb_b"], 1)
                act.wait_ge(s["hF"], l + 1)
                act.activation(qt[:, :, :], qt[:, :, :], ACT.Ln).then_inc(s["hln"], 1)
                act.activation(Xe[:, :, :], Xe[:, :, :], ACT.Ln).then_inc(s["hln"], 1)
                for lev in range(LEVELS + 1):
                    act.wait_ge(s["hx"], (LEVELS + 1) * l + lev + 1)
                    act.activation(Xe[:, :, :], Xe[:, :, :], ACT.Exp).then_inc(s["he"], 1)
                ready(act, (l, "ha", LEVELS, HEADS - 1))
                act.activation(qt[:, :, :], b[:, :, :], ACT.Exp).then_inc(s["he"], 1)
                for hp in range(2):
                    t = ready(act, (l, "hn", hp))
                    release(act.activation(kn[:, hp, :, :], t[:, :].rearrange("p (c n) -> p c n", c=NC), ACT.Copy),
                            (l, "hn", hp))
                act.wait_ge(s["ysq"], l + 1)
                act.activation(QKT[:, :, :].rearrange("p a b -> p (a b)"), tok[:, :, :].rearrange("p a b -> p (a b)"),
                               ACT.Square).then_inc(s["sq"], 1)
                root(l, 3, ms[:, 0:64])
                evens(l, "yt", None)
                copied(act, (l, "wo", NC - 1, 1))
                squares(l, h2n)
                root(l, 4, ms[:, 0:NC])
                evens(l, "h2", C_NF)
                for i in range(2):
                    act.wait_ge(s["rt_x"], 2 * l + i + 1)
                    a = rx[i]
                    act.activation(a, a, ACT.Exp).then_inc(s["rt_e"], 1)
                experts(l)

        @block.vector
        def _(dve):
            sv = Steps(dve, s["dve_own"])
            then = sv.then

            def inv_root(l, u, a):
                dve.wait_ge(s["root"], ROOTS * l + u + 1)
                then(dve.reciprocal(rs[:a.shape[0], 0:a.shape[1]], a))

            def normalise(l, u, dst, sig):
                dve.wait_ge(s["ss"], NC * (2 * l + (u == 4) + 1))
                dve.tensor_scalar(ms[:, 0:NC], ms[:, 0:NC], 1.0 / DIM, EPS, ALU.mult, ALU.add).then_inc(s["mean"], 1)
                inv_root(l, u, ms[:, 0:NC])
                for c in range(NC):
                    ins = dve.tensor_scalar(dst[:, c, :], X[:, c, :], rs[:, c:c + 1], None, ALU.mult)
                ins.then_inc(sig, 1)

            def odds(l, name, col):
                for k in range(1, KD, 2):
                    t = ready(dve, (l, name, k))
                    if col is None:
                        ins = dve.tensor_copy(hT[:, k, :] if name != "qk" else QKT[:, k, :], t[:, :])
                    else:
                        ins = dve.tensor_scalar(hT[:, k, :], t[:, :], C[:, col + k:col + k + 1], None, ALU.mult)
                    release(ins, (l, name, k))

            def mul(o, a, c):
                return dve.tensor_tensor(o, a, c, ALU.mult)

            def qk_norm(l):
                projected(dve, l, (0, 1, 2), True)
                for a, n, o in ((AQ, 512, 0), (DQ, GW, 512), (KS, HD, 768), (KW, HD, 896)):
                    last = mul(tok[:, :, o:o + n], Pn[:, :, a:a + n], Pn[:, :, a:a + n])
                then(last)
                for o, n, w, a in ((0, 512, HALF, 0), (512, GW, HD, 64), (768, HD, HD, 80), (896, HD, HD, 84)):
                    g = n // w
                    last = dve.tensor_reduce(ms[:, a:a + NC * g].rearrange("p (c g) -> p c g", c=NC),
                                             tok[:, :, o:o + n].rearrange("p c (g w) -> p c g w", w=w),
                                             AX.X, ALU.add)
                then(last)
                then(dve.tensor_scalar(ms[:, 0:64], ms[:, 0:64], 1.0 / HALF, EPS, ALU.mult, ALU.add))
                dve.tensor_scalar(ms[:, 64:88], ms[:, 64:88], 1.0 / HD, EPS, ALU.mult, ALU.add).then_inc(s["mean"], 1)
                inv_root(l, 1, ms[:, 0:88])
                rq = rs[:, 0:64].rearrange("p (c g) -> p c g", c=NC)[:, :, 0:8]
                then(dve.tensor_scalar(rq, rq, HALF ** -0.5, None, ALU.mult))
                then(dve.tensor_scalar(rs[:, 64:80], rs[:, 64:80], HD ** -0.5, None, ALU.mult))
                for a, n, w, o, r, g0 in ((AQ, 512, HALF, 0, 0, None), (DQ, GW, HD, 512, 64, None)):
                    g = n // w
                    last = mul(tok[:, :, o:o + n].rearrange("p c (g w) -> p c g w", w=w),
                               Pn[:, :, a:a + n].rearrange("p c (g w) -> p c g w", w=w),
                               rs[:, r:r + NC * g].rearrange("p (c g o) -> p c g o", c=NC, o=1)
                               .to_broadcast([P, NC, g, w]))
                for a, o, r in ((KS, 768, 80), (KW, 896, 84)):
                    for i in range(2):
                        last = mul(tok[:, :, o + HD * i:o + HD * (i + 1)], Pn[:, :, a:a + HD],
                                   rs[:, r:r + NC].rearrange("p (c o) -> p c o", o=1).to_broadcast([P, NC, HD]))
                then(last)
                for o, n, w, r in ((0, GW, HALF, R_DQ), (GW, GW, HALF, R_DK), (512, GW, HD, R_NQ),
                                   (768, P, HD, R_NK + HD), (896, P, HD, R_NK + 2 * HD)):
                    v = tok[:, :, o:o + n].rearrange("p c (g w) -> p c g w", w=w)
                    last = mul(v, v, R[:, r:r + w].rearrange("p (a b w) -> p a b w", a=1, b=1)
                               .to_broadcast([P, NC, n // w, w]))
                last.then_inc(s["qkn_ready"], 1)

            def differential_lambda(l):
                v = R[:, R_LAM:R_LAM + 4 * HALF].rearrange("p (a b w) -> p a b w", a=2, b=2)
                then(mul(tmp[:, 0:2 * HALF].rearrange("p (a w) -> p a w", a=2), v[:, :, 0, :], v[:, :, 1, :]))
                dve.tensor_reduce(lam4, tmp[:, 0:2 * HALF].rearrange("p (a w) -> p a w", a=2), AX.X, ALU.add) \
                    .then_inc(s["lam_d"], 1)
                dve.wait_ge(s["lam_e"], l + 1)
                then(dve.tensor_tensor(lam, lam4[:, 1:2], lam4[:, 0:1], ALU.subtract))
                then(dve.tensor_scalar(lam, lam, -(0.8 - 0.6 * math.exp(-0.3 * l)), None, ALU.add))

            def compress(l):
                t = ready(dve, (l, "cc", 0))
                release(dve.tensor_copy(Kc[0:NCMP, 0, :], t[0:NCMP, 0:HD]), (l, "cc", 0))
                t = ready(dve, (l, "cc", 1))
                release(dve.tensor_copy(Vc[0:NCMP, :], t[0:NCMP, 0:HD]), (l, "cc", 1))
                copied(dve, (l, "cc", 0))
                then(mul(tmp[0:NCMP, 0:HD], Kc[0:NCMP, 0, :], Kc[0:NCMP, 0, :]))
                then(dve.tensor_reduce(ms[0:NCMP, 0:1], tmp[0:NCMP, 0:HD], AX.X, ALU.add))
                dve.tensor_scalar(ms[0:NCMP, 0:1], ms[0:NCMP, 0:1], 1.0 / HD, EPS, ALU.mult, ALU.add) \
                    .then_inc(s["mean"], 1)
                inv_root(l, 2, ms[0:NCMP, 0:1])
                for i in (1, 0):
                    last = dve.scalar_tensor_tensor(Kc[0:NCMP, i, :], Kc[0:NCMP, 0, :], rs[0:NCMP, 0:1],
                                                    R[0:NCMP, R_NK:R_NK + HD], ALU.mult, ALU.mult)
                last.then_inc(s["ck_n"], 1)
                t = ready(dve, (l, "ck"))
                release(dve.tensor_copy(KcT[:, :], t[:, 0:NCMP]), (l, "ck"))
                bc = K[:, K_CMPB:K_CMPB + 16 * NCMP].rearrange("p (a n) -> p a n", n=NCMP)
                for o in range(2):
                    t = ready(dve, (l, "cs", o))
                    release(dve.tensor_tensor(Sc[:, o::2, :], t[:, 0:8 * NCMP].rearrange("p (a n) -> p a n", n=NCMP),
                                              bc[:, o::2, :], ALU.add), (l, "cs", o))
                for o in range(2):
                    copied(dve, (l, "cs", o))
                then(dve.tensor_reduce(cmx[:, :], Sc[:, :, :], AX.X, ALU.max))
                dve.tensor_tensor(Sc[:, :, :], Sc[:, :, :],
                                  cmx.rearrange("p (a o) -> p a o", o=1).to_broadcast([P, 16, NCMP]),
                                  ALU.subtract).then_inc(s["cs_x"], 1)
                dve.wait_ge(s["cs_e"], l + 1)
                dve.wait_ge(s["gsig"], 3 * (l + 1))
                then(dve.tensor_reduce(cfac[:, :], Sc[:, :, :], AX.X, ALU.add))
                then(dve.reciprocal(cfac[:, :], cfac[:, :]))
                f = cfac.rearrange("p (c h) -> p c h", c=NC)
                then(mul(f, f, Pn[:, :, DG:DG + 12:3]))
                S4 = Sc[:, :, :].rearrange("p (c h) n -> p c h n", c=NC)
                V4 = K[:, K_CMPV:K_CMPV + NC * NCMP].rearrange("p (c o n) -> p c o n", c=NC, o=1)
                then(mul(S4, S4, V4.to_broadcast([P, NC, HEADS, NCMP])))
                mul(Sc[:, :, :], Sc[:, :, :], cfac.rearrange("p (a o) -> p a o", o=1).to_broadcast([P, 16, NCMP])) \
                    .then_inc(s["cs_p"], 1)
                for c in range(NC):
                    t = ready(dve, (l, "cp", c))
                    release(dve.tensor_copy(PcT[0:NCMP, HEADS * c:HEADS * (c + 1), :],
                                            t[0:NCMP, :].rearrange("p (h q) -> p h q", h=HEADS)), (l, "cp", c))
                for c in range(NC):
                    t = ready(dve, (l, "co", c))
                    release(dve.tensor_copy(tok[:, c, 768:1024], t[:, 0:GW]), (l, "co", c))

            def attend(l):
                dve.wait_ge(s["bias_in"], 16 * (l + 1))
                for i in range(len(ITERS) + 2):
                    if i < len(ITERS):
                        m, c = ITERS[i]
                        n = (c + 1) * P
                        t = ready(dve, (l, "S", i))
                        if i >= 2:
                            dve.wait_ge(s["exp_done"], len(ITERS) * l + i - 1)
                        release(dve.tensor_tensor_reduce(
                            out=negS[:, i % 2, 0:n], in0=t[:, 0:n], in1=bias[:, MAPS[m][5], SEQ - n:SEQ],
                            scale=-1.0, scalar=3e38, op0=ALU.add, op1=ALU.min, accum_out=nmax[:, i:i + 1]),
                            (l, "S", i))
                    if i < 2:
                        continue
                    i -= 2
                    m, c = ITERS[i]
                    t = ready(dve, (l, "O", i))
                    dst = tok[:, c, MAPS[m][6] * HD:MAPS[m][6] * HD + HD]
                    f = fac[:, i:i + 1]
                    then(dve.reciprocal(f, psumcol[:, i:i + 1]))
                    if m < 8 and m % 2 == 0:
                        release(dve.tensor_scalar(dst, t[:, 0:HD], f, None, ALU.mult), (l, "O", i))
                        continue
                    if m < 8:
                        coef = lam
                    else:
                        g = DG + 3 * (MAPS[m][6] - 12) + 1 + m % 2
                        coef = Pn[:, c, g:g + 1]
                    then(mul(f, f, coef))
                    copied(dve, (l, "co", c) if m >= 8 and m % 2 == 0 else (l, "O", i - NC))
                    release(dve.scalar_tensor_tensor(dst, t[:, 0:HD], f, dst, ALU.mult, ALU.add), (l, "O", i))

            def mlstm(l):
                then(dve.memset(mraw[:, :, 0:3], 0.0))
                projected(dve, l, (4,), True)
                for j in range(4):
                    for i in range(4):
                        w = C[:, C_CONV + 4 * i + j:C_CONV + 4 * i + j + 1]
                        src = mraw[:, i, j:j + SEQ]
                        if j == 0:
                            last = dve.tensor_scalar(mqk[:, i, :], src, w, None, ALU.mult)
                        else:
                            last = dve.scalar_tensor_tensor(mqk[:, i, :], src, w, mqk[:, i, :], ALU.mult, ALU.add)
                    if j < 3:
                        then(last)
                last.then_inc(s["conv_m"], 1)
                t = ready(dve, (l, "gi"))
                release(dve.tensor_scalar(gA[:, :], t[0:HEADS, :], C[0:HEADS, C_GB:C_GB + 1], None, ALU.add),
                        (l, "gi"))
                t = ready(dve, (l, "gf"))
                release(dve.tensor_scalar(gM[:, :], t[0:HEADS, :], C[0:HEADS, C_GB + 1:C_GB + 2], None, ALU.add),
                        (l, "gf"))
                copied(dve, (l, "gf"))
                dve.scalar_tensor_tensor(gMt[:, :], gM[:, :], -1.0, gM[:, :], ALU.mult, ALU.min).then_inc(s["gate_a"], 1)
                dve.wait_ge(s["gate_b"], l + 1)
                then(dve.scalar_tensor_tensor(gM[:, :], gM[:, :], 0.0, gMt[:, :], ALU.min, ALU.subtract))
                then(dve.tensor_tensor_scan(gMt[:, :], K[0:HEADS, K_IOTA + PER_GROUP - 1:K_IOTA + PER_GROUP].to_broadcast([HEADS, SEQ]), gM[:, :], 0.0,
                                            ALU.mult, ALU.add))
                then(dve.tensor_tensor(gA[:, :], gA[:, :], gMt[:, :], ALU.subtract))
                then(dve.tensor_tensor_scan(gM[:, :], gA[:, :], gA[:, :], 0.0, ALU.max, ALU.max))
                dve.tensor_tensor(gMt[:, :], gMt[:, :], gM[:, :], ALU.add).then_inc(s["gate_r"], 1)
                t = ready(dve, (l, "gc"))
                release(dve.tensor_copy(gcol[:, :, :, :].rearrange("p a c h -> p (a c h)"), t[:, 0:32]), (l, "gc"))
                projected(dve, l, (6,), True)
                dve.memset(Vm[:, :, :, HD:HD + 1], 1.0)
                dve.tensor_copy(Vm[:, :, :, 0:HD], Pn[:, :, BV:BV + GW].rearrange("p c (h w) -> p c h w", h=HEADS)) \
                    .then_inc(s["vm_ready"], 1)
                copied(dve, (l, "gc"))
                dve.wait_ge(s["en_d"], l + 1)
                for h in range(HEADS):
                    mb = ready(dve, (l, "mb", h))

                    def weights(c):
                        n = SEQ - c * P
                        i = NC * h + c
                        dve.wait_ge(s["me"], NC * HEADS * l + i + 1)
                        t = ready(dve, (l, "ms", h, c))
                        w = WT[:, h % 2, WOFF[c]:WOFF[c] + n]
                        release(dve.scalar_tensor_tensor(w, t[:, 0:n], HD ** -0.5, E[:, c % 2, 0:n],
                                                         ALU.mult, ALU.mult), (l, "ms", h, c))
                        copied(dve, (l, "ms", h, c))
                        mul(w[:, 0:P], w[:, 0:P], caus).then_inc(s["w_ready"], 1)

                    for c in range(NC):
                        n = SEQ - c * P
                        i = NC * h + c
                        if i >= 2:
                            dve.wait_ge(s["me"], NC * HEADS * l + i - 1)
                        ins = dve.tensor_scalar(D[:, c % 2, 0:n], mb[:, c * P:SEQ], gcol[:, 0, c, h:h + 1], 0.0,
                                                ALU.subtract, ALU.max)
                        if c < NC - 1:
                            ins.then_inc(s["md"], 1)
                        else:
                            release(ins, (l, "mb", h))
                        if c:
                            weights(c - 1)
                    weights(NC - 1)
                    t = ready(dve, (l, "mo", h))
                    t = t[:, 0:NC * 65].rearrange("p (c w) -> p c w", c=NC)
                    den = t[:, :, HD]
                    md = mden[:, :]
                    then(dve.tensor_copy(md, den))
                    then(dve.scalar_tensor_tensor(md, md, -1.0, md, ALU.mult, ALU.max))
                    then(dve.tensor_tensor(md, md, gcol[:, 1, :, h], ALU.max))
                    then(dve.reciprocal(md, md))
                    release(mul(tok[:, :, GW + h * HD:GW + (h + 1) * HD], t[:, :, 0:HD],
                                md.rearrange("p (c o) -> p c o", o=1).to_broadcast([P, NC, HD])), (l, "mo", h))

            def hgrn(l):
                x = C[:, C_LB:C_LB + 4].rearrange("p (l t) -> p l t", l=2)
                m = lbc[:, 0, :]
                then(dve.tensor_tensor(m, x[:, 0, :], x[:, 1, :], ALU.max))
                dve.tensor_tensor(lbx[:, :, :], x, m.rearrange("p (o t) -> p o t", o=1).to_broadcast([P, 2, 2]),
                                  ALU.subtract).then_inc(s["lb_a"], 1)
                dve.wait_ge(s["lb_b"], l + 1)
                then(dve.tensor_tensor(m, lbx[:, 0, :], lbx[:, 1, :], ALU.add))
                then(dve.reciprocal(m, m))
                then(mul(lbs[:, :, :], lbx[:, :, :], m.rearrange("p (o t) -> p o t", o=1).to_broadcast([P, 2, 2])))
                lb, lf, om, df = (lbc[:, i, :] for i in range(4))
                if l == 0:
                    then(dve.tensor_copy(lb, lbs[:, 0, :]))
                else:
                    then(dve.tensor_tensor(lb, lbs[:, 0, :], lbs[:, 1, :], ALU.add))
                then(dve.tensor_tensor(lb, lb, lbs[:, 0, :], ALU.subtract))
                then(dve.tensor_scalar(lf, lb, 1e-30, None, ALU.max))
                then(dve.tensor_scalar(om, lb, -1.0, 1.0, ALU.mult, ALU.add))
                then(dve.tensor_tensor(df, lf, lb, ALU.subtract))
                dve.wait_ge(s["hsig"], 3 * (l + 1))
                for i in range(2):
                    dve.tensor_scalar(Xe[:, i, :], Xe[:, i, :], om[:, i:i + 1], lf[:, i:i + 1], ALU.mult, ALU.add)
                    last = dve.tensor_scalar(kk[:, i, :], kk[:, i, :], om[:, i:i + 1], df[:, i:i + 1],
                                             ALU.mult, ALU.subtract)
                then(last)
                dve.tensor_scalar(qt[:, :, :], Xe[:, :, :], 1.0 / LN_SPLIT, None, ALU.max)
                then(dve.memset(A[:, :, :], 0.0))
                dve.tensor_scalar(Xe[:, :, :], Xe[:, :, :], LN_SPLIT, 1.0, ALU.mult, ALU.min).then_inc(s["hF"], 1)
                dve.wait_ge(s["hF"], l + 1)
                dve.memset(nopcell, 0.0).then_inc(s["hqk"], 1)
                dve.wait_ge(s["hln"], 2 * (l + 1))
                then(dve.tensor_tensor(qt[:, :, :], qt[:, :, :], Xe[:, :, :], ALU.add))
                for i in range(2):
                    last = dve.tensor_tensor_scan(b[:, i, :], K[:, K_SEG:K_SEG + SEQ], qt[:, i, :], 0.0,
                                                  ALU.mult, ALU.add)
                then(last)

                def products(lev):
                    mask = K[:, K_LVL + lev * P:K_LVL + (lev + 1) * P].bitcast(I32) \
                        .rearrange("p (o t) -> p o t", o=1).to_broadcast([P, NC, P])
                    for h in range(HEADS):
                        t = ready(dve, (l, "ha", lev, h))
                        release(dve.copy_predicated(A[:, h, :].rearrange("p (c t) -> p c t", c=NC), mask,
                                                    t[:, :].rearrange("p (c t) -> p c t", c=NC)), (l, "ha", lev, h))

                flat = lambda v: v[:, :, :].rearrange("p a n -> p (a n)")
                for lev in range(1, LEVELS + 2):
                    if lev <= LEVELS:
                        w = HB >> (lev - 1)
                        bv, xv = (flat(v).rearrange("p (n w) -> p n w", w=w) for v in (b, Xe))
                        seam = bv[:, :, w // 2 - 1:w // 2].to_broadcast([P, 2 * SEQ // w, w // 2])
                        dve.tensor_tensor(xv[:, :, w // 2:], bv[:, :, w // 2:], seam, ALU.subtract)
                        dve.tensor_tensor(xv[:, :, 0:w // 2], seam, bv[:, :, 0:w // 2], ALU.subtract) \
                            .then_inc(s["hx"], 1)
                    else:
                        bv, xv = (flat(v).rearrange("p (n w) -> p n w", w=HB) for v in (b, Xe))
                        dve.tensor_tensor(xv, bv[:, :, HB - 1:HB].to_broadcast([P, 2 * NB, HB]), bv, ALU.subtract) \
                            .then_inc(s["hx"], 1)
                    products(lev - 1)
                    dve.wait_ge(s["he"], (LEVELS + 2) * l + lev)
                    if lev <= LEVELS:
                        mul(qt[:, :, :], hqf[:, 0:2, :], Xe[:, :, :])
                    mul(kt[:, :, :], kk[:, :, :], Xe[:, :, :]).then_inc(s["hqk"], 1)
                    dve.wait_ge(s["hqk"], (LEVELS + 2) * l + lev + 1)
                dve.wait_ge(s["he"], (LEVELS + 2) * (l + 1))
                then(dve.tensor_copy(dec[:, :, :], qt[:, :, HB - 1:SEQ:HB]))
                mul(qt[:, :, :], hqf[:, 0:2, :], qt[:, :, :]).then_inc(s["hq_in"], 1)
                for i in range(NB - 1):
                    c, j = i // 4, i % 4
                    for hp in range(2):
                        t = ready(dve, (l, "hu", hp, j))
                        u = t[:, c * P:(c + 1) * P]
                        if i == 0:
                            ins = dve.tensor_copy(St[:, hp, 1, :], u)
                        else:
                            ins = dve.scalar_tensor_tensor(St[:, hp, i + 1, :], St[:, hp, i, :],
                                                           dec[:, hp, i:i + 1], u, ALU.mult, ALU.add)
                        if c == (2 if j == 3 else 3):
                            release(ins, (l, "hu", hp, j))
                            if hp:
                                copied(dve, (l, "hu", 1, j))
                        elif hp:
                            then(ins)
                dve.memset(St[:, :, 0, :], 0.0).then_inc(s["hst"], 1)
                for c in range(NC):
                    for o in range(2):
                        t = ready(dve, (l, "ho", c, o))
                        v = tok[:, c, 512:768].rearrange("p (a o n) -> p o a n", a=2, o=2)
                        release(dve.tensor_copy(v[:, o], t[:, 0:P].rearrange("p (a n) -> p a n", a=2)),
                                (l, "ho", c, o))

            def output_norms(l):
                copied(dve, (l, "ho", NC - 1, 1))
                copied(dve, (l, "O", len(ITERS) - 1))
                dve.memset(nopcell, 0.0).then_inc(s["ysq"], 1)
                dve.wait_ge(s["sq"], l + 1)
                then(dve.tensor_reduce(ms[:, 0:64], QKT[:, :, :].rearrange("p a (g w) -> p (a g) w", w=HD), AX.X, ALU.add))
                dve.tensor_scalar(ms[:, 0:64], ms[:, 0:64], 1.0 / HD, EPS, ALU.mult, ALU.add).then_inc(s["mean"], 1)
                inv_root(l, 3, ms[:, 0:64])
                ra = rs[:, 0:64].rearrange("p (c h) -> p c h", c=NC)[:, :, 0:HEADS]
                then(dve.tensor_scalar(ra, ra, 1.0 - (0.8 - 0.6 * math.exp(-0.3 * l)), None, ALU.mult))
                tv = tok[:, :, :].rearrange("p c (h w) -> p (c h) w", w=HD)
                then(mul(tv, tv, rs[:, 0:64].rearrange("p (g o) -> p g o", o=1).to_broadcast([P, 64, HD])))
                then(mul(tok[:, :, :], tok[:, :, :], R[:, R_OG:R_OG + DIM].rearrange("p (o n) -> p o n", o=1)
                         .to_broadcast([P, NC, DIM])))
                mul(tok[:, :, GW:2 * GW], tok[:, :, GW:2 * GW], Pn[:, :, BO:BO + GW])
                mul(tok[:, :, 2 * GW:3 * GW], tok[:, :, 2 * GW:3 * GW], Pn[:, :, CG:CG + GW]).then_inc(s["y_ready"], 1)

            def route(l):
                t = ready(dve, (l, "rt"))
                release(dve.tensor_tensor(rt[:, :, :], t[:, 0:36 * NC].rearrange("p (c n) -> p c n", c=NC),
                                          R[:, R_BG:R_BG + 36].rearrange("p (o n) -> p o n", o=1)
                                          .to_broadcast([P, NC, 36]), ALU.add), (l, "rt"))
                copied(dve, (l, "rt"))
                desc = K[:, K_IOTA:K_IOTA + PER_GROUP].rearrange("p (o n) -> p o n", o=1)

                def col(v, n):
                    return v.rearrange("p (c o) -> p c o", o=1).to_broadcast([P, NC, n])

                def first_best(v, n, best, hot):
                    then(dve.tensor_reduce(best, v, AX.X, ALU.max))
                    then(dve.tensor_tensor(hot, v, col(best, n), ALU.is_equal))
                    then(mul(hot, hot, desc[:, :, PER_GROUP - n:].to_broadcast([P, NC, n])))
                    then(dve.tensor_reduce(rmark, hot, AX.X, ALU.max))
                    then(dve.tensor_tensor(hot, hot, col(rmark, n), ALU.is_equal))

                first_best(rt[:, :, 0:GROUPS], GROUPS, rbest, ghot)
                dve.tensor_tensor(rx[0], rt[:, :, 0:GROUPS], col(rbest, GROUPS), ALU.subtract).then_inc(s["rt_x"], 1)
                dve.wait_ge(s["rt_e"], 2 * l + 1)
                then(dve.tensor_reduce(gprob, rx[0], AX.X, ALU.add))
                then(dve.reciprocal(gprob, gprob))
                gh4 = ghot.rearrange("p c (g o) -> p c g o", o=1).to_broadcast([P, NC, GROUPS, PER_GROUP])
                then(mul(gate[:, :, :, :], rt[:, :, GROUPS:].rearrange("p c (g e) -> p c g e", g=GROUPS), gh4))
                then(dve.tensor_reduce(l8, gate[:, :, :, :].rearrange("p c g e -> p c e g"), AX.X, ALU.add))
                first_best(l8, PER_GROUP, rbest, hot1)
                then(dve.scalar_tensor_tensor(l8, hot1, -3e38, l8, ALU.mult, ALU.add))
                first_best(l8, PER_GROUP, rsecond, hot2)
                dve.tensor_tensor(rx[1], rsecond, rbest, ALU.subtract).then_inc(s["rt_x"], 1)
                dve.wait_ge(s["rt_e"], 2 * l + 2)
                then(dve.tensor_scalar(rbest, rx[1], 1.0, None, ALU.add))
                then(dve.reciprocal(rbest, rbest))
                then(mul(gprob, gprob, rbest))
                then(mul(rx[1], rx[1], gprob))
                for i, hot in enumerate((hot1, hot2)):
                    last = mul(hots[:, :, EXPERTS * i:EXPERTS * (i + 1)].rearrange("p c (g e) -> p c g e", g=GROUPS),
                               hot.rearrange("p c (o e) -> p c o e", o=1).to_broadcast([P, NC, GROUPS, PER_GROUP]),
                               gh4)
                then(last)
                dve.tensor_tensor(selsum[:, :, :], hots[:, :, 0:EXPERTS], hots[:, :, EXPERTS:], ALU.add) \
                    .then_inc(s["sel_ready"], 1)
                t = ready(dve, (l, "rk"))
                release(dve.tensor_copy(rk[:, :, :].rearrange("p a b -> p (a b)"), t[:, 0:(NC + 1) * EXPERTS]),
                        (l, "rk"))
                copied(dve, (l, "rk"))
                thr = K[:, K_THR:K_THR + 8].rearrange("p (o n) -> p o n", o=1)

                def up(v, n):
                    return v.rearrange("p (a o) -> p a o", o=1).to_broadcast([v.shape[0], v.shape[1], n])

                cmp = rtmp[:, 0:8 * EXPERTS].rearrange("p (a b) -> p a b", b=8)
                then(dve.tensor_tensor(cmp, up(rk[:, NC, :], 8), thr.to_broadcast([P, EXPERTS, 8]), ALU.is_gt))
                then(dve.tensor_reduce(nblk, cmp, AX.X, ALU.add))
                then(dve.tensor_tensor_scan(bend, K[:, K_IOTA + PER_GROUP - 1:K_IOTA + PER_GROUP]
                                            .to_broadcast([P, EXPERTS]), nblk, 0.0, ALU.mult, ALU.add))
                then(dve.tensor_tensor(bst, bend, nblk, ALU.subtract))
                for i in range(2):
                    last = mul(oslot[:, i::2, 0:EXPERTS], hots8[:, i::2, :], rk[:, 0:NC, :])
                mul(oblk8, hots8[:, :, :], bst.rearrange("p (o e) -> p o e", o=1).to_broadcast([P, 2 * NC, EXPERTS]))
                then(dve.memset(hg[:, :, :], 0.0))
                dve.tensor_reduce(rank, oslot[:, :, 0:EXPERTS], AX.X, ALU.add)
                then(dve.tensor_reduce(blk, oblk8, AX.X, ALU.add))
                c8 = rtmp[:, 0:64].rearrange("p (a b) -> p a b", b=8)
                then(dve.tensor_tensor(c8, up(rank, 8), thr.to_broadcast([P, 8, 8]), ALU.is_ge))
                then(dve.tensor_reduce(quot, c8, AX.X, ALU.add))
                then(dve.tensor_tensor(blk, blk, quot, ALU.add))
                dve.tensor_scalar(blk, blk, -1.0, None, ALU.add)
                then(dve.tensor_scalar(quot, quot, -float(SLOTS), float(SLOTS), ALU.mult, ALU.add))
                then(dve.tensor_tensor(rank, rank, quot, ALU.add))
                dve.tensor_tensor(oslot[:, :, :], K[:, K_SLOT:K_SLOT + P].rearrange("p (o n) -> p o n", o=1)
                                  .to_broadcast([P, 8, P]), up(rank, P), ALU.is_equal)
                then(dve.tensor_tensor(oblk[:, :, 2, :], K[:, K_BLK:K_BLK + TABW].rearrange("p (o n) -> p o n", o=1)
                                       .to_broadcast([P, 8, TABW]), up(blk, TABW), ALU.is_equal))
                mul(oblk[:, :, 0, :], oblk[:, :, 2, :], up(K[:, K_T2:K_T2 + 8], TABW))
                mul(oblk[:, :, 1, :], oblk[:, :, 2, :], up(K[:, K_T4:K_T4 + 8], TABW)).then_inc(s["ob_ready"], 1)
                eb = rtmp[0:1, :].rearrange("p (b e) -> p b e", e=EXPERTS)
                be = bend[0:1, :]
                then(dve.tensor_tensor(eb, be.rearrange("p (o e) -> p o e", o=1).to_broadcast([1, BLOCKS, EXPERTS]),
                                       up(K[0:1, K_BLK:K_BLK + BLOCKS], EXPERTS), ALU.is_le))
                then(dve.tensor_reduce(ebf[0:1, 0:BLOCKS], eb, AX.X, ALU.add))
                then(dve.tensor_scalar(ebf[0:1, 0:BLOCKS], ebf[0:1, 0:BLOCKS], float(EXPERTS - 1), None, ALU.min))
                then(dve.tensor_tensor(rtmp[0:1, 0:BLOCKS // 2 - 1], be[:, EXPERTS - 1:].to_broadcast([1, BLOCKS // 2 - 1]),
                                       K[0:1, K_BLK + 2:K_BLK + BLOCKS:2], ALU.is_gt))
                then(dve.tensor_reduce(ebf[0:1, BLOCKS:BLOCKS + 1], rtmp[0:1, 0:BLOCKS // 2 - 1], AX.X, ALU.add))
                dve.tensor_copy(ebt[0:1, 0:BLOCKS + 1], ebf[0:1, 0:BLOCKS + 1])
                t = ready(dve, (l, "rb"))
                release(dve.tensor_copy(tab[:, :, :].rearrange("p a b -> p (a b)"), t[:, 0:3 * TABW]), (l, "rb"))
                copied(dve, (l, "rb"))
                then(dve.tensor_scalar(tab[:, 2, :], tab[:, 2, :], -1.0, 1.0, ALU.mult, ALU.add))
                then(dve.tensor_scalar(tab[:, 2, :], tab[:, 2, :], K[:, K_OOB:K_OOB + 1],
                                       K[:, K_HALF:K_HALF + 1], ALU.mult, ALU.add))
                for i in range(2):
                    last = dve.tensor_tensor(tab[:, i, :], tab[:, i, :], tab[:, 2, :], ALU.add)
                then(last)
                dve.tensor_copy(gi, tab[:, 0, :])
                dve.tensor_copy(si, tab[:, 1, :]).then_inc(s["route_ready"], 1)

            def experts(l):
                m = moe[l]
                last_pair = pairs(dve, l)
                gain = C[:, C_NF:C_NF + KD].rearrange("p (j k o) -> p k j o", j=2, o=1) \
                    .to_broadcast([P, 4, 2, SLOTS])

                def tokens(e, u):
                    static = isinstance(e, int)
                    dve.wait_ge(m["tr_full"], e + 1)
                    if not static or e >= 2:
                        dve.wait_ge(m["au_full"], e - 1)
                    mul(hgT[:, u].rearrange("p k (j n) -> p k j n", j=2),
                        psum[u][:, :].rearrange("p (k j n) -> p k j n", k=4, j=2), gain) \
                        .then_inc(m["tr_copied"], 1)

                def step(e, u):
                    tokens(e + 1, 1 - u)
                    dve.wait_ge(m["silu_done"], e + 1)
                    if not isinstance(e, int) or e >= 2:
                        dve.wait_ge(m["y_full"], e - 1)
                    mul(actT[:, u, :], sil[:, u, :], psum[4 + u][:, P:2 * P]).then_inc(m["act_ready"], 1)

                tokens(0, 0)
                blocks(dve, last_pair, step)
                for c in range(NC):
                    dve.wait_ge(yc_in[c], 16 * (l + 1))
                    for j, w in enumerate((gprob, rx[1])):
                        ins = dve.scalar_tensor_tensor(X[:, c, :], yc[:, c, DIM * j:DIM * (j + 1)], w[:, c:c + 1],
                                                       X[:, c, :], ALU.mult, ALU.add)
                        if j == 0:
                            then(ins)
                ins.then_inc(s["x_new"], 1)

            dve.wait_ge(s["const_in"], 16)
            for l in range(LAYERS):
                x_ready(dve, l)
                normalise(l, 0, tok, s["h_ready"])
                dve.wait_ge(s["par_in"], 32 * (l + 1))
                odds(l, "ht", C_NM)
                for g, kind, a, n, what, c, vector in PTILES:
                    if not vector:
                        continue
                    key = ptile(l, g, kind, what, c)
                    t = ready(dve, key)
                    if kind == "n":
                        ins = dve.tensor_copy(Pn[:, c, what:what + n], t[:, 0:n])
                    elif what == "kv":
                        for j in range(2):
                            src = t[HD * j:HD * (j + 1), :]
                            dve.tensor_copy(kcT[0:HD, j, :], src)
                            ins = dve.tensor_copy(kcT[HD:P, j, 0:SEQ - 1], src[:, 1:])
                    elif what[0] == "m":
                        ins = dve.tensor_copy(mraw[:, int(what[1]), 3:], t[:, :])
                    else:
                        ins = dve.tensor_copy(hqf[:, int(what[1]), :], t[:, :])
                    release(ins, key)
                differential_lambda(l)
                qk_norm(l)
                odds(l, "qk", None)
                compress(l)
                attend(l)
                mlstm(l)
                hgrn(l)
                output_norms(l)
                odds(l, "yt", None)
                for c in range(NC):
                    for j in range(2):
                        t = ready(dve, (l, "wo", c, j))
                        x = X[:, c, 512 * j:512 * j + 512]
                        release(dve.tensor_tensor(x, x, t[:, :], ALU.add), (l, "wo", c, j))
                normalise(l, 4, h2n, s["h2_ready"])
                odds(l, "h2", C_NF)
                route(l)
                experts(l)


_NAMED = ["x", "w_in", "w_out", "nsa_cmp_w1", "nsa_cmp_w2", "moe_w_group", "moe_w_expert",
          "moe_w_gate", "moe_w_up", "moe_w_down"]


def _constants():
    p = np.arange(P)
    k = np.zeros((P, KW_ALL), np.float32)
    k[:, K_ID:K_ID + P] = np.eye(P)
    k[:, K_LVL:K_LVL + P] = np.eye(P)
    s_, t_ = p[:, None], p[None, :]
    for lev in range(1, LEVELS + 1):
        w = HB >> (lev - 1)
        k[:, K_LVL + lev * P:K_LVL + (lev + 1) * P] = \
            (s_ // w == t_ // w) & (s_ % w < w // 2) & (t_ % w >= w // 2)
    k[:, K_CAUS:K_CAUS + P] = s_ <= t_
    slopes = 2.0 ** (-8.0 * np.arange(1, 2 * HEADS + 1) / (2 * HEADS))
    diff, nsa = slopes[0::2].astype(np.float32), slopes[1::2].astype(np.float32)
    tokens = P * np.arange(NC)[None, :, None] + p[:, None, None]
    dist = tokens - (CMP_STRIDE * np.arange(NCMP) + CMP_LEN - 1)[None, None, :]
    v = dist >= 0
    cb = np.where(v[:, :, None, :], -nsa[None, None, :, None] * dist[:, :, None, :].astype(np.float32),
                  np.float32(NEG))
    k[:, K_CMPB:K_CMPB + 16 * NCMP] = cb.reshape(P, -1)
    k[:, K_CMPV:K_CMPV + NC * NCMP] = v.reshape(P, -1)
    k[:, K_SEG:K_SEG + SEQ] = np.arange(SEQ) % HB != 0
    k[:, K_IOTA:K_IOTA + PER_GROUP] = np.arange(PER_GROUP, 0, -1)
    k[:, K_SLOT:K_SLOT + P] = np.arange(P) % SLOTS
    k[:, K_BLK:K_BLK + TABW] = np.arange(TABW)
    k[:, K_THR:K_THR + 8] = SLOTS * np.arange(8)
    k[:, K_UP:K_UP + P] = s_ < t_
    k[:, K_FOLD:K_FOLD + SLOTS] = s_ % SLOTS == np.arange(SLOTS)[None, :]
    token = P * (np.arange(2 * NC) // 2)[None, :] + s_
    k[:, K_T2:K_T2 + 2 * NC] = 2 * token
    k[:, K_T4:K_T4 + 2 * NC] = 4 * token + 2 * (np.arange(2 * NC) % 2)[None, :]
    k[:, K_HALF] = p // SLOTS
    k[:, K_OOB] = OUTSIDE + p
    d = (p[:, None] + (SEQ - P) - np.arange(SEQ)[None, :]).astype(np.float32)
    al = np.stack([np.where(d >= 0, -sl * d, np.float32(NEG)) for sl in np.concatenate([diff, nsa])], 1)
    return k, al.reshape(P, -1).astype(np.float32)


def _layout(v):
    rows = np.concatenate([v[n].reshape(LAYERS, -1) for n in (
        "diff_q_gain", "diff_k_gain", "nsa_q_gain", "nsa_k_gain", "diff_sub_gain", "mlstm_out_gain",
        "hgrn_out_gain", "nsa_out_gain", "moe_b_group", "moe_b_expert", "diff_lambda")], 1)
    cols = np.zeros((LAYERS, P, CW), np.float32)
    for l in range(LAYERS):
        cols[l, :, C_NM:C_NM + KD] = v["norm_mix"][l].reshape(KD, P).T
        cols[l, :, C_NF:C_NF + KD] = v["norm_ffn"][l].reshape(KD, P).T
        cols[l, :, C_CONV:C_CONV + 16] = v["mlstm_conv"][l].reshape(4, 4, P).transpose(2, 1, 0).reshape(P, 16)
        cols[l, :, C_POS:C_POS + 32] = v["nsa_cmp_pos"][l].reshape(2, 16, P).transpose(2, 0, 1).reshape(P, 32)
        cols[l, :, C_LB:C_LB + 4] = v["hgrn_lower_bounds"].reshape(LAYERS, 2, P).transpose(2, 0, 1).reshape(P, 4)
        cols[l, 0:HEADS, C_GB:C_GB + 2] = v["mlstm_gate_bias"][l].T
    return rows, cols


def kernel(**inputs):
    import concourse.bacc as bacc
    from concourse.bass_utils import run_bass_kernel_spmd

    nc = bacc.Bacc("TRN2", target_bir_lowering=False, num_devices=1)
    v = {n: np.ascontiguousarray(a) for n, a in inputs.items()}
    arrays = {n: v[n] for n in _NAMED}
    arrays["x"] = v["x"].reshape(SEQ, DIM)
    for n in ("moe_w_gate", "moe_w_up", "moe_w_down"):
        arrays[n] = v[n].reshape(LAYERS, EXPERTS, *v[n].shape[3:])
    arrays["rows"], arrays["columns"] = _layout(v)
    arrays["constants"], arrays["alibi"] = _constants()
    d = {n: nc.dram_tensor(n, a.shape, mybir.dt.from_np(a.dtype), kind="ExternalInput").ap()
         for n, a in arrays.items()}
    out = nc.dram_tensor("out", (SEQ, DIM), F32, kind="ExternalOutput").ap()
    build(nc, d, out)
    r = run_bass_kernel_spmd(nc, [arrays], core_ids=[0])
    return r.results[0]["out"].reshape(1, SEQ, DIM)
```

```python
import math
from contextlib import ExitStack

import numpy as np
import concourse.bass as bass
from concourse import mybir

F32 = mybir.dt.float32
I32 = mybir.dt.int32
ALU = mybir.AluOpType
ACT = mybir.ActivationFunctionType
AX = mybir.AxisListType

LAYERS, SEQ, DIM = 2, 512, 1024
P = 128
NC = SEQ // P
KD = DIM // P
HEADS, HD = 4, 64
GW = HEADS * HD
HALF = HD // 2
IN_COLS = 3476
EPS = 1e-6
NEG = -1e30
CMP_LEN, CMP_STRIDE = 32, 16
NCMP = (SEQ - CMP_LEN) // CMP_STRIDE + 1
EXPERTS, GROUPS, PER_GROUP, FF = 32, 4, 8, 256
HB = 32
NB = SEQ // HB
LEVELS = 5
LN_SPLIT = 2.0 ** 50

AQ, AK, AV, BV, BI, BF, BO, CI, CG, DQ, KS, VS, KW, VW, DG, PW = (
    0, 256, 512, 768, 1024, 1028, 1032, 1288, 1544, 1800, 2056, 2120, 2184, 2248, 2312, 2324)
W_IN = [(0, 512), (2824, 384), (3208, 268), (512, 256), (768, 512), (1800, 512), (1280, 260), (1540, 260),
        (2312, 512)]
PROJ = [
    [("n", 0, 512, AQ)],
    [("n", 0, 256, DQ), ("t", 256, 128, "kv")],
    [("n", 0, 268, KS)],
    [("n", 0, 256, AV)],
    [("t", 128 * i, 128, f"m{i}") for i in range(4)],
    [("t", 128 * i, 128, f"g{i}") for i in range(4)],
    [("n", 0, 260, BV)],
    [("n", 0, 260, BF)],
    [("n", 0, 512, CI)],
]
LOADS = len(W_IN) + 2

R_DQ, R_DK, R_NQ, R_NK, R_OG, R_BG, R_BE, R_LAM, RW = 0, 32, 64, 128, 320, 1344, 1348, 1380, 1508
C_NM, C_NF, C_CONV, C_POS, C_LB, C_GB, CW = 0, 8, 16, 32, 64, 68, 70
K_ID, K_LVL, K_CAUS, K_CMPB, K_CMPV, K_SEG, K_IOTA = (
    0, 128, 896, 1024, 1520, 1644, 2156)
K_SLOT, K_BLK, K_THR, K_UP, K_FOLD, K_T2, K_T4, K_HALF, K_OOB, K_MASK, KW_ALL = (
    2164, 2292, 2344, 2352, 2480, 2544, 2552, 2560, 2561, 2562, 2568)

MAPS = []
for _h in range(HEADS):
    for _c in range(2):
        MAPS.append((("h", 2 * _h + _c), 2 + _h // 2, AV + HD * _h, _h, _h))
NSA_Q = (0, 1, 4, 5)
for _h in range(HEADS):
    for _c in range(2):
        MAPS.append((("q", NSA_Q[_h]), 6 + _c, (VS, VW)[_c], HEADS + _h, 12 + _h))
ITERS = [(2 * h + m, c) for h in range(HEADS) for c in range(NC) for m in range(2)]
PAIRED = len(ITERS)
ITERS += [(m, c) for m in range(2 * HEADS, 4 * HEADS) for c in range(NC)]
UNITS = [(i, i + 1) for i in range(0, PAIRED, 2)] + [(i,) for i in range(PAIRED, len(ITERS))]
UNIT_OF = {i: n for n, u in enumerate(UNITS) for i in u}
QK_COPIES = [[(("h", 4 * j + i), i) for i in range(4)] for j in range(2)] + \
    [[(("q", 2), None)], [(("q", 3), None)]] + \
    [[(("q", NSA_Q[2 * j + i]), 4 + i) for i in range(2)] for j in range(2)] + \
    [[(("q", 6), None)], [(("q", 7), None)]]


ST = 1560
SLOTS = 64
BLOCKS = 48
TABW = BLOCKS + 4
OUTSIDE = 8192
PEEL = 4
WOFF = [0, 512, 896, 1152]
ROOTS = 5


def attention_order():
    out = []
    for k in range(-1, len(UNITS) + 2):
        if k + 1 < len(UNITS):
            out += [("S", i) for i in UNITS[k + 1]]
        if 0 <= k - 1 < len(UNITS):
            out.append(("T", k - 1))
        if 0 <= k - 2:
            out.append(("O", k - 2))
        if k in (2, 4):
            out += [(("cp", "co")[k // 4], c) for c in range(NC)]
    return out


def psum_plan():
    at, n = {}, 0

    def add(key):
        nonlocal n
        at[key] = n
        n += 1

    for l in range(LAYERS):
        for k in range(KD):
            add((l, "ht", k))
        for g, parts in enumerate(PROJ):
            for kind, _, _, what in parts:
                if kind == "t":
                    add((l, "pt", what))
                else:
                    for c in range(NC):
                        add((l, "pn", g, c))
            if g == 4:
                for j in range(2):
                    add((l, "ch", j))
            if g == 5:
                for j in range(2):
                    add((l, "cc", j))
            if g == 6:
                add((l, "ck"))
            if g == 7:
                add((l, "gi"))
                add((l, "gf"))
        for j in range(8):
            add((l, "qk", j))
        for o in range(2):
            add((l, "cs", o))
        add((l, "gc"))
        for kind, i in attention_order():
            add((l, kind, i))
        for h in range(HEADS):
            add((l, "mb", h))
            for s in range(NC):
                add((l, "ms", h, s))
            add((l, "mo", h))
        for lev in range(LEVELS + 1):
            for h in range(HEADS):
                add((l, "ha", lev, h))
        for hp in range(2):
            add((l, "hn", hp))
        for j in range(P // HB):
            for hp in range(2):
                add((l, "hu", hp, j))
        for c in range(NC):
            for o in range(2):
                add((l, "ho", c, o))
        for k in range(KD):
            add((l, "yt", k))
        for c in range(NC):
            for j in range(2):
                add((l, "wo", c, j))
        for k in range(KD):
            add((l, "h2", k))
        add((l, "rt"))
        add((l, "rk"))
        add((l, "rb"))
    return at


class Steps:

    def __init__(self, eng, own):
        self.eng, self.own, self.n = eng, own, {}

    def count(self, ins, sem):
        ins.then_inc(sem, 1)
        self.n[id(sem)] = self.n.get(id(sem), 0) + 1
        return self.n[id(sem)]

    def then(self, ins, sem=None):
        sem = self.own if sem is None else sem
        self.eng.wait_ge(sem, self.count(ins, sem))


def build(nc, d, out):
    ctx = ExitStack()
    with ctx:
        def sb(name, shape, dt=F32):
            return ctx.enter_context(nc.sbuf_tensor(name, shape, dt))

        def sem(name):
            return ctx.enter_context(nc.semaphore(name))

        X = sb("X", [P, NC, DIM])
        hT = sb("hT", [P, KD, SEQ])
        K = sb("K", [P, KW_ALL])
        R = sb("R", [P, RW])
        C = sb("C", [P, CW])
        M = sb("area", [P, 39008])
        st = sb("stats", [P, ST])

        def area(a, shape):
            n = int(np.prod(shape))
            v = M[:, a:a + n]
            if len(shape) == 2:
                v = v.rearrange("p (a b) -> p a b", a=shape[0])
            if len(shape) == 3:
                v = v.rearrange("p (a b c) -> p a b c", a=shape[0], b=shape[1])
            return v

        tok = area(0, [NC, DIM])
        Pn = area(4096, [NC, PW])
        wring = area(13392, [2, KD, 512])
        bias = area(21584, [8, 512])
        QKT = area(25680, [8, SEQ])
        mraw = area(29776, [4, SEQ + 3])
        mqk = area(31836, [4, SEQ])
        hqf = area(33884, [4, SEQ])
        probs = [area(13392 + 4096 * j, [4, 512]) for j in range(2)]
        negSs = [area(13392 + 4096 * j + 2048, [4, 512]) for j in range(2)]
        probT = area(37980, [2, 512])
        w1 = area(31836, [2, 16, HD])
        kcT = area(35932, [2, SEQ])
        Sc = area(36956, [16, NCMP])
        w2 = area(37984, [2, HD])
        PcT = area(29776, [16, P])
        gA, gMt, gM = (area(a, [SEQ])[0:HEADS, :] for a in (35932, 36444, 37460))
        WT = area(25680, [2, 1280])
        D = area(28240, [2, SEQ])
        E = area(35932, [2, SEQ])
        Vm = area(21584, [NC, HEADS, HD + 1])
        b = area(25680, [2, SEQ])
        kk = area(26704, [2, SEQ])
        Xe = area(27728, [2, SEQ])
        qt = area(28752, [2, SEQ])
        kt = area(29776, [2, SEQ])
        kn = area(30800, [2, NC, P])
        A = area(31836, [HEADS, SEQ])
        St = area(21584, [2, 16, P])
        ysq = area(35932, [NC, 3 * GW])
        hsq = area(25680, [NC, GW])
        wgu = area(0, [2, KD, 2 * FF])
        wdn = area(8192, [2, 2, DIM])
        h2n = area(13392, [NC, DIM])
        gi = area(21584, [TABW]).bitcast(I32)
        si = area(21636, [TABW]).bitcast(I32)
        ebt = area(21688, [TABW])[0:1, :].bitcast(I32)
        hots = area(21744, [NC, 2 * EXPERTS])
        hots8 = area(21744, [2 * NC, EXPERTS])
        rk = area(22000, [NC + 1, EXPERTS])
        nblk = area(22160, [EXPERTS])
        bend = area(22192, [EXPERTS])
        bst = area(22224, [EXPERTS])
        selsum = area(22256, [NC, EXPERTS])
        oslot = area(22384, [2 * NC, P])
        oblk = area(23408, [2 * NC, 3, TABW])
        tab = area(24656, [3, TABW])
        rtmp = area(25680, [BLOCKS * EXPERTS])
        yc = area(25680, [NC, 2 * DIM])
        wr = area(33872, [KD, 36])
        rt = area(34160, [NC, 36])
        hg = area(34304, [2, 512])
        hgT = area(35328, [2, 4, P])
        au = area(36352, [2, 512])
        ysb = area(37376, [2, 512])
        sil = area(38400, [2, P])
        actT = area(38656, [2, P])

        ident = K[:, K_ID:K_ID + P]
        caus = K[:, K_CAUS:K_CAUS + P]

        index = sb("index", [P, 2, 2], I32)

        psum = [ctx.enter_context(nc.psum_tensor(f"bank{i}", [P, 512], F32)) for i in range(8)]
        at = psum_plan()

        at_st = [0]

        def small(*shape):
            n = int(np.prod(shape))
            v = st[:, at_st[0]:at_st[0] + n]
            at_st[0] += n
            if len(shape) == 2:
                v = v.rearrange("p (a b) -> p a b", a=shape[0])
            if len(shape) == 3:
                v = v.rearrange("p (a b c) -> p a b c", a=shape[0], b=shape[1])
            return v

        Hd, posb, Kc, KcT, Vc = small(2, NCMP), small(2), small(2, HD), small(NCMP), small(HD)
        nmax, psumcol, fac = small(len(ITERS)), small(len(ITERS)), small(len(ITERS))
        ms, rs = small(88), small(88)
        lam4, lam = small(2), small(1)
        cmx, cfac = small(16), small(16)
        gcol = small(2, NC, HEADS)
        mden = small(NC)
        lbx, lbs, lbc = small(2, 2), small(2, 2), small(4, 2)
        dec = small(2, NB)

        nopcell, tmp = small(1), sb("scratch", [P, 2 * HD])
        rbest, rsecond, rmark, gprob, rx1 = (small(NC) for _ in range(5))
        ghot, rx0 = small(NC, GROUPS), small(NC, GROUPS)
        hot1, hot2, l8 = (small(NC, PER_GROUP) for _ in range(3))
        rx = (rx0, rx1)
        group_logits = small(NC, GROUPS, PER_GROUP)
        rank, blk, quot = (small(2 * NC) for _ in range(3))
        ebf = small(TABW)
        oblk8 = small(2 * NC, EXPERTS)
        assert at_st[0] <= ST

        names = """h2_ready h2_out sel_ready ob_ready route_ready x_new const_in par_in w1_in bias_in wr_in out_done
            act_own dve_own ss mean root h_ready qkn_ready ck_n cs_x cs_e cs_p mixed gsig exp_done
            lam_d lam_e conv_m silu_m gate_a gate_b gate_r en_d vm_ready md me w_ready
            lb_a lb_b hsig hF hln hx he hqk hst hq_in sq ysq y_ready rt_x rt_e""".split()
        s = {n: sem(n) for n in names}
        full = [sem(f"bank_full{i}") for i in range(8)]
        free = [sem(f"bank_free{i}") for i in range(8)]
        x_in = [sem(f"x_in{c}") for c in range(NC)]
        yc_in = [sem(f"yc_in{c}") for c in range(NC)]
        w_in_sem = [sem(f"w_in{i}") for i in range(2)]
        moe = [{n: sem(f"{n}_{l}") for n in """tr_full tr_copied au_full au_copied fold_full silu_done act_ready
            y_full y_copied gather0 gather1 scatter0 scatter1 gu_in0 gu_in1 dn_in0 dn_in1 gather_index scatter_index""".split()}
               for l in range(LAYERS)]
        h_rows = nc.dram_tensor("h_rows", (2 * SEQ, 512), F32, kind="Internal").ap()
        y_rows = nc.dram_tensor("y_rows", (4 * SEQ, 512), F32, kind="Internal").ap()

        def take(eng, key):
            n = at[key]
            if n >= 8:
                eng.wait_ge(free[n % 8], n // 8)
            return psum[n % 8]

        def filled(ins, key):
            ins.then_inc(full[at[key] % 8], 1)

        def ready(eng, key):
            n = at[key]
            eng.wait_ge(full[n % 8], n // 8 + 1)
            return psum[n % 8]

        def release(ins, key):
            ins.then_inc(free[at[key] % 8], 1)

        def copied(eng, key):
            n = at[key]
            eng.wait_ge(free[n % 8], n // 8 + 1)

        def x_ready(eng, l, c=NC - 1):
            if l:
                eng.wait_ge(s["x_new"], NC * (l - 1) + c + 1)
            else:
                eng.wait_ge(x_in[c], 16)

        def pairs(eng, l):
            eng.wait_ge(s["route_ready"], l + 1)
            return eng.value_load(ebt[0:1, BLOCKS:BLOCKS + 1], min_val=7, max_val=BLOCKS // 2 - 1)

        def gathered(e, u):
            return 16 * (e // 2 + 1) if isinstance(e, int) else e * 8 + (16 - 8 * u)

        def blocks(eng, last_pair, step):
            for e in range(PEEL):
                step(e, e % 2)
            with eng.Fori(PEEL // 2, last_pair + 1) as turn:
                for u in range(2):
                    step(turn * 2 + u, u)

        def scratch(l):
            j = (l * LOADS + len(W_IN) - 1) % 2
            return probs[j], negSs[j]

        def qk_tile(where):
            return (hT if where[0] == "h" else QKT)[:, where[1], :]

        PTILES = []
        for g, parts in enumerate(PROJ):
            for kind, a, n, what in parts:
                for c in range(NC if kind == "n" else 1):
                    PTILES.append((g, kind, a, n, what, c, what == "kv" or len(PTILES) % 2 == 1))

        def ptile(l, g, kind, what, c):
            return (l, "pn", g, c) if kind == "n" else (l, "pt", what)

        LAST_OF = {g: ptile(0, *[(t[0], t[1], t[4], t[5]) for t in PTILES if t[0] == g][-1])[1:]
                   for g in range(len(PROJ))}

        def projected(eng, l, groups):
            for g in groups:
                for t in [t for t in PTILES if t[0] == g][-4:]:
                    copied(eng, ptile(l, g, t[1], t[4], t[5]))

        block = ctx.enter_context(nc.Block())

        @block.sync
        def _(sp):
            for c in range(NC):
                sp.dma_start(X[:, c, :], d["x"][P * c:P * (c + 1), :]).then_inc(x_in[c], 16)
            sp.dma_start(K[:, :], d["constants"]).then_inc(s["const_in"], 16)

            def load_in(l, n):
                j = l * LOADS + n
                if n >= 2:
                    ready(sp, (l,) + LAST_OF[n - 2])
                if n < len(W_IN):
                    a, w = W_IN[n]
                    src = d["w_in"][l, :, a:a + w].rearrange("(k p) n -> p k n", p=P)
                else:
                    w = 512
                    a = 512 * (n - len(W_IN))
                    if n == LOADS - 1:
                        ready(sp, (l, "O", len(UNITS) - 1))
                    src = d["w_out"][l, :, a:a + w].rearrange("(k p) n -> p k n", p=P)
                sp.dma_start(wring[:, j % 2, :, 0:w], src).then_inc(w_in_sem[j % 2], 16)

            def load_experts(l):
                m = moe[l]
                last_pair = pairs(sp, l)

                def expert(e):
                    return bass.ds(sp.value_load(ebt[0:1, bass.ds(e, 1)], min_val=0, max_val=EXPERTS - 1), 1)

                def down_weights(e, u):
                    x = expert(e)
                    if not isinstance(e, int) or e >= 2:
                        sp.wait_ge(m["y_full"], e - 1)
                    sp.dma_start(wdn[:, u, :, :], d["moe_w_down"][l, x].rearrange("e (k p) f -> p (e k) f", p=P)) \
                        .then_inc(m[f"dn_in{u}"], 16)

                def step(e, u):
                    x = expert(e)
                    if not isinstance(e, int) or e >= 2:
                        sp.wait_ge(m["au_full"], e - 1)
                    for i, name in enumerate(("moe_w_gate", "moe_w_up")):
                        sp.dma_start(wgu[:, u, :, FF * i:FF * (i + 1)],
                                     d[name][l, x].rearrange("e (k p) f -> p (e k) f", p=P)) \
                            .then_inc(m[f"gu_in{u}"], 16)
                    if not isinstance(e, int) or e >= 1:
                        down_weights(e - 1, 1 - u)

                blocks(sp, last_pair, step)
                down_weights(last_pair * 2 + 1, 1)
                if l + 1 < LAYERS:
                    for i in range(2):
                        load_in(l + 1, i)
                for u in range(2):
                    sp.wait_ge(m[f"scatter{u}"], last_pair * 16 + 16)
                for c in range(NC):
                    sp.dma_start(yc[:, c, :], y_rows[4 * P * c:4 * P * (c + 1), :]
                                 .rearrange("(p j) n -> p (j n)", j=4)).then_inc(yc_in[c], 16)

            for l in range(LAYERS):
                if l:
                    x_ready(sp, l)
                sp.dma_start(R[:, :], d["rows"][l:l + 1, :].to_broadcast([P, RW])).then_inc(s["par_in"], 16)
                sp.dma_start(C[:, :], d["columns"][l]).then_inc(s["par_in"], 16)
                for n in range(LOADS):
                    if l == 0 or n >= 2:
                        load_in(l, n)
                    if n == 1:
                        for i in range(2):
                            sp.dma_start(w1[:, i], d["nsa_cmp_w1"][l, i].rearrange("(j p) m -> p j m", p=P)) \
                                .then_inc(s["w1_in"], 16)
                        sp.dma_start(w2[0:HD, :, :], d["nsa_cmp_w2"][l].rearrange("j k m -> k j m")) \
                            .then_inc(s["w1_in"], 16)
                        sp.dma_start(bias[:, :, :], d["alibi"].rearrange("p (n m) -> p n m", n=8)) \
                            .then_inc(s["bias_in"], 16)
                copied(sp, (l, "wo", NC - 1, 1))
                sp.dma_start(wr[:, :, 0:GROUPS], d["moe_w_group"][l].rearrange("(k p) n -> p k n", p=P)) \
                    .then_inc(s["wr_in"], 16)
                sp.dma_start(wr[:, :, GROUPS:], d["moe_w_expert"][l].rearrange("(k p) n -> p k n", p=P)) \
                    .then_inc(s["wr_in"], 16)
                sp.wait_ge(s["h2_ready"], l + 1)
                sp.dma_start(h_rows.rearrange("(c p t) n -> p c (t n)", p=P, t=2), h2n[:, :, :]) \
                    .then_inc(s["h2_out"], 16)
                load_experts(l)
            for c in range(NC):
                x_ready(sp, LAYERS, c)
                sp.dma_start(out[P * c:P * (c + 1), :], X[:, c, :]).then_inc(s["out_done"], 16)
            sp.wait_ge(s["out_done"], 16 * NC)

        @block.tensor
        def _(pe):
            def to_channels(l, name, src):
                for k in range(KD):
                    t = take(pe, (l, name, k))
                    for c in range(NC):
                        last = pe.transpose(t[:, c * P:(c + 1) * P], src[:, c, k * P:(k + 1) * P], ident)
                    filled(last, (l, name, k))

            def loaded(j):
                pe.wait_ge(w_in_sem[j % 2], 16 * (j // 2 + 1))

            def project(l, groups):
                for g, kind, a, n, what, c, _ in PTILES:
                    if g not in groups:
                        continue
                    j = l * LOADS + g
                    if c == 0 and a == PROJ[g][0][1]:
                        loaded(j)
                    w = wring[:, j % 2]
                    key = ptile(l, g, kind, what, c)
                    t = take(pe, key)
                    for k in range(KD):
                        if kind == "n":
                            last = pe.matmul(t[:, 0:n], hT[:, k, c * P:(c + 1) * P], w[:, k, a:a + n],
                                             start=(k == 0), stop=(k == KD - 1))
                        else:
                            last = pe.matmul(t[:, :], w[:, k, a:a + n], hT[:, k, :],
                                             start=(k == 0), stop=(k == KD - 1))
                    filled(last, key)

            def compress_hidden(l):
                pe.wait_ge(s["w1_in"], 48 * (l + 1))
                copied(pe, (l, "pt", "kv"))
                for j in range(2):
                    t = take(pe, (l, "ch", j))
                    for i in range(16):
                        pe.matmul(t[0:HD, 0:NCMP], w1[:, j, i, :],
                                  kcT[:, j, 2 * i:2 * i + CMP_STRIDE * (NCMP - 1) + 1:CMP_STRIDE],
                                  start=(i == 0), stop=(i == 15))
                    for i in range(16):
                        last = pe.matmul(t[0:HD, NCMP:NCMP + 1], w1[:, j, i, :],
                                         C[:, C_POS + 16 * j + i:C_POS + 16 * j + i + 1],
                                         start=(i == 0), stop=(i == 15))
                    filled(last, (l, "ch", j))

            def compress_out(l):
                for j in range(2):
                    t = take(pe, (l, "cc", j))
                    copied(pe, (l, "ch", j))
                    filled(pe.matmul(t[0:NCMP, 0:HD], Hd[0:HD, j, :], w2[0:HD, j, :], start=True, stop=True),
                           (l, "cc", j))

            def compress_keys(l):
                t = take(pe, (l, "ck"))
                pe.wait_ge(s["ck_n"], l + 1)
                filled(pe.transpose(t[:, 0:NCMP], Kc[0:NCMP, :, :].rearrange("p a b -> p (a b)"),
                                    ident[0:NCMP, 0:NCMP]), (l, "ck"))

            def compressed_scores(l):
                copied(pe, (l, "ck"))
                for o in range(2):
                    t = take(pe, (l, "cs", o))
                    for c in range(NC):
                        for i in range(2):
                            n = (2 * c + i) * NCMP
                            last = pe.matmul(t[:, n:n + NCMP], QKT[:, NSA_Q[2 * i + o], c * P:(c + 1) * P],
                                             KcT[:, :], start=True, stop=True)
                    filled(last, (l, "cs", o))

            def attend(l):
                prob, _ = scratch(l)
                for kind, i in attention_order():
                    if kind == "cp" and i == 0:
                        pe.wait_ge(s["cs_p"], l + 1)
                    t = take(pe, (l, kind, i))
                    if kind == "S":
                        m, c = ITERS[i]
                        q, k = MAPS[m][:2]
                        last = pe.matmul(t[:, 0:(c + 1) * P], qk_tile(q)[:, c * P:(c + 1) * P],
                                         QKT[:, k, 0:(c + 1) * P], start=True, stop=True)
                    elif kind == "T":
                        u = UNITS[i]
                        if len(u) == 2:
                            pe.wait_ge(s["mixed"], PAIRED // 2 * l + i + 1)
                        else:
                            pe.wait_ge(s["exp_done"], len(ITERS) * l + u[0] + 1)
                        for j in range(ITERS[u[0]][1] + 1):
                            last = pe.transpose(t[:, j * P:(j + 1) * P], prob[:, u[0] % 4, j * P:(j + 1) * P], ident)
                    elif kind == "O":
                        m, c = ITERS[UNITS[i][0]]
                        v = MAPS[m][2]
                        copied(pe, (l, "T", i))
                        for j in range(c + 1):
                            last = pe.matmul(t[:, 0:HD], probT[:, i % 2, j * P:(j + 1) * P],
                                             Pn[:, j, v:v + HD], start=(j == 0), stop=(j == c))
                    elif kind == "cp":
                        for h in range(HEADS):
                            last = pe.transpose(t[0:NCMP, h * P:(h + 1) * P], Sc[:, i * HEADS + h, :], ident)
                    else:
                        copied(pe, (l, "cp", i))
                        for h in range(HEADS):
                            last = pe.matmul(t[:, h * HD:(h + 1) * HD], PcT[0:NCMP, i * HEADS + h, :], Vc[0:NCMP, :],
                                             start=True, stop=True)
                    filled(last, (l, kind, i))

            def gate_rows(l):
                for name, a in (("gi", BI), ("gf", BF)):
                    t = take(pe, (l, name))
                    for c in range(NC):
                        last = pe.transpose(t[0:HEADS, c * P:(c + 1) * P], Pn[:, c, a:a + HEADS], ident)
                    filled(last, (l, name))

            def gate_columns(l):
                t = take(pe, (l, "gc"))
                pe.wait_ge(s["gate_r"], l + 1)
                for n, row in enumerate((gA, gMt)):
                    for c in range(NC):
                        last = pe.transpose(t[:, 16 * n + HEADS * c:16 * n + HEADS * c + HEADS],
                                            row[:, c * P:(c + 1) * P], ident[0:HEADS, 0:HEADS])
                filled(last, (l, "gc"))

            def mlstm(l):
                pe.wait_ge(s["silu_m"], l + 1)
                pe.wait_ge(s["vm_ready"], l + 1)
                for h in range(HEADS):
                    o = 64 * (h % 2)
                    t = take(pe, (l, "mb", h))
                    filled(pe.matmul(t[:, :], ident[0:HEADS, h:h + 1].to_broadcast([HEADS, P]), gM[:, :],
                                     start=True, stop=True), (l, "mb", h))
                    for c in range(NC):
                        t = take(pe, (l, "ms", h, c))
                        filled(pe.matmul(t[:, 0:SEQ - c * P], mqk[o:o + HD, 2 + h // 2, c * P:(c + 1) * P],
                                         mqk[o:o + HD, h // 2, c * P:SEQ], start=True, stop=True), (l, "ms", h, c))
                    t = take(pe, (l, "mo", h))
                    pe.wait_ge(s["w_ready"], NC * (HEADS * l + h + 1))
                    for c in range(NC):
                        for j in range(c + 1):
                            a = WOFF[j] + (c - j) * P
                            last = pe.matmul(t[:, c * 65:c * 65 + 65], WT[:, h % 2, a:a + P], Vm[:, j, h, :],
                                             start=(j == 0), stop=(j == c))
                    filled(last, (l, "mo", h))

            def hgrn(l):
                for lev in range(LEVELS + 1):
                    qs, ks = (hqf, kk) if lev == 0 else (qt, kt)
                    pe.wait_ge(s["hqk"], (LEVELS + 2) * l + lev + 1)
                    for h in range(HEADS):
                        o = 64 * (h % 2)
                        t = take(pe, (l, "ha", lev, h))
                        for c in range(NC):
                            last = pe.matmul(t[:, c * P:(c + 1) * P], ks[o:o + HD, h // 2, c * P:(c + 1) * P],
                                             qs[o:o + HD, h // 2, c * P:(c + 1) * P], start=True, stop=True)
                        filled(last, (l, "ha", lev, h))
                pe.wait_ge(s["hqk"], (LEVELS + 2) * (l + 1))
                for hp in range(2):
                    t = take(pe, (l, "hn", hp))
                    for c in range(NC):
                        last = pe.transpose(t[:, c * P:(c + 1) * P], kt[:, hp, c * P:(c + 1) * P], ident)
                    filled(last, (l, "hn", hp))
                for hp in range(2):
                    copied(pe, (l, "hn", hp))
                for j in range(P // HB):
                    r = slice(j * HB, (j + 1) * HB)
                    for hp in range(2):
                        t = take(pe, (l, "hu", hp, j))
                        for c in range(NC):
                            last = pe.matmul(t[:, c * P:(c + 1) * P], kn[r, hp, c, :],
                                             Pn[r, c, CI + hp * P:CI + (hp + 1) * P], start=True, stop=True,
                                             tile_position=(j * HB, 0))
                        filled(last, (l, "hu", hp, j))
                pe.wait_ge(s["hq_in"], l + 1)
                pe.wait_ge(s["hst"], l + 1)
                for c in range(NC):
                    for o in range(2):
                        t = take(pe, (l, "ho", c, o))
                        for hp in range(2):
                            h = 2 * hp + o
                            last = pe.matmul(t[:, hp * HD:(hp + 1) * HD], A[:, h, c * P:(c + 1) * P],
                                             Pn[:, c, CI + h * HD:CI + (h + 1) * HD], start=True, stop=False)
                            for j in range(P // HB):
                                i = c * (P // HB) + j
                                last = pe.matmul(t[j * HB:(j + 1) * HB, hp * HD:(hp + 1) * HD],
                                                 qt[64 * o:64 * o + HD, hp, i * HB:(i + 1) * HB],
                                                 St[64 * o:64 * o + HD, hp, i, 64 * o:64 * o + HD],
                                                 start=False, stop=True, tile_position=(64 * o, j * HB))
                        filled(last, (l, "ho", c, o))

            def route(l):
                t = take(pe, (l, "rk"))
                pe.wait_ge(s["sel_ready"], l + 1)
                one = K[:, K_IOTA + PER_GROUP - 1:K_IOTA + PER_GROUP].to_broadcast([P, P])
                for c in range(NC + 1):
                    before = min(c, NC)
                    for i in range(before):
                        last = pe.matmul(t[:, EXPERTS * c:EXPERTS * (c + 1)], one, selsum[:, i, :],
                                         start=(i == 0), stop=(c == NC and i == NC - 1))
                    if c < NC:
                        last = pe.matmul(t[:, EXPERTS * c:EXPERTS * (c + 1)], K[:, K_UP:K_UP + P], selsum[:, c, :],
                                         start=(c == 0), stop=True)
                filled(last, (l, "rk"))
                t = take(pe, (l, "rb"))
                pe.wait_ge(s["ob_ready"], l + 1)
                for i in range(2 * NC):
                    last = pe.matmul(t[:, 0:3 * TABW], oslot[:, i, :],
                                     oblk[:, i, :, :].rearrange("p a b -> p (a b)"),
                                     start=(i == 0), stop=(i == 2 * NC - 1))
                filled(last, (l, "rb"))

            def experts(l):
                m = moe[l]
                last_pair = pairs(pe, l)
                for i in range(8):
                    last = max(v for v in at.values() if v % 8 == i and v <= at[(l, "rb")])
                    pe.wait_ge(free[i], last // 8 + 1)

                def turn_tokens(e, u):
                    pe.wait_ge(m[f"gather{u}"], gathered(e, u))
                    if not isinstance(e, int) or e >= 2:
                        pe.wait_ge(m["tr_copied"], e - 1)
                    for k in range(4):
                        last = pe.transpose(psum[u][:, k * P:(k + 1) * P], hg[:, u, k * P:(k + 1) * P], ident)
                    last.then_inc(m["tr_full"], 1)

                def down(e, u):
                    static = isinstance(e, int)
                    pe.wait_ge(m["act_ready"], e + 1)
                    pe.wait_ge(m[f"dn_in{u}"], gathered(e, u))
                    if not static or e >= 2:
                        pe.wait_ge(m["y_copied"], e - 1)
                    for k in range(2):
                        for j in range(2):
                            last = pe.matmul(psum[6 + u][SLOTS * j:SLOTS * (j + 1), :],
                                             actT[:, u, SLOTS * k:SLOTS * (k + 1)],
                                             wdn[:, u, k, 512 * j:512 * (j + 1)], start=(k == 0), stop=(k == 1),
                                             tile_position=(0, SLOTS * j))
                    last.then_inc(m["y_full"], 1)

                def step(e, u):
                    static = isinstance(e, int)
                    pe.wait_ge(m["tr_copied"], e + 1)
                    pe.wait_ge(m[f"gu_in{u}"], gathered(e, u) * 2)
                    if not static or e >= 2:
                        pe.wait_ge(m["au_copied"], e - 1)
                    for k in range(4):
                        for j in range(2):
                            last = pe.matmul(psum[2 + u][SLOTS * j:SLOTS * (j + 1), :],
                                             hgT[:, u, k, SLOTS * j:SLOTS * (j + 1)], wgu[:, u, 4 * j + k, :],
                                             start=(k == 0), stop=(k == 3), tile_position=(0, SLOTS * j))
                    last.then_inc(m["au_full"], 1)
                    turn_tokens(e + 1, 1 - u)
                    if not static or e >= 1:
                        down(e - 1, 1 - u)
                    pe.wait_ge(m["au_copied"], e + 1)
                    if not static or e >= 2:
                        pe.wait_ge(m["act_ready"], e - 1)
                    for k in range(4):
                        last = pe.matmul(psum[4 + u][:, SLOTS * k:SLOTS * (k + 1)], au[:, u, k * P:(k + 1) * P],
                                         K[:, K_FOLD:K_FOLD + SLOTS], start=True, stop=True)
                    last.then_inc(m["fold_full"], 1)

                turn_tokens(0, 0)
                blocks(pe, last_pair, step)
                pe.wait_ge(m["gather1"], last_pair * 16 + 32)
                pe.wait_ge(m["gather_index"], last_pair * 2 + 5)
                down(last_pair * 2 + 1, 1)

            pe.wait_ge(s["const_in"], 16)
            for l in range(LAYERS):
                pe.wait_ge(s["h_ready"], l + 1)
                to_channels(l, "ht", tok)
                for k in range(KD):
                    copied(pe, (l, "ht", k))
                project(l, (0, 1, 2, 3, 4))
                compress_hidden(l)
                project(l, (5,))
                compress_out(l)
                project(l, (6,))
                compress_keys(l)
                project(l, (7,))
                projected(pe, l, (6, 7))
                gate_rows(l)
                project(l, (8,))
                pe.wait_ge(s["qkn_ready"], l + 1)
                to_channels(l, "qk", tok)
                for k in range(KD):
                    copied(pe, (l, "qk", k))
                compressed_scores(l)
                gate_columns(l)
                projected(pe, l, (2, 3))
                copied(pe, (l, "cc", 1))
                attend(l)
                projected(pe, l, (6, 7, 8))
                mlstm(l)
                hgrn(l)
                pe.wait_ge(s["y_ready"], l + 1)
                to_channels(l, "yt", tok)
                for k in range(KD):
                    copied(pe, (l, "yt", k))
                for j in range(2):
                    loaded(l * LOADS + len(W_IN) + j)
                for c in range(NC):
                    for j in range(2):
                        w = wring[:, (l * LOADS + len(W_IN) + j) % 2]
                        t = take(pe, (l, "wo", c, j))
                        for k in range(KD):
                            last = pe.matmul(t[:, :], hT[:, k, c * P:(c + 1) * P], w[:, k, :],
                                             start=(k == 0), stop=(k == KD - 1))
                        filled(last, (l, "wo", c, j))
                pe.wait_ge(s["h2_ready"], l + 1)
                to_channels(l, "h2", h2n)
                for k in range(KD):
                    copied(pe, (l, "h2", k))
                pe.wait_ge(s["wr_in"], 32 * (l + 1))
                t = take(pe, (l, "rt"))
                for c in range(NC):
                    for k in range(KD):
                        last = pe.matmul(t[:, 36 * c:36 * c + 36], hT[:, k, c * P:(c + 1) * P], wr[:, k, :],
                                         start=(k == 0), stop=(k == KD - 1))
                filled(last, (l, "rt"))
                route(l)
                experts(l)

        @block.gpsimd
        def _(pool):
            last_h_row, last_y_row = pool.to_reg(2 * SEQ - 1), pool.to_reg(4 * SEQ - 1)
            for l in range(LAYERS):
                m = moe[l]
                last_pair = pairs(pool, l)
                pool.wait_ge(s["h2_out"], 16 * (l + 1))

                def next_column(table, i, e, u, done, filled):
                    if not isinstance(e, int) or e >= 1:
                        pool.wait_ge(m[f"{done}{1 - u}"], gathered(e - 1, 1 - u))
                    pool.wait_ge(m[filled], e + 1)
                    pool.tensor_copy(index[:, i, 1 - u:2 - u], table[:, bass.ds(e + 1, 1)]).then_inc(m[filled], 1)

                def gather(e, u):
                    if not isinstance(e, int) or e >= 2:
                        pool.wait_ge(m["tr_full"], e - 1)
                    next_column(gi, 0, e, u, "gather", "gather_index")
                    pool.indirect_dma_start(
                        out=hg[:, u, :], out_offset=None, in_=h_rows,
                        in_offset=bass.IndirectOffsetOnAxis(ap=index[:, 0, u:u + 1], axis=0),
                        bounds_check=last_h_row, oob_is_err=False).then_inc(m[f"gather{u}"], 16)

                def scatter(e, u):
                    pool.wait_ge(m["y_copied"], e + 1)
                    next_column(si, 1, e, u, "scatter", "scatter_index")
                    pool.indirect_dma_start(
                        out=y_rows, out_offset=bass.IndirectOffsetOnAxis(ap=index[:, 1, u:u + 1], axis=0),
                        in_=ysb[:, u, :], in_offset=None,
                        bounds_check=last_y_row, oob_is_err=False).then_inc(m[f"scatter{u}"], 16)

                def step(e, u):
                    gather(e + 2, u)
                    if not isinstance(e, int) or e >= 2:
                        scatter(e - 2, u)

                for i, table in enumerate((gi, si)):
                    pool.tensor_copy(index[:, i, 0:1], table[:, 0:1]) \
                        .then_inc(m[("gather_index", "scatter_index")[i]], 1)
                for e in range(2):
                    gather(e, e)
                blocks(pool, last_pair, step)
                for u in range(2):
                    scatter(last_pair * 2 + u, u)

        @block.scalar
        def _(act):
            sc = Steps(act, s["act_own"])

            def squares(l, first):
                for c in range(NC):
                    if first:
                        x_ready(act, l, c)
                    else:
                        for j in range(2):
                            copied(act, (l, "wo", c, j))
                    act.activation(tok[:, c, :], X[:, c, :], ACT.Square, accum_out=ms[:, c:c + 1]).then_inc(s["ss"], 1)

            def root(l, u, a):
                act.wait_ge(s["mean"], ROOTS * l + u + 1)
                act.activation(a, a, ACT.Sqrt).then_inc(s["root"], 1)

            def evens(l, name, col):
                for k in range(0, KD, 2):
                    t = ready(act, (l, name, k))
                    if name == "qk":
                        for where, mask in QK_COPIES[k]:
                            scale = 1.0 if mask is None else K[:, K_MASK + mask:K_MASK + mask + 1]
                            ins = act.activation(qk_tile(where), t[:, :], ACT.Copy, scale=scale)
                    elif col is None:
                        ins = act.activation(hT[:, k, :], t[:, :], ACT.Copy)
                    else:
                        ins = act.activation(hT[:, k, :], t[:, :], ACT.Copy, scale=C[:, col + k:col + k + 1])
                    release(ins, (l, name, k))

            def copies(l, groups):
                for g, kind, a, n, what, c, vector in PTILES:
                    if vector or g not in groups:
                        continue
                    key = ptile(l, g, kind, what, c)
                    t = ready(act, key)
                    if kind == "n":
                        ins = act.activation(Pn[:, c, what:what + n], t[:, 0:n], ACT.Copy)
                    elif what[0] == "m":
                        ins = act.activation(mraw[:, int(what[1]), 3:], t[:, :], ACT.Copy)
                    else:
                        ins = act.activation(hqf[:, int(what[1]), :], t[:, :], ACT.Copy)
                    release(ins, key)

            def gates(l, a, n):
                act.activation(Pn[:, :, a:a + n], Pn[:, :, a:a + n], ACT.Sigmoid).then_inc(s["gsig"], 1)

            def experts(l):
                m = moe[l]
                last_pair = pairs(act, l)

                def outputs(e, u):
                    act.wait_ge(m["y_full"], e + 1)
                    if not isinstance(e, int) or e >= 2:
                        act.wait_ge(m[f"scatter{u}"], gathered(e - 2, u))
                    act.activation(ysb[:, u, :], psum[6 + u][:, :], ACT.Copy).then_inc(m["y_copied"], 1)

                def step(e, u):
                    static = isinstance(e, int)
                    act.wait_ge(m["au_full"], e + 1)
                    if not static or e >= 2:
                        act.wait_ge(m["fold_full"], e - 1)
                    act.activation(au[:, u, :], psum[2 + u][:, :], ACT.Copy).then_inc(m["au_copied"], 1)
                    if not static or e >= 1:
                        outputs(e - 1, 1 - u)
                    act.wait_ge(m["fold_full"], e + 1)
                    if not static or e >= 2:
                        act.wait_ge(m["act_ready"], e - 1)
                    act.activation(sil[:, u, :], psum[4 + u][:, 0:P], ACT.Silu).then_inc(m["silu_done"], 1)

                blocks(act, last_pair, step)
                outputs(last_pair * 2 + 1, 1)

            act.wait_ge(s["const_in"], 16)
            for l in range(LAYERS):
                squares(l, True)
                root(l, 0, ms[:, 0:NC])
                act.wait_ge(s["par_in"], 32 * (l + 1))
                evens(l, "ht", C_NM)
                copies(l, (0, 1, 2, 3))
                act.wait_ge(s["lam_d"], l + 1)
                act.activation(lam4, lam4, ACT.Exp).then_inc(s["lam_e"], 1)
                projected(act, l, (2,))
                gates(l, DG, 12)
                root(l, 1, ms[:, 0:88])
                copies(l, (4,))
                for j in range(2):
                    t = ready(act, (l, "ch", j))
                    sc.then(act.activation(posb[0:HD, j:j + 1], t[0:HD, NCMP:NCMP + 1], ACT.Copy))
                    release(act.activation(Hd[0:HD, j, :], t[0:HD, 0:NCMP], ACT.Gelu_apprx_tanh,
                                           bias=posb[0:HD, j:j + 1]), (l, "ch", j))
                copies(l, (5,))
                root(l, 2, ms[0:NCMP, 0:1])
                copies(l, (6, 7))
                act.wait_ge(s["gate_a"], l + 1)
                sc.then(act.activation(gMt[:, :], gMt[:, :], ACT.Exp))
                act.activation(gMt[:, :], gMt[:, :], ACT.Ln, bias=1.0).then_inc(s["gate_b"], 1)
                act.wait_ge(s["lb_a"], l + 1)
                act.activation(lbx[:, :, :], lbx[:, :, :], ACT.Exp).then_inc(s["lb_b"], 1)
                act.wait_ge(s["conv_m"], l + 1)
                act.activation(mqk[:, :, :], mqk[:, :, :], ACT.Silu).then_inc(s["silu_m"], 1)
                projected(act, l, (5,))
                hq = hqf[:, 0:2, :]
                act.activation(hq, hq, ACT.Silu).then_inc(s["hsig"], 1)
                copies(l, (8,))
                evens(l, "qk", None)
                projected(act, l, (7, 8))
                gates(l, BO, GW)
                gates(l, CG, GW)
                act.wait_ge(s["cs_x"], l + 1)
                act.activation(Sc[:, :, :], Sc[:, :, :], ACT.Exp).then_inc(s["cs_e"], 1)
                prob, negS = scratch(l)
                for k in range(len(UNITS) + 1):
                    for i in UNITS[k] if k < len(UNITS) else ():
                        n = (ITERS[i][1] + 1) * P
                        copied(act, (l, "S", i))
                        if i >= 4:
                            ready(act, (l, "T", UNIT_OF[i - 4]))
                        act.activation(prob[:, i % 4, 0:n], negS[:, i % 4, 0:n], ACT.Exp, scale=-1.0,
                                       bias=nmax[:, i:i + 1], accum_out=psumcol[:, i:i + 1]).then_inc(s["exp_done"], 1)
                    if k:
                        n = (ITERS[UNITS[k - 1][0]][1] + 1) * P
                        t = ready(act, (l, "T", k - 1))
                        if k >= 3:
                            ready(act, (l, "O", k - 3))
                        release(act.activation(probT[:, (k - 1) % 2, 0:n], t[:, 0:n], ACT.Copy), (l, "T", k - 1))
                copied(act, (l, "gc"))
                act.activation(gcol[:, 1], gcol[:, 1], ACT.Exp, scale=-1.0).then_inc(s["en_d"], 1)
                for h in range(HEADS):
                    for c in range(NC):
                        i = NC * h + c
                        n = SEQ - c * P
                        if c < NC - 1:
                            act.wait_ge(s["md"], 3 * (HEADS * l + h) + c + 1)
                        else:
                            copied(act, (l, "mb", h))
                        if i >= 2:
                            act.wait_ge(s["w_ready"], NC * HEADS * l + i - 1)
                        act.activation(E[:, c % 2, 0:n], D[:, c % 2, 0:n], ACT.Exp, scale=-1.0).then_inc(s["me"], 1)
                ready(act, (l, "mo", HEADS - 1))
                act.activation(Xe[:, :, :], hqf[:, 2:4, :], ACT.Sigmoid).then_inc(s["hsig"], 1)
                act.activation(kk[:, :, :], hqf[:, 2:4, :], ACT.Sigmoid, scale=-1.0).then_inc(s["hsig"], 1)
                act.wait_ge(s["hF"], l + 1)
                act.activation(qt[:, :, :], qt[:, :, :], ACT.Ln).then_inc(s["hln"], 1)
                act.activation(Xe[:, :, :], Xe[:, :, :], ACT.Ln).then_inc(s["hln"], 1)
                for lev in range(LEVELS + 1):
                    act.wait_ge(s["hx"], (LEVELS + 1) * l + lev + 1)
                    act.activation(Xe[:, :, :], Xe[:, :, :], ACT.Exp).then_inc(s["he"], 1)
                ready(act, (l, "ha", LEVELS, HEADS - 1))
                act.activation(qt[:, :, :], b[:, :, :], ACT.Exp).then_inc(s["he"], 1)
                for hp in range(2):
                    t = ready(act, (l, "hn", hp))
                    release(act.activation(kn[:, hp, :, :], t[:, :].rearrange("p (c n) -> p c n", c=NC), ACT.Copy),
                            (l, "hn", hp))
                act.wait_ge(s["ysq"], l + 1)
                act.activation(hsq[:, :, :], tok[:, :, 2 * GW:3 * GW], ACT.Square).then_inc(s["sq"], 1)
                root(l, 3, ms[:, 0:64])
                evens(l, "yt", None)
                squares(l, False)
                root(l, 4, ms[:, 0:NC])
                evens(l, "h2", C_NF)
                for i in range(2):
                    act.wait_ge(s["rt_x"], 2 * l + i + 1)
                    a = rx[i]
                    act.activation(a, a, ACT.Exp).then_inc(s["rt_e"], 1)
                experts(l)

        @block.vector
        def _(dve):
            sv = Steps(dve, s["dve_own"])
            then = sv.then

            def inv_root(l, u, a):
                dve.wait_ge(s["root"], ROOTS * l + u + 1)
                then(dve.reciprocal(rs[:a.shape[0], 0:a.shape[1]], a))

            def normalise(l, u, dst, sig):
                dve.wait_ge(s["ss"], NC * (2 * l + (u == 4) + 1))
                dve.tensor_scalar(ms[:, 0:NC], ms[:, 0:NC], 1.0 / DIM, EPS, ALU.mult, ALU.add).then_inc(s["mean"], 1)
                inv_root(l, u, ms[:, 0:NC])
                for c in range(NC):
                    ins = dve.tensor_scalar(dst[:, c, :], X[:, c, :], rs[:, c:c + 1], None, ALU.mult)
                ins.then_inc(sig, 1)

            def odds(l, name, col):
                for k in range(1, KD, 2):
                    t = ready(dve, (l, name, k))
                    if name == "qk":
                        for where, mask in QK_COPIES[k]:
                            if mask is None:
                                ins = dve.tensor_copy(qk_tile(where), t[:, :])
                            else:
                                ins = dve.tensor_scalar(qk_tile(where), t[:, :], K[:, K_MASK + mask:K_MASK + mask + 1],
                                                        None, ALU.mult)
                    elif col is None:
                        ins = dve.tensor_copy(hT[:, k, :], t[:, :])
                    else:
                        ins = dve.tensor_scalar(hT[:, k, :], t[:, :], C[:, col + k:col + k + 1], None, ALU.mult)
                    release(ins, (l, name, k))

            def copies(l, groups):
                for g, kind, a, n, what, c, vector in PTILES:
                    if not vector or g not in groups:
                        continue
                    key = ptile(l, g, kind, what, c)
                    t = ready(dve, key)
                    if kind == "n":
                        ins = dve.tensor_copy(Pn[:, c, what:what + n], t[:, 0:n])
                    elif what == "kv":
                        for j in range(2):
                            src = t[HD * j:HD * (j + 1), :]
                            dve.tensor_copy(kcT[0:HD, j, :], src)
                            ins = dve.tensor_copy(kcT[HD:P, j, 0:SEQ - 1], src[:, 1:])
                    elif what[0] == "m":
                        ins = dve.tensor_copy(mraw[:, int(what[1]), 3:], t[:, :])
                    else:
                        ins = dve.tensor_copy(hqf[:, int(what[1]), :], t[:, :])
                    release(ins, key)

            def mul(o, a, c):
                return dve.tensor_tensor(o, a, c, ALU.mult)

            def qk_norm(l):
                projected(dve, l, (0, 1, 2))
                for a, n, o in ((AQ, 512, 0), (DQ, GW, 512), (KS, HD, 768), (KW, HD, 896)):
                    last = mul(tok[:, :, o:o + n], Pn[:, :, a:a + n], Pn[:, :, a:a + n])
                then(last)
                for o, n, w, a in ((0, 512, HALF, 0), (512, GW, HD, 64), (768, HD, HD, 80), (896, HD, HD, 84)):
                    g = n // w
                    last = dve.tensor_reduce(ms[:, a:a + NC * g].rearrange("p (c g) -> p c g", c=NC),
                                             tok[:, :, o:o + n].rearrange("p c (g w) -> p c g w", w=w),
                                             AX.X, ALU.add)
                then(last)
                then(dve.tensor_scalar(ms[:, 0:64], ms[:, 0:64], 1.0 / HALF, EPS, ALU.mult, ALU.add))
                dve.tensor_scalar(ms[:, 64:88], ms[:, 64:88], 1.0 / HD, EPS, ALU.mult, ALU.add).then_inc(s["mean"], 1)
                inv_root(l, 1, ms[:, 0:88])
                rq = rs[:, 0:64].rearrange("p (c g) -> p c g", c=NC)[:, :, 0:8]
                then(dve.tensor_scalar(rq, rq, HALF ** -0.5, None, ALU.mult))
                then(dve.tensor_scalar(rs[:, 64:80], rs[:, 64:80], HD ** -0.5, None, ALU.mult))
                for a, n, w, o, r, g0 in ((AQ, 512, HALF, 0, 0, None), (DQ, GW, HD, 512, 64, None)):
                    g = n // w
                    last = mul(tok[:, :, o:o + n].rearrange("p c (g w) -> p c g w", w=w),
                               Pn[:, :, a:a + n].rearrange("p c (g w) -> p c g w", w=w),
                               rs[:, r:r + NC * g].rearrange("p (c g o) -> p c g o", c=NC, o=1)
                               .to_broadcast([P, NC, g, w]))
                for a, o, r in ((KS, 768, 80), (KW, 896, 84)):
                    for i in range(2):
                        last = mul(tok[:, :, o + HD * i:o + HD * (i + 1)], Pn[:, :, a:a + HD],
                                   rs[:, r:r + NC].rearrange("p (c o) -> p c o", o=1).to_broadcast([P, NC, HD]))
                then(last)
                for o, n, w, r in ((0, GW, HALF, R_DQ), (GW, GW, HALF, R_DK), (512, GW, HD, R_NQ),
                                   (768, P, HD, R_NK + HD), (896, P, HD, R_NK + 2 * HD)):
                    v = tok[:, :, o:o + n].rearrange("p c (g w) -> p c g w", w=w)
                    last = mul(v, v, R[:, r:r + w].rearrange("p (a b w) -> p a b w", a=1, b=1)
                               .to_broadcast([P, NC, n // w, w]))
                last.then_inc(s["qkn_ready"], 1)

            def differential_lambda(l):
                v = R[:, R_LAM:R_LAM + 4 * HALF].rearrange("p (a b w) -> p a b w", a=2, b=2)
                then(mul(tmp[:, 0:2 * HALF].rearrange("p (a w) -> p a w", a=2), v[:, :, 0, :], v[:, :, 1, :]))
                dve.tensor_reduce(lam4, tmp[:, 0:2 * HALF].rearrange("p (a w) -> p a w", a=2), AX.X, ALU.add) \
                    .then_inc(s["lam_d"], 1)
                dve.wait_ge(s["lam_e"], l + 1)
                then(dve.tensor_tensor(lam, lam4[:, 1:2], lam4[:, 0:1], ALU.subtract))
                then(dve.tensor_scalar(lam, lam, -(0.8 - 0.6 * math.exp(-0.3 * l)), None, ALU.add))

            def compress_norm(l):
                t = ready(dve, (l, "cc", 0))
                release(dve.tensor_copy(Kc[0:NCMP, 0, :], t[0:NCMP, 0:HD]), (l, "cc", 0))
                t = ready(dve, (l, "cc", 1))
                release(dve.tensor_copy(Vc[0:NCMP, :], t[0:NCMP, 0:HD]), (l, "cc", 1))
                copied(dve, (l, "cc", 0))
                then(mul(tmp[0:NCMP, 0:HD], Kc[0:NCMP, 0, :], Kc[0:NCMP, 0, :]))
                then(dve.tensor_reduce(ms[0:NCMP, 0:1], tmp[0:NCMP, 0:HD], AX.X, ALU.add))
                dve.tensor_scalar(ms[0:NCMP, 0:1], ms[0:NCMP, 0:1], 1.0 / HD, EPS, ALU.mult, ALU.add) \
                    .then_inc(s["mean"], 1)
                inv_root(l, 2, ms[0:NCMP, 0:1])
                for i in (1, 0):
                    last = dve.scalar_tensor_tensor(Kc[0:NCMP, i, :], Kc[0:NCMP, 0, :], rs[0:NCMP, 0:1],
                                                    R[0:NCMP, R_NK:R_NK + HD], ALU.mult, ALU.mult)
                last.then_inc(s["ck_n"], 1)

            def compress_keys(l):
                t = ready(dve, (l, "ck"))
                release(dve.tensor_copy(KcT[:, :], t[:, 0:NCMP]), (l, "ck"))

            def compressed_scores(l):
                bc = K[:, K_CMPB:K_CMPB + 16 * NCMP].rearrange("p (a n) -> p a n", n=NCMP)
                for o in range(2):
                    t = ready(dve, (l, "cs", o))
                    release(dve.tensor_tensor(Sc[:, o::2, :], t[:, 0:8 * NCMP].rearrange("p (a n) -> p a n", n=NCMP),
                                              bc[:, o::2, :], ALU.add), (l, "cs", o))
                for o in range(2):
                    copied(dve, (l, "cs", o))
                then(dve.tensor_reduce(cmx[:, :], Sc[:, :, :], AX.X, ALU.max))
                dve.tensor_tensor(Sc[:, :, :], Sc[:, :, :],
                                  cmx.rearrange("p (a o) -> p a o", o=1).to_broadcast([P, 16, NCMP]),
                                  ALU.subtract).then_inc(s["cs_x"], 1)

            def compressed_probabilities(l):
                dve.wait_ge(s["cs_e"], l + 1)
                dve.wait_ge(s["gsig"], 3 * (l + 1))
                then(dve.tensor_reduce(cfac[:, :], Sc[:, :, :], AX.X, ALU.add))
                then(dve.reciprocal(cfac[:, :], cfac[:, :]))
                f = cfac.rearrange("p (c h) -> p c h", c=NC)
                then(mul(f, f, Pn[:, :, DG:DG + 12:3]))
                S4 = Sc[:, :, :].rearrange("p (c h) n -> p c h n", c=NC)
                V4 = K[:, K_CMPV:K_CMPV + NC * NCMP].rearrange("p (c o n) -> p c o n", c=NC, o=1)
                then(mul(S4, S4, V4.to_broadcast([P, NC, HEADS, NCMP])))
                mul(Sc[:, :, :], Sc[:, :, :], cfac.rearrange("p (a o) -> p a o", o=1).to_broadcast([P, 16, NCMP])) \
                    .then_inc(s["cs_p"], 1)

            def compressed_turned(l):
                for c in range(NC):
                    t = ready(dve, (l, "cp", c))
                    release(dve.tensor_copy(PcT[0:NCMP, HEADS * c:HEADS * (c + 1), :],
                                            t[0:NCMP, :].rearrange("p (h q) -> p h q", h=HEADS)), (l, "cp", c))

            def compressed_outputs(l):
                for c in range(NC):
                    t = ready(dve, (l, "co", c))
                    release(dve.tensor_copy(tok[:, c, 768:1024], t[:, 0:GW]), (l, "co", c))

            def attend(l):
                dve.wait_ge(s["bias_in"], 16 * (l + 1))
                prob, negS = scratch(l)

                def negated(i):
                    m, c = ITERS[i]
                    n = (c + 1) * P
                    t = ready(dve, (l, "S", i))
                    if i >= 4:
                        dve.wait_ge(s["exp_done"], len(ITERS) * l + i - 3)
                    release(dve.tensor_tensor_reduce(
                        out=negS[:, i % 4, 0:n], in0=t[:, 0:n], in1=bias[:, MAPS[m][3], SEQ - n:SEQ],
                        scale=-1.0, scalar=3e38, op0=ALU.add, op1=ALU.min, accum_out=nmax[:, i:i + 1]),
                        (l, "S", i))

                def mix(i):
                    n = (ITERS[i][1] + 1) * P
                    dve.wait_ge(s["exp_done"], len(ITERS) * l + i + 2)
                    f = fac[:, i + 1:i + 2]
                    then(dve.reciprocal(f, psumcol[:, i + 1:i + 2]))
                    then(dve.scalar_tensor_tensor(f, f, lam, psumcol[:, i:i + 1], ALU.mult, ALU.mult))
                    dve.scalar_tensor_tensor(prob[:, i % 4, 0:n], prob[:, (i + 1) % 4, 0:n], f, prob[:, i % 4, 0:n],
                                             ALU.mult, ALU.add).then_inc(s["mixed"], 1)

                def outputs(u):
                    i = UNITS[u][0]
                    m, c = ITERS[i]
                    t = ready(dve, (l, "O", u))
                    head = MAPS[m][4]
                    dst = tok[:, c, head * HD:head * HD + HD]
                    f = fac[:, i:i + 1]
                    then(dve.reciprocal(f, psumcol[:, i:i + 1]))
                    if i < PAIRED:
                        release(dve.tensor_scalar(dst, t[:, 0:HD], f, None, ALU.mult), (l, "O", u))
                        return
                    g = DG + 3 * (head - 12) + 1 + m % 2
                    then(mul(f, f, Pn[:, c, g:g + 1]))
                    copied(dve, (l, "O", u - NC) if m % 2 else (l, "co", c))
                    release(dve.scalar_tensor_tensor(dst, t[:, 0:HD], f, dst, ALU.mult, ALU.add), (l, "O", u))

                for k in range(len(UNITS) + 3):
                    for i in UNITS[k] if k < len(UNITS) else ():
                        negated(i)
                    if 1 <= k <= PAIRED // 2:
                        mix(UNITS[k - 1][0])
                    if k >= 3:
                        outputs(k - 3)
                    if k == 1:
                        compressed_probabilities(l)
                    if k == 3:
                        compressed_turned(l)
                    if k == 5:
                        compressed_outputs(l)

            def convolve(l):
                then(dve.memset(mraw[:, :, 0:3], 0.0))
                ready(dve, (l, "ch", 1))
                projected(dve, l, (4,))
                for j in range(4):
                    for i in range(4):
                        w = C[:, C_CONV + 4 * i + j:C_CONV + 4 * i + j + 1]
                        src = mraw[:, i, j:j + SEQ]
                        if j == 0:
                            last = dve.tensor_scalar(mqk[:, i, :], src, w, None, ALU.mult)
                        else:
                            last = dve.scalar_tensor_tensor(mqk[:, i, :], src, w, mqk[:, i, :], ALU.mult, ALU.add)
                    if j < 3:
                        then(last)
                last.then_inc(s["conv_m"], 1)

            def gate_rows(l):
                t = ready(dve, (l, "gi"))
                release(dve.tensor_scalar(gA[:, :], t[0:HEADS, :], C[0:HEADS, C_GB:C_GB + 1], None, ALU.add),
                        (l, "gi"))
                t = ready(dve, (l, "gf"))
                release(dve.tensor_scalar(gM[:, :], t[0:HEADS, :], C[0:HEADS, C_GB + 1:C_GB + 2], None, ALU.add),
                        (l, "gf"))
                copied(dve, (l, "gf"))
                dve.scalar_tensor_tensor(gMt[:, :], gM[:, :], -1.0, gM[:, :], ALU.mult, ALU.min).then_inc(s["gate_a"], 1)
                dve.wait_ge(s["gate_b"], l + 1)
                then(dve.scalar_tensor_tensor(gM[:, :], gM[:, :], 0.0, gMt[:, :], ALU.min, ALU.subtract))
                then(dve.tensor_tensor_scan(gMt[:, :], K[0:HEADS, K_IOTA + PER_GROUP - 1:K_IOTA + PER_GROUP].to_broadcast([HEADS, SEQ]), gM[:, :], 0.0,
                                            ALU.mult, ALU.add))
                then(dve.tensor_tensor(gA[:, :], gA[:, :], gMt[:, :], ALU.subtract))
                then(dve.tensor_tensor_scan(gM[:, :], gA[:, :], gA[:, :], 0.0, ALU.max, ALU.max))
                dve.tensor_tensor(gMt[:, :], gMt[:, :], gM[:, :], ALU.add).then_inc(s["gate_r"], 1)

            def gate_columns(l):
                t = ready(dve, (l, "gc"))
                release(dve.tensor_copy(gcol[:, :, :, :].rearrange("p a c h -> p (a c h)"), t[:, 0:32]), (l, "gc"))

            def mlstm(l):
                projected(dve, l, (6,))
                dve.memset(Vm[:, :, :, HD:HD + 1], 1.0)
                dve.tensor_copy(Vm[:, :, :, 0:HD], Pn[:, :, BV:BV + GW].rearrange("p c (h w) -> p c h w", h=HEADS)) \
                    .then_inc(s["vm_ready"], 1)
                copied(dve, (l, "gc"))
                dve.wait_ge(s["en_d"], l + 1)
                for h in range(HEADS):
                    mb = ready(dve, (l, "mb", h))

                    def weights(c):
                        n = SEQ - c * P
                        i = NC * h + c
                        dve.wait_ge(s["me"], NC * HEADS * l + i + 1)
                        t = ready(dve, (l, "ms", h, c))
                        w = WT[:, h % 2, WOFF[c]:WOFF[c] + n]
                        release(dve.scalar_tensor_tensor(w, t[:, 0:n], HD ** -0.5, E[:, c % 2, 0:n],
                                                         ALU.mult, ALU.mult), (l, "ms", h, c))
                        copied(dve, (l, "ms", h, c))
                        mul(w[:, 0:P], w[:, 0:P], caus).then_inc(s["w_ready"], 1)

                    for c in range(NC):
                        n = SEQ - c * P
                        i = NC * h + c
                        if i >= 2:
                            dve.wait_ge(s["me"], NC * HEADS * l + i - 1)
                        ins = dve.tensor_scalar(D[:, c % 2, 0:n], mb[:, c * P:SEQ], gcol[:, 0, c, h:h + 1], 0.0,
                                                ALU.subtract, ALU.max)
                        if c < NC - 1:
                            ins.then_inc(s["md"], 1)
                        else:
                            release(ins, (l, "mb", h))
                        if c:
                            weights(c - 1)
                    weights(NC - 1)
                    t = ready(dve, (l, "mo", h))
                    t = t[:, 0:NC * 65].rearrange("p (c w) -> p c w", c=NC)
                    den = t[:, :, HD]
                    md = mden[:, :]
                    then(dve.tensor_copy(md, den))
                    then(dve.scalar_tensor_tensor(md, md, -1.0, md, ALU.mult, ALU.max))
                    then(dve.tensor_tensor(md, md, gcol[:, 1, :, h], ALU.max))
                    then(dve.reciprocal(md, md))
                    release(mul(tok[:, :, GW + h * HD:GW + (h + 1) * HD], t[:, :, 0:HD],
                                md.rearrange("p (c o) -> p c o", o=1).to_broadcast([P, NC, HD])), (l, "mo", h))

            def lower_bounds(l):
                x = C[:, C_LB:C_LB + 4].rearrange("p (l t) -> p l t", l=2)
                m = lbc[:, 0, :]
                then(dve.tensor_tensor(m, x[:, 0, :], x[:, 1, :], ALU.max))
                dve.tensor_tensor(lbx[:, :, :], x, m.rearrange("p (o t) -> p o t", o=1).to_broadcast([P, 2, 2]),
                                  ALU.subtract).then_inc(s["lb_a"], 1)
                dve.wait_ge(s["lb_b"], l + 1)
                then(dve.tensor_tensor(m, lbx[:, 0, :], lbx[:, 1, :], ALU.add))
                then(dve.reciprocal(m, m))
                then(mul(lbs[:, :, :], lbx[:, :, :], m.rearrange("p (o t) -> p o t", o=1).to_broadcast([P, 2, 2])))
                lb, lf, om, df = (lbc[:, i, :] for i in range(4))
                if l == 0:
                    then(dve.tensor_copy(lb, lbs[:, 0, :]))
                else:
                    then(dve.tensor_tensor(lb, lbs[:, 0, :], lbs[:, 1, :], ALU.add))
                then(dve.tensor_tensor(lb, lb, lbs[:, 0, :], ALU.subtract))
                then(dve.tensor_scalar(lf, lb, 1e-30, None, ALU.max))
                then(dve.tensor_scalar(om, lb, -1.0, 1.0, ALU.mult, ALU.add))
                then(dve.tensor_tensor(df, lf, lb, ALU.subtract))

            def hgrn(l):
                _, lf, om, df = (lbc[:, i, :] for i in range(4))
                output_squares(l)
                dve.wait_ge(s["hsig"], 3 * (l + 1))
                for i in range(2):
                    dve.tensor_scalar(Xe[:, i, :], Xe[:, i, :], om[:, i:i + 1], lf[:, i:i + 1], ALU.mult, ALU.add)
                    last = dve.tensor_scalar(kk[:, i, :], kk[:, i, :], om[:, i:i + 1], df[:, i:i + 1],
                                             ALU.mult, ALU.subtract)
                then(last)
                dve.tensor_scalar(qt[:, :, :], Xe[:, :, :], 1.0 / LN_SPLIT, None, ALU.max)
                then(dve.memset(A[:, :, :], 0.0))
                dve.tensor_scalar(Xe[:, :, :], Xe[:, :, :], LN_SPLIT, 1.0, ALU.mult, ALU.min).then_inc(s["hF"], 1)
                dve.wait_ge(s["hF"], l + 1)
                dve.memset(nopcell, 0.0).then_inc(s["hqk"], 1)
                sum_squares()
                dve.wait_ge(s["hln"], 2 * (l + 1))
                then(dve.tensor_tensor(qt[:, :, :], qt[:, :, :], Xe[:, :, :], ALU.add))
                for i in range(2):
                    last = dve.tensor_tensor_scan(b[:, i, :], K[:, K_SEG:K_SEG + SEQ], qt[:, i, :], 0.0,
                                                  ALU.mult, ALU.add)
                then(last)

                def products(lev):
                    mask = K[:, K_LVL + lev * P:K_LVL + (lev + 1) * P].bitcast(I32) \
                        .rearrange("p (o t) -> p o t", o=1).to_broadcast([P, NC, P])
                    for h in range(HEADS):
                        t = ready(dve, (l, "ha", lev, h))
                        release(dve.copy_predicated(A[:, h, :].rearrange("p (c t) -> p c t", c=NC), mask,
                                                    t[:, :].rearrange("p (c t) -> p c t", c=NC)), (l, "ha", lev, h))

                flat = lambda v: v[:, :, :].rearrange("p a n -> p (a n)")
                for lev in range(1, LEVELS + 2):
                    if lev <= LEVELS:
                        w = HB >> (lev - 1)
                        bv, xv = (flat(v).rearrange("p (n w) -> p n w", w=w) for v in (b, Xe))
                        seam = bv[:, :, w // 2 - 1:w // 2].to_broadcast([P, 2 * SEQ // w, w // 2])
                        dve.tensor_tensor(xv[:, :, w // 2:], bv[:, :, w // 2:], seam, ALU.subtract)
                        dve.tensor_tensor(xv[:, :, 0:w // 2], seam, bv[:, :, 0:w // 2], ALU.subtract) \
                            .then_inc(s["hx"], 1)
                    else:
                        bv, xv = (flat(v).rearrange("p (n w) -> p n w", w=HB) for v in (b, Xe))
                        dve.tensor_tensor(xv, bv[:, :, HB - 1:HB].to_broadcast([P, 2 * NB, HB]), bv, ALU.subtract) \
                            .then_inc(s["hx"], 1)
                    if lev <= LEVELS:
                        output_gain(l, lev - 1)
                    products(lev - 1)
                    dve.wait_ge(s["he"], (LEVELS + 2) * l + lev)
                    if lev <= LEVELS:
                        mul(qt[:, :, :], hqf[:, 0:2, :], Xe[:, :, :])
                    mul(kt[:, :, :], kk[:, :, :], Xe[:, :, :]).then_inc(s["hqk"], 1)
                    dve.wait_ge(s["hqk"], (LEVELS + 2) * l + lev + 1)
                dve.wait_ge(s["he"], (LEVELS + 2) * (l + 1))
                then(dve.tensor_copy(dec[:, :, :], qt[:, :, HB - 1:SEQ:HB]))
                mul(qt[:, :, :], hqf[:, 0:2, :], qt[:, :, :]).then_inc(s["hq_in"], 1)
                for i in range(NB - 1):
                    c, j = i // 4, i % 4
                    for hp in range(2):
                        t = ready(dve, (l, "hu", hp, j))
                        u = t[:, c * P:(c + 1) * P]
                        if i == 0:
                            ins = dve.tensor_copy(St[:, hp, 1, :], u)
                        else:
                            ins = dve.scalar_tensor_tensor(St[:, hp, i + 1, :], St[:, hp, i, :],
                                                           dec[:, hp, i:i + 1], u, ALU.mult, ALU.add)
                        if c == (2 if j == 3 else 3):
                            release(ins, (l, "hu", hp, j))
                            if hp:
                                copied(dve, (l, "hu", 1, j))
                        elif hp:
                            then(ins)
                dve.memset(St[:, :, 0, :], 0.0).then_inc(s["hst"], 1)
                for c in range(NC):
                    for o in range(2):
                        t = ready(dve, (l, "ho", c, o))
                        v = tok[:, c, 512:768].rearrange("p (a o n) -> p o a n", a=2, o=2)
                        release(dve.tensor_copy(v[:, o], t[:, 0:P].rearrange("p (a n) -> p a n", a=2)),
                                (l, "ho", c, o))

            def squares_mean(sq, cols, first, heads):
                return dve.tensor_reduce(ms[:, 0:64].rearrange("p (c h) -> p c h", c=NC)[:, :, first:first + heads],
                                         sq[:, :, cols:cols + heads * HD].rearrange("p c (h w) -> p c h w", w=HD),
                                         AX.X, ALU.add)

            def output_squares(l):
                copied(dve, (l, "mo", HEADS - 1))
                copied(dve, (l, "O", len(UNITS) - 1))
                mul(ysq[:, :, 0:2 * GW], tok[:, :, 0:2 * GW], tok[:, :, 0:2 * GW])
                then(mul(ysq[:, :, 2 * GW:], tok[:, :, 3 * GW:], tok[:, :, 3 * GW:]))

            def sum_squares():
                squares_mean(ysq, 0, 0, 8)
                squares_mean(ysq, 2 * GW, 12, HEADS)

            def output_gain(l, part):
                def gain(a):
                    return R[:, R_OG + a:R_OG + a + GW].rearrange("p (o n) -> p o n", o=1).to_broadcast([P, NC, GW])

                dve.wait_ge(s["gsig"], 3 * (l + 1))
                v, by = ((Pn[:, :, BO:BO + GW], gain(GW)), (tok[:, :, GW:2 * GW], Pn[:, :, BO:BO + GW]),
                         (Pn[:, :, CG:CG + GW], gain(2 * GW)), (tok[:, :, 0:GW], gain(0)),
                         (tok[:, :, 3 * GW:], gain(3 * GW)))[part]
                then(mul(v, v, by))

            def output_norms(l):
                copied(dve, (l, "ho", NC - 1, 1))
                dve.memset(nopcell, 0.0).then_inc(s["ysq"], 1)
                dve.wait_ge(s["sq"], l + 1)
                then(squares_mean(hsq, 0, 8, HEADS))
                dve.tensor_scalar(ms[:, 0:64], ms[:, 0:64], 1.0 / HD, EPS, ALU.mult, ALU.add).then_inc(s["mean"], 1)
                inv_root(l, 3, ms[:, 0:64])
                ra = rs[:, 0:64].rearrange("p (c h) -> p c h", c=NC)[:, :, 0:HEADS]
                then(dve.tensor_scalar(ra, ra, 1.0 - (0.8 - 0.6 * math.exp(-0.3 * l)), None, ALU.mult))
                y = tok[:, :, 2 * GW:3 * GW]
                then(mul(y, y, Pn[:, :, CG:CG + GW]))
                tv = tok[:, :, :].rearrange("p c (h w) -> p (c h) w", w=HD)
                mul(tv, tv, rs[:, 0:64].rearrange("p (g o) -> p g o", o=1).to_broadcast([P, 64, HD])) \
                    .then_inc(s["y_ready"], 1)

            def route(l):
                t = ready(dve, (l, "rt"))
                release(dve.tensor_tensor(rt[:, :, :], t[:, 0:36 * NC].rearrange("p (c n) -> p c n", c=NC),
                                          R[:, R_BG:R_BG + 36].rearrange("p (o n) -> p o n", o=1)
                                          .to_broadcast([P, NC, 36]), ALU.add), (l, "rt"))
                copied(dve, (l, "rt"))
                desc = K[:, K_IOTA:K_IOTA + PER_GROUP].rearrange("p (o n) -> p o n", o=1)

                def col(v, n):
                    return v.rearrange("p (c o) -> p c o", o=1).to_broadcast([P, NC, n])

                def first_best(v, n, best, hot):
                    then(dve.tensor_reduce(best, v, AX.X, ALU.max))
                    then(dve.tensor_tensor(hot, v, col(best, n), ALU.is_equal))
                    then(mul(hot, hot, desc[:, :, PER_GROUP - n:].to_broadcast([P, NC, n])))
                    then(dve.tensor_reduce(rmark, hot, AX.X, ALU.max))
                    then(dve.tensor_tensor(hot, hot, col(rmark, n), ALU.is_equal))

                first_best(rt[:, :, 0:GROUPS], GROUPS, rbest, ghot)
                dve.tensor_tensor(rx[0], rt[:, :, 0:GROUPS], col(rbest, GROUPS), ALU.subtract).then_inc(s["rt_x"], 1)
                dve.wait_ge(s["rt_e"], 2 * l + 1)
                then(dve.tensor_reduce(gprob, rx[0], AX.X, ALU.add))
                then(dve.reciprocal(gprob, gprob))
                gh4 = ghot.rearrange("p c (g o) -> p c g o", o=1).to_broadcast([P, NC, GROUPS, PER_GROUP])
                then(mul(group_logits[:, :, :, :], rt[:, :, GROUPS:].rearrange("p c (g e) -> p c g e", g=GROUPS), gh4))
                then(dve.tensor_reduce(l8, group_logits[:, :, :, :].rearrange("p c g e -> p c e g"), AX.X, ALU.add))
                first_best(l8, PER_GROUP, rbest, hot1)
                then(dve.scalar_tensor_tensor(l8, hot1, -3e38, l8, ALU.mult, ALU.add))
                first_best(l8, PER_GROUP, rsecond, hot2)
                dve.tensor_tensor(rx[1], rsecond, rbest, ALU.subtract).then_inc(s["rt_x"], 1)
                dve.wait_ge(s["rt_e"], 2 * l + 2)
                then(dve.tensor_scalar(rbest, rx[1], 1.0, None, ALU.add))
                then(dve.reciprocal(rbest, rbest))
                then(mul(gprob, gprob, rbest))
                then(mul(rx[1], rx[1], gprob))
                for i, hot in enumerate((hot1, hot2)):
                    last = mul(hots[:, :, EXPERTS * i:EXPERTS * (i + 1)].rearrange("p c (g e) -> p c g e", g=GROUPS),
                               hot.rearrange("p c (o e) -> p c o e", o=1).to_broadcast([P, NC, GROUPS, PER_GROUP]),
                               gh4)
                then(last)
                dve.tensor_tensor(selsum[:, :, :], hots[:, :, 0:EXPERTS], hots[:, :, EXPERTS:], ALU.add) \
                    .then_inc(s["sel_ready"], 1)
                t = ready(dve, (l, "rk"))
                release(dve.tensor_copy(rk[:, :, :].rearrange("p a b -> p (a b)"), t[:, 0:(NC + 1) * EXPERTS]),
                        (l, "rk"))
                copied(dve, (l, "rk"))
                thr = K[:, K_THR:K_THR + 8].rearrange("p (o n) -> p o n", o=1)

                def up(v, n):
                    return v.rearrange("p (a o) -> p a o", o=1).to_broadcast([v.shape[0], v.shape[1], n])

                cmp = rtmp[:, 0:8 * EXPERTS].rearrange("p (a b) -> p a b", b=8)
                then(dve.tensor_tensor(cmp, up(rk[:, NC, :], 8), thr.to_broadcast([P, EXPERTS, 8]), ALU.is_gt))
                then(dve.tensor_reduce(nblk, cmp, AX.X, ALU.add))
                then(dve.tensor_tensor_scan(bend, K[:, K_IOTA + PER_GROUP - 1:K_IOTA + PER_GROUP]
                                            .to_broadcast([P, EXPERTS]), nblk, 0.0, ALU.mult, ALU.add))
                then(dve.tensor_tensor(bst, bend, nblk, ALU.subtract))
                for i in range(2):
                    last = mul(oslot[:, i::2, 0:EXPERTS], hots8[:, i::2, :], rk[:, 0:NC, :])
                mul(oblk8, hots8[:, :, :], bst.rearrange("p (o e) -> p o e", o=1).to_broadcast([P, 2 * NC, EXPERTS]))
                then(dve.memset(hg[:, :, :], 0.0))
                dve.tensor_reduce(rank, oslot[:, :, 0:EXPERTS], AX.X, ALU.add)
                then(dve.tensor_reduce(blk, oblk8, AX.X, ALU.add))
                c8 = rtmp[:, 0:64].rearrange("p (a b) -> p a b", b=8)
                then(dve.tensor_tensor(c8, up(rank, 8), thr.to_broadcast([P, 8, 8]), ALU.is_ge))
                then(dve.tensor_reduce(quot, c8, AX.X, ALU.add))
                then(dve.tensor_tensor(blk, blk, quot, ALU.add))
                dve.tensor_scalar(blk, blk, -1.0, None, ALU.add)
                then(dve.tensor_scalar(quot, quot, -float(SLOTS), float(SLOTS), ALU.mult, ALU.add))
                then(dve.tensor_tensor(rank, rank, quot, ALU.add))
                dve.tensor_tensor(oslot[:, :, :], K[:, K_SLOT:K_SLOT + P].rearrange("p (o n) -> p o n", o=1)
                                  .to_broadcast([P, 8, P]), up(rank, P), ALU.is_equal)
                then(dve.tensor_tensor(oblk[:, :, 2, :], K[:, K_BLK:K_BLK + TABW].rearrange("p (o n) -> p o n", o=1)
                                       .to_broadcast([P, 8, TABW]), up(blk, TABW), ALU.is_equal))
                mul(oblk[:, :, 0, :], oblk[:, :, 2, :], up(K[:, K_T2:K_T2 + 8], TABW))
                mul(oblk[:, :, 1, :], oblk[:, :, 2, :], up(K[:, K_T4:K_T4 + 8], TABW)).then_inc(s["ob_ready"], 1)
                eb = rtmp[0:1, :].rearrange("p (b e) -> p b e", e=EXPERTS)
                be = bend[0:1, :]
                then(dve.tensor_tensor(eb, be.rearrange("p (o e) -> p o e", o=1).to_broadcast([1, BLOCKS, EXPERTS]),
                                       up(K[0:1, K_BLK:K_BLK + BLOCKS], EXPERTS), ALU.is_le))
                then(dve.tensor_reduce(ebf[0:1, 0:BLOCKS], eb, AX.X, ALU.add))
                then(dve.tensor_scalar(ebf[0:1, 0:BLOCKS], ebf[0:1, 0:BLOCKS], float(EXPERTS - 1), None, ALU.min))
                then(dve.tensor_tensor(rtmp[0:1, 0:BLOCKS // 2 - 1], be[:, EXPERTS - 1:].to_broadcast([1, BLOCKS // 2 - 1]),
                                       K[0:1, K_BLK + 2:K_BLK + BLOCKS:2], ALU.is_gt))
                then(dve.tensor_reduce(ebf[0:1, BLOCKS:BLOCKS + 1], rtmp[0:1, 0:BLOCKS // 2 - 1], AX.X, ALU.add))
                dve.tensor_copy(ebt[0:1, 0:BLOCKS + 1], ebf[0:1, 0:BLOCKS + 1])
                t = ready(dve, (l, "rb"))
                release(dve.tensor_copy(tab[:, :, :].rearrange("p a b -> p (a b)"), t[:, 0:3 * TABW]), (l, "rb"))
                copied(dve, (l, "rb"))
                then(dve.tensor_scalar(tab[:, 2, :], tab[:, 2, :], -1.0, 1.0, ALU.mult, ALU.add))
                then(dve.tensor_scalar(tab[:, 2, :], tab[:, 2, :], K[:, K_OOB:K_OOB + 1],
                                       K[:, K_HALF:K_HALF + 1], ALU.mult, ALU.add))
                for i in range(2):
                    last = dve.tensor_tensor(tab[:, i, :], tab[:, i, :], tab[:, 2, :], ALU.add)
                then(last)
                dve.tensor_copy(gi, tab[:, 0, :])
                dve.tensor_copy(si, tab[:, 1, :]).then_inc(s["route_ready"], 1)

            def experts(l):
                m = moe[l]
                last_pair = pairs(dve, l)
                gain = C[:, C_NF:C_NF + KD].rearrange("p (j k o) -> p k j o", j=2, o=1) \
                    .to_broadcast([P, 4, 2, SLOTS])

                def tokens(e, u):
                    static = isinstance(e, int)
                    dve.wait_ge(m["tr_full"], e + 1)
                    if not static or e >= 2:
                        dve.wait_ge(m["au_full"], e - 1)
                    mul(hgT[:, u].rearrange("p k (j n) -> p k j n", j=2),
                        psum[u][:, :].rearrange("p (k j n) -> p k j n", k=4, j=2), gain) \
                        .then_inc(m["tr_copied"], 1)

                def step(e, u):
                    tokens(e + 1, 1 - u)
                    dve.wait_ge(m["silu_done"], e + 1)
                    if not isinstance(e, int) or e >= 2:
                        dve.wait_ge(m["y_full"], e - 1)
                    mul(actT[:, u, :], sil[:, u, :], psum[4 + u][:, P:2 * P]).then_inc(m["act_ready"], 1)

                tokens(0, 0)
                blocks(dve, last_pair, step)
                dve.wait_ge(m["scatter_index"], last_pair * 2 + 3)
                for c in range(NC):
                    dve.wait_ge(yc_in[c], 16 * (l + 1))
                    for j, w in enumerate((gprob, rx[1])):
                        ins = dve.scalar_tensor_tensor(X[:, c, :], yc[:, c, DIM * j:DIM * (j + 1)], w[:, c:c + 1],
                                                       X[:, c, :], ALU.mult, ALU.add)
                        if j == 0:
                            then(ins)
                    ins.then_inc(s["x_new"], 1)

            dve.wait_ge(s["const_in"], 16)
            for l in range(LAYERS):
                for c in range(NC):
                    x_ready(dve, l, c)
                normalise(l, 0, tok, s["h_ready"])
                dve.wait_ge(s["par_in"], 32 * (l + 1))
                odds(l, "ht", C_NM)
                copies(l, (0, 1, 2, 3))
                differential_lambda(l)
                qk_norm(l)
                copies(l, (4, 5))
                compress_norm(l)
                convolve(l)
                copies(l, (6,))
                compress_keys(l)
                copies(l, (7,))
                gate_rows(l)
                lower_bounds(l)
                copies(l, (8,))
                odds(l, "qk", None)
                compressed_scores(l)
                gate_columns(l)
                attend(l)
                mlstm(l)
                hgrn(l)
                output_norms(l)
                odds(l, "yt", None)
                for c in range(NC):
                    for j in range(2):
                        t = ready(dve, (l, "wo", c, j))
                        x = X[:, c, 512 * j:512 * j + 512]
                        release(dve.tensor_tensor(x, x, t[:, :], ALU.add), (l, "wo", c, j))
                normalise(l, 4, h2n, s["h2_ready"])
                odds(l, "h2", C_NF)
                route(l)
                experts(l)


_NAMED = ["x", "w_in", "w_out", "nsa_cmp_w1", "nsa_cmp_w2", "moe_w_group", "moe_w_expert",
          "moe_w_gate", "moe_w_up", "moe_w_down"]


def _constants():
    p = np.arange(P)
    k = np.zeros((P, KW_ALL), np.float32)
    k[:, K_ID:K_ID + P] = np.eye(P)
    k[:, K_LVL:K_LVL + P] = np.eye(P)
    s_, t_ = p[:, None], p[None, :]
    for lev in range(1, LEVELS + 1):
        w = HB >> (lev - 1)
        k[:, K_LVL + lev * P:K_LVL + (lev + 1) * P] = \
            (s_ // w == t_ // w) & (s_ % w < w // 2) & (t_ % w >= w // 2)
    k[:, K_CAUS:K_CAUS + P] = s_ <= t_
    slopes = 2.0 ** (-8.0 * np.arange(1, 2 * HEADS + 1) / (2 * HEADS))
    diff, nsa = slopes[0::2].astype(np.float32), slopes[1::2].astype(np.float32)
    tokens = P * np.arange(NC)[None, :, None] + p[:, None, None]
    dist = tokens - (CMP_STRIDE * np.arange(NCMP) + CMP_LEN - 1)[None, None, :]
    v = dist >= 0
    cb = np.where(v[:, :, None, :], -nsa[None, None, :, None] * dist[:, :, None, :].astype(np.float32),
                  np.float32(NEG))
    k[:, K_CMPB:K_CMPB + 16 * NCMP] = cb.reshape(P, -1)
    k[:, K_CMPV:K_CMPV + NC * NCMP] = v.reshape(P, -1)
    k[:, K_SEG:K_SEG + SEQ] = np.arange(SEQ) % HB != 0
    k[:, K_IOTA:K_IOTA + PER_GROUP] = np.arange(PER_GROUP, 0, -1)
    k[:, K_SLOT:K_SLOT + P] = np.arange(P) % SLOTS
    k[:, K_BLK:K_BLK + TABW] = np.arange(TABW)
    k[:, K_THR:K_THR + 8] = SLOTS * np.arange(8)
    k[:, K_UP:K_UP + P] = s_ < t_
    k[:, K_FOLD:K_FOLD + SLOTS] = s_ % SLOTS == np.arange(SLOTS)[None, :]
    token = P * (np.arange(2 * NC) // 2)[None, :] + s_
    k[:, K_T2:K_T2 + 2 * NC] = 2 * token
    k[:, K_T4:K_T4 + 2 * NC] = 4 * token + 2 * (np.arange(2 * NC) % 2)[None, :]
    k[:, K_HALF] = p // SLOTS
    k[:, K_OOB] = OUTSIDE + p
    for i in range(6):
        k[:, K_MASK + i] = p // HALF == i if i < 4 else p // HD == i - 4
    d = (p[:, None] + (SEQ - P) - np.arange(SEQ)[None, :]).astype(np.float32)
    al = np.stack([np.where(d >= 0, -sl * d, np.float32(NEG)) for sl in np.concatenate([diff, nsa])], 1)
    return k, al.reshape(P, -1).astype(np.float32)


def _layout(v):
    rows = np.concatenate([v[n].reshape(LAYERS, -1) for n in (
        "diff_q_gain", "diff_k_gain", "nsa_q_gain", "nsa_k_gain", "diff_sub_gain", "mlstm_out_gain",
        "hgrn_out_gain", "nsa_out_gain", "moe_b_group", "moe_b_expert", "diff_lambda")], 1)
    cols = np.zeros((LAYERS, P, CW), np.float32)
    for l in range(LAYERS):
        cols[l, :, C_NM:C_NM + KD] = v["norm_mix"][l].reshape(KD, P).T
        cols[l, :, C_NF:C_NF + KD] = v["norm_ffn"][l].reshape(KD, P).T
        cols[l, :, C_CONV:C_CONV + 16] = v["mlstm_conv"][l].reshape(4, 4, P).transpose(2, 1, 0).reshape(P, 16)
        cols[l, :, C_POS:C_POS + 32] = v["nsa_cmp_pos"][l].reshape(2, 16, P).transpose(2, 0, 1).reshape(P, 32)
        cols[l, :, C_LB:C_LB + 4] = v["hgrn_lower_bounds"].reshape(LAYERS, 2, P).transpose(2, 0, 1).reshape(P, 4)
        cols[l, 0:HEADS, C_GB:C_GB + 2] = v["mlstm_gate_bias"][l].T
    return rows, cols


def kernel(**inputs):
    import concourse.bacc as bacc
    from concourse.bass_utils import run_bass_kernel_spmd

    nc = bacc.Bacc("TRN2", target_bir_lowering=False, num_devices=1)
    v = {n: np.ascontiguousarray(a) for n, a in inputs.items()}
    arrays = {n: v[n] for n in _NAMED}
    arrays["x"] = v["x"].reshape(SEQ, DIM)
    for n in ("moe_w_gate", "moe_w_up", "moe_w_down"):
        arrays[n] = v[n].reshape(LAYERS, EXPERTS, *v[n].shape[3:])
    arrays["rows"], arrays["columns"] = _layout(v)
    arrays["constants"], arrays["alibi"] = _constants()
    d = {n: nc.dram_tensor(n, a.shape, mybir.dt.from_np(a.dtype), kind="ExternalInput").ap()
         for n, a in arrays.items()}
    out = nc.dram_tensor("out", (SEQ, DIM), F32, kind="ExternalOutput").ap()
    build(nc, d, out)
    r = run_bass_kernel_spmd(nc, [arrays], core_ids=[0])
    return r.results[0]["out"].reshape(1, SEQ, DIM)
```
